# Optimizing a Trainium2 kernel written in Bass

```python
import math
import jax
import jax.numpy as jnp
from jax import lax
import numpy as np

D_MODEL = 1024
BATCH = 1
SEQ = 1024
DEPTH = 1

N_META = 16
RMS_EPS = 1e-6
MASK_VALUE = -1e30
LB_FLOOR = 1e-30

S5_WIDTH = D_MODEL // 4
S5_GROUP_CH = 16
S5_GROUPS = S5_WIDTH // S5_GROUP_CH
S5_STATE = 64
S5_DT_MIN = 1e-3
S5_DT_MAX = 1e-1

HGRN_WIDTH = D_MODEL // 4
HGRN_HEADS = 4
HGRN_HEAD_DIM = HGRN_WIDTH // HGRN_HEADS
HGRN_CHUNK = 64

ATTN_WIDTH = D_MODEL // 2
ATTN_HEADS = 4
ATTN_V_DIM = ATTN_WIDTH // ATTN_HEADS
ATTN_QK_DIM = ATTN_V_DIM // 2
ATTN_BLOCK = 128
ROPE_THETA = 10000.0

MIX_WIDTH = S5_WIDTH + HGRN_WIDTH + ATTN_WIDTH
IN_SECTION_WIDTHS = (S5_WIDTH, HGRN_WIDTH, HGRN_WIDTH, HGRN_WIDTH, HGRN_WIDTH, ATTN_WIDTH, ATTN_WIDTH, ATTN_WIDTH)
IN_WIDTH = sum(IN_SECTION_WIDTHS)

MOE_GROUPS = 4
MOE_EXPERTS_PER_GROUP = 4
MOE_EXPERTS = MOE_GROUPS * MOE_EXPERTS_PER_GROUP
MOE_TOP_K = 2
MOE_FF = 512

kernel_name = 'hymba_s5_hgrn2_diffattn_hmoe'

def rms_norm(x, gain):
    xf = x.astype(jnp.float32)
    y = xf * lax.rsqrt(jnp.mean(xf * xf, axis=-1, keepdims=True) + RMS_EPS)
    return (y * gain.astype(jnp.float32)).astype(x.dtype)

def rotary_tables(length):
    inv_freq = 1.0 / (ROPE_THETA ** (jnp.arange(0, ATTN_QK_DIM, 2, dtype=jnp.float32) / ATTN_QK_DIM))
    ang = jnp.arange(length, dtype=jnp.float32)[:, None] * inv_freq[None, :]
    ang = jnp.concatenate([ang, ang], axis=-1)
    return jnp.cos(ang), jnp.sin(ang)

def apply_rope(t, cos, sin):
    tf = t.astype(jnp.float32)
    t1, t2 = jnp.split(tf, 2, axis=-1)
    rot = jnp.concatenate([-t2, t1], axis=-1)
    c = cos[:, None, None, :]
    s = sin[:, None, None, :]
    return (tf * c + rot * s).astype(t.dtype)

def _cmul(ar, ai, br, bi):
    return ar * br - ai * bi, ar * bi + ai * br

def s5_mixer(u, lam_re, lam_im, log_dt, b_re, b_im, c_re, c_im, d_skip, w_glu):
    f32 = jnp.float32
    bsz, length, _ = u.shape
    uf = u.astype(f32).reshape(bsz, length, S5_GROUPS, S5_GROUP_CH)
    lr = lam_re.astype(f32)
    li = lam_im.astype(f32)
    dt = jnp.exp(log_dt.astype(f32))[:, None]
    mag = jnp.exp(lr * dt)
    abar_r = mag * jnp.cos(li * dt)
    abar_i = mag * jnp.sin(li * dt)
    den = lr * lr + li * li
    zr = abar_r - 1.0
    zi = abar_i
    fr = (zr * lr + zi * li) / den
    fi = (zi * lr - zr * li) / den
    bb_r, bb_i = _cmul(fr[..., None], fi[..., None], b_re.astype(f32), b_im.astype(f32))
    xr = jnp.einsum('blgc,gnc->blgn', uf, bb_r)
    xi = jnp.einsum('blgc,gnc->blgn', uf, bb_i)
    ar = jnp.broadcast_to(abar_r[None, None], (1, length, S5_GROUPS, S5_STATE))
    ai = jnp.broadcast_to(abar_i[None, None], (1, length, S5_GROUPS, S5_STATE))

    def combine(e1, e2):
        a1r, a1i, s1r, s1i = e1
        a2r, a2i, s2r, s2i = e2
        na_r, na_i = _cmul(a2r, a2i, a1r, a1i)
        ns_r, ns_i = _cmul(a2r, a2i, s1r, s1i)
        return na_r, na_i, ns_r + s2r, ns_i + s2i

    _, _, sr, si = lax.associative_scan(combine, (ar, ai, xr, xi), axis=1)
    y = jnp.einsum('blgn,gcn->blgc', sr, c_re.astype(f32)) - jnp.einsum('blgn,gcn->blgc', si, c_im.astype(f32))
    y = y.reshape(bsz, length, S5_WIDTH) + d_skip.astype(f32) * u.astype(f32)
    g = jax.nn.gelu(y)
    gl = g @ w_glu.astype(f32)
    out = gl[..., :S5_WIDTH] * jax.nn.sigmoid(gl[..., S5_WIDTH:])
    return out.astype(u.dtype)

def _gla_chunk(state, q, k, v, log_f):
    c = q.shape[2]
    cum = jnp.cumsum(log_f, axis=2)
    causal = jnp.tril(jnp.ones((c, c), dtype=bool))[None, None, :, :, None]
    rel = cum[:, :, :, None, :] - cum[:, :, None, :, :]
    decay = jnp.where(causal, jnp.exp(jnp.where(causal, rel, 0.0)), 0.0)
    scores = jnp.einsum('bhtd,bhsd,bhtsd->bhts', q, k, decay)
    out = jnp.einsum('bhts,bhsv->bhtv', scores, v) + jnp.einsum('bhtd,bhdv->bhtv', q * jnp.exp(cum), state)
    last = cum[:, :, -1:, :]
    new_state = jnp.exp(last[:, :, 0, :, None]) * state + jnp.einsum('bhsd,bhsv->bhdv', k * jnp.exp(last - cum), v)
    return new_state, out

def hgrn2_mixer(zq, zf, zi, zg, lower_bound, norm_g):
    f32 = jnp.float32
    bsz, length, _ = zq.shape

    def heads(t):
        return t.astype(f32).reshape(bsz, length, HGRN_HEADS, HGRN_HEAD_DIM).transpose(0, 2, 1, 3)

    q = jax.nn.silu(heads(zq))
    v = heads(zi)
    lb = lower_bound.astype(f32).reshape(1, HGRN_HEADS, 1, HGRN_HEAD_DIM)
    log_f = jnp.logaddexp(jnp.log(jnp.maximum(lb, LB_FLOOR)), jnp.log1p(-lb) + jax.nn.log_sigmoid(heads(zf)))
    k = -jnp.expm1(log_f)
    state0 = jnp.zeros((bsz, HGRN_HEADS, HGRN_HEAD_DIM, HGRN_HEAD_DIM), f32)
    state, o_meta = _gla_chunk(state0, q[:, :, :N_META], k[:, :, :N_META], v[:, :, :N_META], log_f[:, :, :N_META])
    n_chunks = (length - N_META) // HGRN_CHUNK

    def to_chunks(t):
        return t[:, :, N_META:].reshape(bsz, HGRN_HEADS, n_chunks, HGRN_CHUNK, -1).transpose(2, 0, 1, 3, 4)

    def step(s, xs):
        return _gla_chunk(s, *xs)

    _, o_rest = lax.scan(step, state, (to_chunks(q), to_chunks(k), to_chunks(v), to_chunks(log_f)))
    o_rest = o_rest.transpose(1, 2, 0, 3, 4).reshape(bsz, HGRN_HEADS, length - N_META, HGRN_HEAD_DIM)
    o = jnp.concatenate([o_meta, o_rest], axis=2).transpose(0, 2, 1, 3)
    o = rms_norm(o, norm_g).reshape(bsz, length, HGRN_WIDTH) * jax.nn.silu(zg.astype(f32))
    return o.astype(zq.dtype)

def diff_attention(zq, zk, zv, lq1, lk1, lq2, lk2, subln_g, lam_init, cos, sin):
    f32 = jnp.float32
    bsz, length, _ = zq.shape
    q = apply_rope(zq.reshape(bsz, length, ATTN_HEADS, 2, ATTN_QK_DIM), cos, sin)
    k = apply_rope(zk.reshape(bsz, length, ATTN_HEADS, 2, ATTN_QK_DIM), cos, sin)
    v = zv.reshape(bsz, length, ATTN_HEADS, ATTN_V_DIM)
    lam = (jnp.exp(jnp.sum(lq1.astype(f32) * lk1.astype(f32)))
           - jnp.exp(jnp.sum(lq2.astype(f32) * lk2.astype(f32))) + lam_init)
    scale = ATTN_QK_DIM ** -0.5
    bounds = [(0, N_META)] + [(s, s + ATTN_BLOCK) for s in range(N_META, length, ATTN_BLOCK)]
    outs = []
    for qs, qe in bounds:
        s = jnp.einsum('bqhcd,bkhcd->bhcqk', q[:, qs:qe], k[:, :qe]).astype(f32) * scale
        causal = jnp.arange(qe)[None, :] <= jnp.arange(qs, qe)[:, None]
        p = jax.nn.softmax(jnp.where(causal, s, MASK_VALUE), axis=-1)
        a = p[:, :, 0] - lam * p[:, :, 1]
        outs.append(jnp.einsum('bhqk,bkhv->bqhv', a.astype(v.dtype), v[:, :qe]))
    o = jnp.concatenate(outs, axis=1)
    o = rms_norm(o, subln_g) * (1.0 - lam_init)
    return o.reshape(bsz, length, ATTN_WIDTH)

def hier_moe(h, w_group, b_group, w_expert, b_expert, w_gate, w_up, w_down):
    f32 = jnp.float32
    bsz, length, d = h.shape
    t = h.reshape(-1, d)
    group_prob = jax.nn.softmax((t @ w_group).astype(f32) + b_group.astype(f32), axis=-1)
    gp, gi = lax.top_k(group_prob, 1)
    exp_logits = ((t @ w_expert).astype(f32) + b_expert.astype(f32)).reshape(-1, MOE_GROUPS, MOE_EXPERTS_PER_GROUP)
    in_group = jnp.einsum('tg,tge->te', jax.nn.one_hot(gi[:, 0], MOE_GROUPS, dtype=f32), exp_logits)
    ev, ei = lax.top_k(in_group, MOE_TOP_K)
    ew = jax.nn.softmax(ev, axis=-1) * gp
    expert_id = gi * MOE_EXPERTS_PER_GROUP + ei
    gates = jnp.einsum('tke,tk->te', jax.nn.one_hot(expert_id, MOE_EXPERTS, dtype=f32), ew).astype(t.dtype)
    y = jnp.zeros_like(t)
    for e in range(MOE_EXPERTS):
        he = jax.nn.silu(t @ w_gate[e]) * (t @ w_up[e])
        y = y + gates[:, e:e + 1] * (he @ w_down[e])
    return y.reshape(bsz, length, d)

def setup_inputs(seed: int = 0) -> dict:
    key = jax.random.key(seed)
    ks = jax.random.split(key, 32)
    f32 = jnp.float32

    def nrm(k, shape, scale):
        return scale * jax.random.normal(k, shape, f32)

    n_idx = jnp.arange(S5_STATE, dtype=f32)
    return {
        'x': nrm(ks[0], (BATCH, SEQ, D_MODEL), 1.0),
        'meta_tokens': nrm(ks[1], (N_META, D_MODEL), 1.0),
        'norm_mix_g': 1.0 + nrm(ks[2], (DEPTH, D_MODEL), 0.02),
        'w_in': nrm(ks[3], (DEPTH, D_MODEL, IN_WIDTH), D_MODEL ** -0.5),
        's5_lambda_re': -0.5 + nrm(ks[4], (DEPTH, S5_GROUPS, S5_STATE), 0.01),
        's5_lambda_im': math.pi * n_idx + nrm(ks[5], (DEPTH, S5_GROUPS, S5_STATE), 0.01),
        's5_log_dt': jax.random.uniform(ks[6], (DEPTH, S5_GROUPS), f32, math.log(S5_DT_MIN), math.log(S5_DT_MAX)),
        's5_b_re': nrm(ks[7], (DEPTH, S5_GROUPS, S5_STATE, S5_GROUP_CH), (2 * S5_GROUP_CH) ** -0.5),
        's5_b_im': nrm(ks[8], (DEPTH, S5_GROUPS, S5_STATE, S5_GROUP_CH), (2 * S5_GROUP_CH) ** -0.5),
        's5_c_re': nrm(ks[9], (DEPTH, S5_GROUPS, S5_GROUP_CH, S5_STATE), S5_STATE ** -0.5),
        's5_c_im': nrm(ks[10], (DEPTH, S5_GROUPS, S5_GROUP_CH, S5_STATE), S5_STATE ** -0.5),
        's5_d': nrm(ks[11], (DEPTH, S5_WIDTH), 1.0),
        's5_w_glu': nrm(ks[12], (DEPTH, S5_WIDTH, 2 * S5_WIDTH), S5_WIDTH ** -0.5),
        'hgrn_lower_bounds': nrm(ks[13], (DEPTH, HGRN_WIDTH), 0.1),
        'hgrn_norm_g': 1.0 + nrm(ks[14], (DEPTH, HGRN_HEAD_DIM), 0.02),
        'diff_lambda_q1': nrm(ks[15], (DEPTH, ATTN_QK_DIM), 0.1),
        'diff_lambda_k1': nrm(ks[16], (DEPTH, ATTN_QK_DIM), 0.1),
        'diff_lambda_q2': nrm(ks[17], (DEPTH, ATTN_QK_DIM), 0.1),
        'diff_lambda_k2': nrm(ks[18], (DEPTH, ATTN_QK_DIM), 0.1),
        'diff_subln_g': 1.0 + nrm(ks[19], (DEPTH, ATTN_V_DIM), 0.02),
        'w_out': nrm(ks[20], (DEPTH, MIX_WIDTH, D_MODEL), MIX_WIDTH ** -0.5),
        'norm_ffn_g': 1.0 + nrm(ks[21], (DEPTH, D_MODEL), 0.02),
        'moe_w_group': nrm(ks[22], (DEPTH, D_MODEL, MOE_GROUPS), D_MODEL ** -0.5),
        'moe_b_group': nrm(ks[23], (DEPTH, MOE_GROUPS), 0.01),
        'moe_w_expert': nrm(ks[24], (DEPTH, D_MODEL, MOE_EXPERTS), D_MODEL ** -0.5),
        'moe_b_expert': nrm(ks[25], (DEPTH, MOE_EXPERTS), 0.01),
        'moe_w_gate': nrm(ks[26], (DEPTH, MOE_EXPERTS, D_MODEL, MOE_FF), D_MODEL ** -0.5),
        'moe_w_up': nrm(ks[27], (DEPTH, MOE_EXPERTS, D_MODEL, MOE_FF), D_MODEL ** -0.5),
        'moe_w_down': nrm(ks[28], (DEPTH, MOE_EXPERTS, MOE_FF, D_MODEL), MOE_FF ** -0.5),
        'final_norm_g': 1.0 + nrm(ks[29], (D_MODEL,), 0.02),
    }

def reference(x, meta_tokens, norm_mix_g, w_in, s5_lambda_re, s5_lambda_im, s5_log_dt, s5_b_re, s5_b_im,
              s5_c_re, s5_c_im, s5_d, s5_w_glu, hgrn_lower_bounds, hgrn_norm_g, diff_lambda_q1, diff_lambda_k1,
              diff_lambda_q2, diff_lambda_k2, diff_subln_g, w_out, norm_ffn_g, moe_w_group, moe_b_group,
              moe_w_expert, moe_b_expert, moe_w_gate, moe_w_up, moe_w_down, final_norm_g):
    bsz = x.shape[0]
    meta = jnp.broadcast_to(meta_tokens.astype(x.dtype)[None], (bsz, N_META, D_MODEL))
    h = jnp.concatenate([meta, x], axis=1)
    length = h.shape[1]
    cos, sin = rotary_tables(length)
    lb_w = jax.nn.softmax(hgrn_lower_bounds.astype(jnp.float32), axis=0)
    lower_bounds = jnp.cumsum(lb_w, axis=0) - lb_w[0:1]
    split_points = [int(p) for p in np.cumsum(IN_SECTION_WIDTHS)[:-1]]
    for layer in range(DEPTH):
        lam_init = 0.8 - 0.6 * math.exp(-0.3 * layer)
        proj = rms_norm(h, norm_mix_g[layer]) @ w_in[layer]
        u, hq, hf, hi, hg, aq, ak, av = jnp.split(proj, split_points, axis=-1)
        y_ssm = s5_mixer(u, s5_lambda_re[layer], s5_lambda_im[layer], s5_log_dt[layer], s5_b_re[layer],
                         s5_b_im[layer], s5_c_re[layer], s5_c_im[layer], s5_d[layer], s5_w_glu[layer])
        y_rec = hgrn2_mixer(hq, hf, hi, hg, lower_bounds[layer], hgrn_norm_g[layer])
        y_att = diff_attention(aq, ak, av, diff_lambda_q1[layer], diff_lambda_k1[layer], diff_lambda_q2[layer],
                               diff_lambda_k2[layer], diff_subln_g[layer], lam_init, cos, sin)
        mixed = jnp.concatenate([y_ssm.astype(h.dtype), y_rec.astype(h.dtype), y_att.astype(h.dtype)], axis=-1)
        h = h + mixed @ w_out[layer]
        h = h + hier_moe(rms_norm(h, norm_ffn_g[layer]), moe_w_group[layer], moe_b_group[layer],
                         moe_w_expert[layer], moe_b_expert[layer], moe_w_gate[layer], moe_w_up[layer],
                         moe_w_down[layer])
    h = rms_norm(h, final_norm_g)
    return h[:, N_META:]


_drawn_inputs = setup_inputs


def setup_inputs(seed=0):
    import zlib

    import numpy as np

    out = dict(_drawn_inputs(seed))
    spreads = {}
    factors = {'s5_lambda_re': 200.0,
     's5_b_re': 11.08,
     's5_b_im': 87.32,
     's5_c_re': 86.992,
     's5_c_im': 11.365,
     'hgrn_norm_g': 27.262,
     'diff_lambda_k2': 2.683,
     'diff_subln_g': 13.961,
     'moe_b_group': 39.137,
     'moe_b_expert': 23.405,
     'final_norm_g': 25.076,
     's5_lambda_im': 2.748,
     's5_log_dt': 3.022,
     'norm_ffn_g': 6.267}
    for name, (base, spread) in spreads.items():
        noise = np.random.default_rng([zlib.crc32(name.encode()), seed]).standard_normal(out[name].shape)
        drawn = base * np.exp(spread * noise) if base else spread * noise
        out[name] = jnp.asarray(drawn.astype(out[name].dtype))
    for name, factor in factors.items():
        out[name] = (out[name] * factor).astype(out[name].dtype)
    return out
```

```python
from contextlib import ExitStack

import numpy as np

import concourse.bass as bass
from concourse import mybir

F32 = mybir.dt.float32
I32 = mybir.dt.int32
ACT = mybir.ActivationFunctionType
ALU = mybir.AluOpType
AX = mybir.AxisListType

P = 128
D = 1024
KD = D // P
META = 16
X = 1024
L = META + X
NT = X // P
EPS = 1e-6

S5_G, S5_C, S5_N = 16, 16, 64
S5_T = P // S5_C
S5_K = L // S5_T
S5_KM = META // S5_T

HC = 64
HL = 6
NH = 4
LAM_INIT = 0.8 - 0.6 * 1.0
SCALE = 64 ** -0.5

NG, NPG, NE, FF = 4, 4, 16, 512
SLOTS = X * 2
NB = (SLOTS + NE * (P - 1)) // P

C_ID, C_MASK, C_TRI, C_ONES, C_HM = 0, 128, 256, 384, 512
C_TOK, C_DESC4, C_J9, C_128J, C_SG, C_IOTAB = 896, 912, 916, 928, 936, 937
C_COS = 976
C_SIN = C_COS + L
C_END = C_SIN + L
P_GMIX, P_S5, P_D, P_LB, P_LAM = 0, 8, 56, 58, 60
P_B1, P_B2, P_C1, P_C2 = 64, 64 + 256, 64 + 512, 64 + 768
P_END = 64 + 1024


def constants():
    c = np.zeros((P, C_END), np.float32)
    i = np.arange(P)
    c[:, C_ID:C_ID + P] = np.eye(P)
    c[:, C_MASK:C_MASK + P] = np.where(i[None, :] <= i[:, None], 0.0, -1e30)
    c[:, C_TRI:C_TRI + P] = i[:, None] < i[None, :]
    c[:, C_ONES:C_ONES + P] = 1.0
    s, t = (i % HC)[:, None], np.arange(HC)[None, :]
    for lv in range(HL):
        if lv == 0:
            m = (s // 2 == t // 2) & (s <= t)
        else:
            b = 2 << lv
            m = (s // b == t // b) & (s % b < b // 2) & (t % b >= b // 2)
        c[:, C_HM + lv * HC:C_HM + (lv + 1) * HC] = m
    c[:, C_TOK:C_TOK + NT] = P * np.arange(NT)[None, :] + i[:, None]
    c[:, C_DESC4:C_DESC4 + 4] = [4, 3, 2, 1]
    c[:, C_J9:C_J9 + 9] = np.arange(9)
    c[:, C_128J:C_128J + 8] = 128 * np.arange(8)
    c[:, C_SG] = np.where(i < 64, -1.0, 1.0)
    c[:, C_IOTAB:C_IOTAB + NB] = np.arange(NB)
    inv = (np.float32(1.0) / (np.float32(10000.0) ** (np.arange(0, 64, 2, dtype=np.float32) / np.float32(64)))).astype(np.float32)
    ang = (np.arange(L, dtype=np.float32)[:, None] * inv[None, :]).astype(np.float32)
    cos, sin = np.cos(ang).T, np.sin(ang).T
    c[:, C_COS:C_COS + L] = np.concatenate([cos] * 4)
    c[:, C_SIN:C_SIN + L] = np.concatenate([-sin, sin, -sin, sin])
    return c


class Chain:

    def __init__(self, eng, sem):
        self.eng, self.sem, self.n = eng, sem, 0

    def __call__(self, ins):
        self.n += 1
        ins.then_inc(self.sem, 1)
        self.eng.wait_ge(self.sem, self.n)


def build(nc, a, out, stage=99):
    ctx = ExitStack()
    with ctx:
        def sem(name):
            return ctx.enter_context(nc.semaphore(name))

        con = ctx.enter_context(nc.sbuf_tensor("con", [P, C_END], F32))
        par = ctx.enter_context(nc.sbuf_tensor("par", [P, P_END], F32))
        mem = ctx.enter_context(nc.sbuf_tensor("mem", [P, 48420], F32))
        sml = ctx.enter_context(nc.sbuf_tensor("sml", [P, 600], F32))
        ps = ctx.enter_context(nc.psum_tensor("ps", [P, 8, 512], F32))

        def view(off, *shape):
            n = int(np.prod(shape))
            v = mem[:, off:off + n]
            if len(shape) == 2:
                v = v.rearrange("p (a b) -> p a b", a=shape[0])
            if len(shape) == 3:
                v = v.rearrange("p (a b c) -> p a b c", a=shape[0], b=shape[1])
            return v

        ident = con[:, C_ID:C_ID + P]

        oV = 0
        oAK = oV + 9 * 1024
        oHF = oAK + 4 * L
        oU = oHF + 2 * L
        oHQ = oU + 2 * L
        oAQ = oHQ + 2 * X
        oC = oAQ + 4 * X
        V = view(oV, 9, 1024)
        AK, HF, AQ, HQ = view(oAK, 4, L), view(oHF, 2, L), view(oAQ, 4, X), view(oHQ, 2, X)
        UP = view(oU, 2, S5_T, S5_K)
        XT = view(oC, KD, L)
        WR = [view(oC + KD * L + i * 4096, KD, 512) for i in range(3)]
        oX = oC + KD * L + 3 * 4096
        XN = view(oX, 3, 1024)
        JUNK = view(oX + 3072, 1024)
        SSQ, VAR, SD, RSTD = (sml[:, i * 9:i * 9 + 9] for i in range(4))

        params_loaded = sem("params_loaded")
        x_loaded = [sem(f"x_loaded{i}") for i in range(3)]
        w_loaded = [sem(f"w_loaded{i}") for i in range(6)]
        ssq_ready, var_ready, sd_ready, xn_ready = sem("ssq_ready"), sem("var_ready"), sem("sd_ready"), sem("xn_ready")
        xt_ready, xt_copied = sem("xt_ready"), sem("xt_copied")
        proj_done = sem("proj_done")
        proj_evac = [sem("proj_evac_act"), sem("proj_evac_dve")]
        dve_chain, act_chain, pool_chain = sem("dve_chain"), sem("act_chain"), sem("pool_chain")

        SECT = [(0, 512, 0), (512, 768, 1), (768, 1280, 2), (1792, 2304, 0), (1280, 1792, 1), (2304, 2816, 2)]
        CH = [(0, META), (META, META + 512), (META + 512, L)]
        jobs = []
        for m in range(2):
            for c in range(3):
                jobs.append((0, "u", m, c))
        for m in range(2):
            for c in (1, 2):
                jobs.append((0, "hq", m, c))
        for m in range(2):
            for c in range(3):
                jobs.append((1, "hf", m, c))
        for t in range(9):
            jobs.append((2, "vl", 0, t))
        for m in range(4):
            for c in range(3):
                jobs.append((3, "ak", m, c))
        for m in range(4):
            for c in (1, 2):
                jobs.append((4, "aq", m, c))
        for t in range(9):
            jobs.append((5, "vr", 0, t))
        last_of = {j[0]: n + 1 for n, j in enumerate(jobs)}
        first_of = {}
        for n, j in enumerate(jobs):
            first_of.setdefault(j[0], n)

        def evacs(n, parity):
            return (n + 1 - parity) // 2

        def rows(t):
            return META if t == 0 else P

        def cols(t):
            return (0, META) if t == 0 else (META + P * (t - 1), META + P * t)

        def sp_project(sp):
            sp.dma_start(con[:, :], a["consts"]).then_inc(params_loaded, 16)
            sp.dma_start(par[:, :], a["params"]).then_inc(params_loaded, 16)
            for t in range(9):
                if t >= 3:
                    sp.wait_ge(xt_ready, 2 * (t - 2))
                src = a["meta_tokens"] if t == 0 else a["x"][P * (t - 1):P * t, :]
                sp.dma_start(XN[0:rows(t), t % 3, :], src).then_inc(x_loaded[t % 3], 16)
            for s in range(3, 6):
                lo, hi, slot = SECT[s]
                sp.wait_ge(proj_done, last_of[s - 3])
                sp.dma_start(WR[slot][:, :, 0:hi - lo],
                             a["w_in"].rearrange("(k p) n -> p k n", p=P)[:, :, lo:hi]).then_inc(w_loaded[s], 16)

        def act_project(act):
            for s in range(3):
                lo, hi, slot = SECT[s]
                act.dma_start(WR[slot][:, :, 0:hi - lo],
                              a["w_in"].rearrange("(k p) n -> p k n", p=P)[:, :, lo:hi]).then_inc(w_loaded[s], 16)
            for t in range(9):
                R = rows(t)
                act.wait_ge(x_loaded[t % 3], 16 * (t // 3 + 1))
                nc.scalar.activation(JUNK[0:R, :], XN[0:R, t % 3, :], ACT.Square,
                                     accum_out=SSQ[0:R, t:t + 1]).then_inc(ssq_ready, 1)
                act.wait_ge(var_ready, t + 1)
                nc.scalar.activation(SD[0:R, t:t + 1], VAR[0:R, t:t + 1], ACT.Sqrt).then_inc(sd_ready, 1)
            for n in range(0, len(jobs), 2):
                evacuate(act, nc.scalar.copy, n)

        def dve_norm(dve, link, t):
            R = rows(t)
            dve.wait_ge(ssq_ready, t + 1)
            nc.vector.tensor_scalar(VAR[0:R, t:t + 1], SSQ[0:R, t:t + 1], 1.0 / D, EPS, ALU.mult, ALU.add).then_inc(var_ready, 1)
            dve.wait_ge(sd_ready, t + 1)
            link(nc.vector.reciprocal(RSTD[0:R, t:t + 1], SD[0:R, t:t + 1]))
            nc.vector.tensor_scalar(XN[0:R, t % 3, :], XN[0:R, t % 3, :], RSTD[0:R, t:t + 1], None, ALU.mult).then_inc(xn_ready, 1)

        def dve_gain(dve, t):
            R = rows(t)
            lo, hi = cols(t)
            for j in range(2):
                dve.wait_ge(xt_ready, 2 * t + j + 1)
                nc.vector.tensor_tensor(XT[:, 4 * j:4 * j + 4, lo:hi],
                                        ps[:, 6 + j, 0:4 * R].rearrange("p (k t) -> p k t", k=4),
                                        par[:, P_GMIX + 4 * j:P_GMIX + 4 * j + 4].unsqueeze(2).to_broadcast([P, 4, R]),
                                        ALU.mult).then_inc(xt_copied, 1)

        def dve_project(dve, link):
            dve.wait_ge(params_loaded, 32)
            for t in range(10):
                if t < 9:
                    dve_norm(dve, link, t)
                if t >= 1:
                    dve_gain(dve, t - 1)
            for n in range(1, len(jobs), 2):
                evacuate(dve, nc.vector.tensor_copy, n)

        def evacuate(eng, copy, n):
            s, kind, m, c = jobs[n]
            eng.wait_ge(proj_done, n + 1)
            b = ps[:, n % 6, :]
            if kind in ("vl", "vr"):
                R = rows(c)
                w = 256 if (kind == "vl" and c == 0) else 512
                o = 0 if kind == "vl" else 512
                ins = copy(V[0:R, c, o:o + w], b[0:R, 0:w])
            elif kind == "u":
                lo, hi = CH[c]
                ins = copy(UP[:, m, :, lo // S5_T:hi // S5_T], b[:, 0:hi - lo].rearrange("p (k s) -> p s k", s=S5_T))
            else:
                lo, hi = CH[c]
                dst = {"hq": HQ, "hf": HF, "ak": AK, "aq": AQ}[kind]
                sh = META if kind in ("hq", "aq") else 0
                ins = copy(dst[:, m, lo - sh:hi - sh], b[:, 0:hi - lo])
            ins.then_inc(proj_evac[n % 2], 1)

        def pe_project(pe):
            pe.wait_ge(params_loaded, 32)
            for t in range(9):
                R = rows(t)
                pe.wait_ge(xn_ready, t + 1)
                for j in range(2):
                    if t >= 1:
                        pe.wait_ge(xt_copied, 2 * t + j - 1)
                    for k in range(4):
                        mm = nc.tensor.transpose(ps[:, 6 + j, k * R:(k + 1) * R], XN[0:R, t % 3, (4 * j + k) * P:(4 * j + k + 1) * P],
                                                 ident[0:R, 0:R])
                    mm.then_inc(xt_ready, 1)
            pe.wait_ge(xt_copied, 18)
            for n, (s, kind, m, c) in enumerate(jobs):
                if first_of[s] == n:
                    pe.wait_ge(w_loaded[s], 16)
                if n >= 6:
                    pe.wait_ge(proj_evac[n % 2], evacs(n - 5, n % 2))
                W = WR[SECT[s][2]]
                for k in range(KD):
                    if kind in ("vl", "vr"):
                        R = rows(c)
                        lo, hi = cols(c)
                        w = 256 if (kind == "vl" and c == 0) else 512
                        mm = nc.tensor.matmul(ps[0:R, n % 6, 0:w], XT[:, k, lo:hi], W[:, k, 0:w], start=(k == 0), stop=(k == KD - 1))
                    else:
                        lo, hi = CH[c]
                        m0 = m + (2 if kind == "hq" else 0)
                        mm = nc.tensor.matmul(ps[:, n % 6, 0:hi - lo], W[:, k, m0 * P:(m0 + 1) * P], XT[:, k, lo:hi],
                                              start=(k == 0), stop=(k == KD - 1))
                mm.then_inc(proj_done, 1)

        NJ = len(jobs)
        projected = [(proj_evac[0], evacs(NJ, 0)), (proj_evac[1], evacs(NJ, 1))]

        oS = oC
        def take(*shape):
            nonlocal oS
            v = view(oS, *shape)
            oS += int(np.prod(shape))
            return v
        US = take(S5_G, S5_K)
        COS, SIN = take(S5_G, S5_K), take(S5_G, S5_K)
        T1, T2 = take(S5_G * S5_K), take(S5_G * S5_K)
        WIN = [take(S5_G, P), take(S5_G, P)]
        L1, L2 = take(S5_G, S5_T + 1, S5_C), take(S5_G, S5_T, S5_C)
        TO = take(S5_G, P)
        WGLU = take(2, 512)
        UC, UI, MJ, PR, PI, SPR, SPI = (take(S5_T + 1, S5_G) for _ in range(7))
        BB, BX = take(S5_G, S5_C), take(S5_G, S5_C)
        q = [take(S5_G) for _ in range(16)]
        SNI, SN = take(2, S5_G), take(2, S5_G)
        assert oS <= 48420
        G3 = T1[:, 0:2048].rearrange("p (g s c) -> p g s c", g=S5_G, s=S5_T)
        H3 = T2[:, 0:2048].rearrange("p (g s c) -> p g s c", g=S5_G, s=S5_T)
        GA = COS[:, :, 0:P].rearrange("p g (s c) -> p g s c", s=S5_T)
        GB = SIN[:, :, 0:P].rearrange("p g (s c) -> p g s c", s=S5_T)
        HS = T1[0:S5_C, 0:2048].rearrange("p (g n) -> p g n", g=S5_G)
        XR = T1.rearrange("p (g k) -> p g k", g=S5_G)
        XS = T2.rearrange("p (g k) -> p g k", g=S5_G)
        YO = T1[:, 0:2048].rearrange("p (g k) -> p g k", g=S5_G)
        YT = WIN[0].rearrange("p (m t) k -> p m t k", m=2)
        GT = WIN[1].rearrange("p (m t) k -> p m (t k)", m=2)
        SGM = T2[:, 0:2048].rearrange("p (m t) -> p m t", m=2)
        MIX = [view(oU, 2, X), HQ, AQ]

        def mix(k):
            return MIX[0][:, k, :] if k < 2 else MIX[1][:, k - 2, :] if k < 4 else MIX[2][:, k - 4, :]

        up_d = nc.dram_tensor("up_d", (2 * P, S5_T, S5_K), F32, kind="Internal").ap()
        y_d = nc.dram_tensor("y_d", (2 * P, S5_T, P), F32, kind="Internal").ap()
        dt_ready, phase_ready, sin_ready = sem("dt_ready"), sem("phase_ready"), sem("sin_ready")
        mag_ready, g_ready, win_turned, win_copied = sem("mag_ready"), sem("g_ready"), sem("win_turned"), sem("win_copied")
        l_ready, h_done, h_copied = sem("l_ready"), sem("h_done"), sem("h_copied")
        to_zeroed, to_loaded, up_stored, us_loaded = sem("to_zeroed"), sem("to_loaded"), sem("up_stored"), sem("us_loaded")
        x_done, x_turned, w_ready = sem("x_done"), sem("x_turned"), sem("w_ready")
        y_done, y_copied, y_stored, y_loaded = sem("y_done"), sem("y_copied"), sem("y_stored"), sem("y_loaded")
        yu_ready, gelu_ready, glu_done, glu_gate, s5_done = sem("yu_ready"), sem("gelu_ready"), sem("glu_done"), sem("glu_gate"), sem("s5_done")
        late_loaded = sem("late_loaded")
        UNITS = [(g, min(g + 3, S5_G)) for g in range(0, S5_G, 3)]

        def sp_s5(sp):
            for s, v in projected:
                sp.wait_ge(s, v)
            for m in range(2):
                sp.dma_start(up_d[m * P:(m + 1) * P], UP[:, m]).then_inc(up_stored, 16)
            sp.dma_start(WGLU, a["w_glu"].rearrange("(k p) n -> p k n", p=P)).then_inc(late_loaded, 16)
            sp.wait_ge(up_stored, 32)
            src = up_d.rearrange("(g c) s k -> s c g k", c=S5_C)
            for s in range(S5_T):
                sp.dma_start(US[S5_C * s:S5_C * (s + 1)], src[s]).then_inc(us_loaded, 16)
            sp.wait_ge(to_zeroed, 1)
            sp.wait_ge(h_copied, 4)
            for s in range(S5_T):
                sp.dma_start(TO[S5_C * s:S5_C * (s + 1), :, S5_C * s:], HS[:, :, 0:P - S5_C * s]).then_inc(to_loaded, 16)
            sp.wait_ge(y_copied, 4)
            dst = y_d.rearrange("(g c) t k -> t c g k", c=S5_C)
            for t in range(S5_T):
                sp.dma_start(dst[t], YO[S5_C * t:S5_C * (t + 1)]).then_inc(y_stored, 16)
            sp.wait_ge(y_stored, 16 * S5_T)
            for m in range(2):
                sp.dma_start(YT[:, m], y_d[m * P:(m + 1) * P]).then_inc(y_loaded, 16)

        def pool_s5(pool, link):
            pool.wait_ge(proj_done, NJ)
            nc.gpsimd.memset(TO, 0.0).then_inc(to_zeroed, 1)

        def act_s5(act, link):
            act.wait_ge(proj_done, NJ)
            nc.scalar.activation(q[0], par[:, P_S5 + 32:P_S5 + 48], ACT.Exp).then_inc(dt_ready, 1)
            act.wait_ge(phase_ready, 1)
            nc.scalar.activation(q[8], q[1], ACT.Exp).then_inc(mag_ready, 1)
            act.wait_ge(phase_ready, 2)
            nc.scalar.activation(SN, SNI, ACT.Sin).then_inc(sin_ready, 1)
            for w in range(2):
                for b in range(4):
                    act.wait_ge(win_turned, 4 * w + b + 1)
                    nc.scalar.copy(WIN[w][:, 4 * b:4 * b + 4, :],
                                   ps[:, 4 * w + b, :].rearrange("p (g n) -> p g n", g=4)).then_inc(win_copied, 1)
            act.wait_ge(g_ready, 2)
            for b in range(4):
                act.wait_ge(h_done, b + 1)
                nc.scalar.copy(HS[:, 4 * b:4 * b + 4, :], ps[0:S5_C, b, :].rearrange("p (g n) -> p g n", g=4)).then_inc(h_copied, 1)
            for b in range(4):
                act.wait_ge(y_done, b + 1)
                nc.scalar.copy(YO[:, 4 * b:4 * b + 4, :], ps[:, b, :].rearrange("p (g n) -> p g n", g=4)).then_inc(y_copied, 1)
            for m in range(2):
                act.wait_ge(yu_ready, m + 1)
                nc.scalar.activation(GT[:, m], YT[:, m].rearrange("p t k -> p (t k)"), ACT.Gelu_apprx_tanh).then_inc(gelu_ready, 1)
            for m in range(2):
                for h in range(2):
                    act.wait_ge(glu_done, 2 * m + h + 1)
                    nc.scalar.activation(SGM[:, m, 512 * h:512 * h + 512], ps[:, 2 * m + h, :], ACT.Sigmoid).then_inc(glu_gate, 1)

        def dve_s5(dve, link):
            lr, li = par[:, P_S5:P_S5 + 16], par[:, P_S5 + 16:P_S5 + 32]
            sg = con[:, C_SG:C_SG + 1]
            tt, ts, stt = nc.vector.tensor_tensor, nc.vector.tensor_scalar, nc.vector.scalar_tensor_tensor
            dt_, lrdt, th, kf, em, e2, zr, den, mag, t0, t1, fr, fi, sfi = q[:14]
            dve.wait_ge(dt_ready, 1)
            tt(lrdt, lr, dt_, ALU.mult).then_inc(phase_ready, 1)
            link(tt(th, li, dt_, ALU.mult))
            MAGIC = 12582912.0
            link(ts(kf, th, float(1 / (2 * np.pi)), MAGIC, ALU.mult, ALU.add))
            link(ts(kf, kf, -MAGIC, None, ALU.add))
            for part in (6.28125, 0.0019350051879882812, 3.0199157e-07):
                link(stt(th, kf, -part, th, ALU.mult, ALU.add))
            link(ts(SNI[:, 0], th, 3.1415925, -3.1415925, ALU.min, ALU.max))
            ts(SNI[:, 1], th, 0.5, None, ALU.mult).then_inc(phase_ready, 1)
            dve.wait_ge(phase_ready, 1)
            link(ts(t0, lrdt, 1.0 / 8, 1.0, ALU.mult, ALU.add))
            for j in range(7, 1, -1):
                link(tt(t0, t0, lrdt, ALU.mult))
                link(ts(t0, t0, 1.0 / j, 1.0, ALU.mult, ALU.add))
            link(tt(em, t0, lrdt, ALU.mult))
            link(tt(t1, lrdt, lrdt, ALU.mult))
            link(ts(t1, t1, 0.16, None, ALU.is_gt))
            dve.wait_ge(mag_ready, 1)
            link(ts(e2, mag, -1.0, None, ALU.add))
            link(nc.vector.copy_predicated(em, t1.bitcast(I32), e2))
            link(ts(MJ[:, 1], em, 1.0, None, ALU.add))
            link(nc.vector.memset(MJ[:, 0], 1.0))
            dve.wait_ge(sin_ready, 1)
            link(nc.vector.memset(UC[:, 0], 1.0))
            link(nc.vector.memset(UI[:, 0], 0.0))
            link(nc.vector.tensor_copy(UI[:, 1], SN[:, 0]))
            link(tt(t0, SN[:, 1], SN[:, 1], ALU.mult))
            link(ts(t1, t0, -2.0, None, ALU.mult))
            link(ts(UC[:, 1], t1, 1.0, None, ALU.add))

            def cmul(oc, os_, ac, as_, bc, bs, shape):
                n = int(np.prod(shape[1:]))
                pa, pb = T1[:, 0:n], T1[:, 1040:1040 + n]
                if len(shape) == 3:
                    pa, pb = (v.rearrange("p (a b) -> p a b", a=shape[1]) for v in (pa, pb))
                link(tt(pa, ac, bc, ALU.mult))
                link(tt(pb, as_, bs, ALU.mult))
                link(tt(oc, pa, pb, ALU.subtract))
                link(tt(pa, ac, bs, ALU.mult))
                link(tt(pb, as_, bc, ALU.mult))
                link(tt(os_, pa, pb, ALU.add))

            for m in (1, 2, 4):
                sh = [P, m, S5_G]
                b = [v[:, m:m + 1].to_broadcast(sh) for v in (UC, UI, MJ)]
                cmul(UC[:, m + 1:2 * m + 1], UI[:, m + 1:2 * m + 1], UC[:, 1:m + 1], UI[:, 1:m + 1], b[0], b[1], sh)
                link(tt(MJ[:, m + 1:2 * m + 1], MJ[:, 1:m + 1], b[2], ALU.mult))
            link(tt(PR, MJ, UC, ALU.mult))
            link(tt(PI, MJ, UI, ALU.mult))
            link(ts(SPR, PR, sg, None, ALU.mult))
            link(ts(SPI, PI, sg, None, ALU.mult))
            link(tt(t0, em, UC[:, 1], ALU.mult))
            link(tt(zr, t0, t1, ALU.add))
            link(tt(den, lr, lr, ALU.mult))
            link(tt(t0, li, li, ALU.mult))
            link(tt(den, den, t0, ALU.add))
            link(nc.vector.reciprocal(den, den))
            link(tt(t0, zr, lr, ALU.mult))
            link(tt(t1, PI[:, 1], li, ALU.mult))
            link(tt(t0, t0, t1, ALU.add))
            link(tt(fr, t0, den, ALU.mult))
            link(tt(t0, PI[:, 1], lr, ALU.mult))
            link(tt(t1, zr, li, ALU.mult))
            link(tt(t0, t0, t1, ALU.subtract))
            link(tt(fi, t0, den, ALU.mult))
            link(ts(sfi, fi, sg, None, ALU.mult))
            B1, B2, C1, C2 = (par[:, o:o + 256].rearrange("p (g c) -> p g c", g=S5_G) for o in (P_B1, P_B2, P_C1, P_C2))
            g2 = [P, S5_G, S5_C]
            ta, tb = (T1[:, o:o + 256].rearrange("p (g c) -> p g c", g=S5_G) for o in (0, 256))
            bf, bs = fr.unsqueeze(2).to_broadcast(g2), sfi.unsqueeze(2).to_broadcast(g2)
            for o, u, v, op in ((BB, B1, B2, ALU.add), (BX, B2, B1, ALU.subtract)):
                link(tt(ta, u, bf, ALU.mult))
                link(tt(tb, v, bs, ALU.mult))
                link(tt(o, ta, tb, op))

            def powers(tab, lo, n, rev=False):
                v = tab[:, lo:lo + n].rearrange("p s g -> p g s")
                if rev:
                    v = v[:, :, ::-1]
                return v.unsqueeze(3).to_broadcast([P, S5_G, n, S5_C])

            def rep(v, n):
                return v.unsqueeze(2).to_broadcast([P, S5_G, n, S5_C])

            link(tt(G3, rep(BB, 8), powers(PR, 0, 8, True), ALU.mult))
            link(tt(H3, rep(BX, 8), powers(SPI, 0, 8, True), ALU.mult))
            tt(GA, G3, H3, ALU.add).then_inc(g_ready, 1)
            dve.wait_ge(g_ready, 1)
            link(tt(G3, rep(BB, 8), powers(PI, 0, 8, True), ALU.mult))
            link(tt(H3, rep(BX, 8), powers(SPR, 0, 8, True), ALU.mult))
            tt(GB, G3, H3, ALU.subtract).then_inc(g_ready, 1)
            U3 = T2[:, 0:2048].rearrange("p (g s c) -> p g s c", g=S5_G, s=S5_T)
            link(tt(L1, rep(C1, 9), powers(SPR, 0, 9), ALU.mult))
            dve.wait_ge(g_ready, 2)
            for lo, n in ((0, 8), (8, 1)):
                t3 = T2[:, 0:256 * n].rearrange("p (g s c) -> p g s c", g=S5_G, s=n)
                link(tt(t3, rep(C2, n), powers(PI, lo, n), ALU.mult))
                ins = stt_neg(L1[:, :, lo:lo + n], t3)
                if lo == 8:
                    ins.then_inc(l_ready, 1)
                else:
                    link(ins)
            link(tt(L2, rep(C1, 8), powers(SPI, 1, 8), ALU.mult))
            link(tt(U3, rep(C2, 8), powers(PR, 1, 8), ALU.mult))
            link(tt(L2, L2, U3, ALU.subtract))
            dve.wait_ge(win_turned, 8)
            link(nc.vector.memset(COS[:, :, 0], 1.0))
            link(nc.vector.memset(SIN[:, :, 0], 0.0))
            link(nc.vector.tensor_copy(COS[:, :, 1], UC[:, 8]))
            link(nc.vector.tensor_copy(SIN[:, :, 1], UI[:, 8]))
            for m in (1, 2, 4, 8, 16, 32, 64, 128):
                w = min(m, S5_K - 1 - m)
                sh = [P, S5_G, w]
                n = S5_G * w
                pa, pb = (T2[:, o:o + n].rearrange("p (g k) -> p g k", g=S5_G) for o in (0, 1040))
                bc, bs = (v[:, :, m:m + 1].to_broadcast(sh) for v in (COS, SIN))
                ac, as_, oc, os_ = COS[:, :, 1:w + 1], SIN[:, :, 1:w + 1], COS[:, :, m + 1:m + 1 + w], SIN[:, :, m + 1:m + 1 + w]
                link(tt(pa, ac, bc, ALU.mult))
                link(tt(pb, as_, bs, ALU.mult))
                link(tt(oc, pa, pb, ALU.subtract))
                link(tt(pa, ac, bs, ALU.mult))
                link(tt(pb, as_, bc, ALU.mult))
                link(tt(os_, pa, pb, ALU.add))
            dve.wait_ge(to_loaded, 16 * S5_T)
            for n, (lo, hi) in enumerate(UNITS):
                b = 2 * (n % 4)
                w = (hi - lo) * S5_K
                dve.wait_ge(x_done, n + 1)
                link(tt(XR[:, lo:hi], ps[:, b, 0:w].rearrange("p (g k) -> p g k", k=S5_K), COS[:, lo:hi], ALU.mult))
                tt(XS[:, lo:hi], ps[:, b + 1, 0:w].rearrange("p (g k) -> p g k", k=S5_K), SIN[:, lo:hi], ALU.mult).then_inc(x_turned, 1)
                dve.wait_ge(x_turned, n + 1)
                link(tt(XR[:, lo:hi], XR[:, lo:hi], XS[:, lo:hi], ALU.add))
            for g in range(S5_G):
                ins = nc.vector.tensor_tensor_scan(XS[:, g], MJ[:, 8, g:g + 1].to_broadcast([P, S5_K]), XR[:, g], 0.0, ALU.mult, ALU.add)
            link(ins)
            tt(COS, COS, XS, ALU.mult).then_inc(w_ready, 1)
            tt(SIN, SIN, XS, ALU.mult).then_inc(w_ready, 1)
            for m in range(2):
                dve.wait_ge(y_loaded, 32)
                stt(YT[:, m], UP[:, m, :, S5_KM:], par[:, P_D + m:P_D + m + 1], YT[:, m], ALU.mult, ALU.add).then_inc(yu_ready, 1)
            for m in range(2):
                for h in range(2):
                    dve.wait_ge(glu_done, 4 + 2 * m + h + 1)
                    dve.wait_ge(glu_gate, 2 * m + h + 1)
                    tt(mix(m).rearrange("p (k t) -> p t k", t=S5_T)[:, 4 * h:4 * h + 4],
                       ps[:, 4 + 2 * m + h, :].rearrange("p (t k) -> p t k", t=4),
                       SGM[:, m, 512 * h:512 * h + 512].rearrange("p (t k) -> p t k", t=4), ALU.mult).then_inc(s5_done, 1)

        def stt_neg(x, y):
            return nc.vector.scalar_tensor_tensor(x, x, -1.0, y, ALU.mult, ALU.subtract)

        def pe_s5(pe):
            for s, v in projected:
                pe.wait_ge(s, v)
            for w, G in enumerate((COS, SIN)):
                pe.wait_ge(g_ready, w + 1)
                for g in range(S5_G):
                    mm = nc.tensor.transpose(ps[:, 4 * w + g // 4, (g % 4) * P:(g % 4 + 1) * P], G[:, g, 0:P], ident)
                    if g % 4 == 3:
                        mm.then_inc(win_turned, 1)
            pe.wait_ge(l_ready, 1)
            pe.wait_ge(win_copied, 4)
            for g in range(S5_G):
                mm = nc.tensor.matmul(ps[0:S5_C, g // 4, (g % 4) * P:(g % 4 + 1) * P], BB[:, g], L1[:, g, 0:S5_T].rearrange("p t c -> p (t c)"),
                                      start=True, stop=True)
                if g % 4 == 3:
                    mm.then_inc(h_done, 1)
            pe.wait_ge(us_loaded, 16 * S5_T)
            pe.wait_ge(win_copied, 8)
            pe.wait_ge(h_copied, 4)
            for n, (lo, hi) in enumerate(UNITS):
                b = 2 * (n % 4)
                if n >= 4:
                    pe.wait_ge(x_turned, n - 3)
                for g in range(lo, hi):
                    for w in range(2):
                        mm = nc.tensor.matmul(ps[:, b + w, (g - lo) * S5_K:(g - lo + 1) * S5_K], WIN[w][:, g], US[:, g], start=True, stop=True)
                mm.then_inc(x_done, 1)
            pe.wait_ge(x_turned, len(UNITS))
            pe.wait_ge(to_loaded, 16 * S5_T)
            pe.wait_ge(w_ready, 2)
            for g in range(S5_G):
                o = ps[:, g // 4, (g % 4) * P:(g % 4 + 1) * P]
                nc.tensor.matmul(o, TO[:, g], US[:, g, S5_KM:], start=True, stop=False)
                nc.tensor.matmul(o, L1[:, g, 1:].rearrange("p t c -> p (t c)"), COS[:, g, S5_KM - 1:S5_K - 1], start=False, stop=False)
                mm = nc.tensor.matmul(o, L2[:, g].rearrange("p t c -> p (t c)"), SIN[:, g, S5_KM - 1:S5_K - 1], start=False, stop=True)
                if g % 4 == 3:
                    mm.then_inc(y_done, 1)
            pe.wait_ge(late_loaded, 16)
            pe.wait_ge(gelu_ready, 2)
            pe.wait_ge(y_copied, 4)
            for n, m in enumerate((2, 3, 0, 1)):
                for h in range(2):
                    for k in range(2):
                        mm = nc.tensor.matmul(ps[:, 2 * n + h, :], WGLU[:, k, m * P:(m + 1) * P], GT[:, k, 512 * h:512 * h + 512],
                                              start=(k == 0), stop=(k == 1))
                    mm.then_inc(glu_done, 1)

        oS = oC
        CU, LF, KK = take(2, L), take(2, L), take(2, L)
        QE, KE = [take(HL, 512) for _ in range(2)], [take(HL, 512) for _ in range(2)]
        DE = take(3, 512)
        KT = take(9, P)
        SH = take(X // HC, P)
        TM = take(2, HL * HC)
        PB = take(2, HC)
        assert oS <= 48420
        QC, KP = view(oC + 2 * L, X), view(oC + 2 * L + L, L)
        RM = QE[0].rearrange("p a b -> p (a b)")[:, 0:L]
        OH = view(oHF, NT, 256)
        OSQ = QE[0].rearrange("p a b -> p (a b)")[:, 0:2048].rearrange("p (t c) -> p t c", t=NT)
        GN, GS = sml[:, 40:104], sml[:, 104:232]
        LBD, LBE, LBW, LBV, LBF, LFL, OML, L1P, LC0 = (sml[:, 240 + 2 * i:242 + 2 * i] for i in range(9))
        DEC, OMS, OSD, ORS = sml[:, 260:277], sml[:, 280:312], sml[:, 312:344], sml[:, 344:376]
        gains_loaded = sem("gains_loaded")
        lb_dve, lb_act = sem("lb_dve"), sem("lb_act")
        silu_ready = sem("silu_ready")
        zl_ready, ls_ready, ksig_ready, gap_ready, gapl_ready, lf_ready = (
            sem(n) for n in ("zl_ready", "ls_ready", "ksig_ready", "gap_ready", "gapl_ready", "lf_ready"))
        rm_ready, cum_ready, qdec_ready, kd_ready, kdec_ready, qc_ready, kp_ready = (
            sem(n) for n in ("rm_ready", "cum_ready", "qdec_ready", "kd_ready", "kdec_ready", "qc_ready", "kp_ready"))
        kt_turned, kt_copied, u_done, state_ready = sem("kt_turned"), sem("kt_copied"), sem("u_done"), sem("state_ready")
        d_ready, e_ready, qe_done, ke_done = sem("d_ready"), sem("e_ready"), sem("qe_done"), sem("ke_done")
        sc_done, sc_masked, p_ready, o_done, o1_copied, o_added = (
            sem(n) for n in ("sc_done", "sc_masked", "p_ready", "o_done", "o1_copied", "o_added"))
        osq_ready, oms_ready, osd_ready, oh_ready, ot_done, hgrn_done = (
            sem(n) for n in ("osq_ready", "oms_ready", "osd_ready", "oh_ready", "ot_done", "hgrn_done"))
        LN2_64 = float(64 * np.log(2.0))

        def sp_hgrn(sp):
            sp.dma_start(GN, a["hgrn_norm_g"].to_broadcast([P, 64])).then_inc(gains_loaded, 16)
            sp.dma_start(GS, a["subln_g"].to_broadcast([P, P])).then_inc(gains_loaded, 16)

        def pool_hgrn(pool, link):
            pool.wait_ge(s5_done, 4)
            link(nc.gpsimd.memset(RM, 1.0))
            link(nc.gpsimd.memset(RM[:, 0:1], 0.0))
            nc.gpsimd.memset(RM[:, META::HC], 0.0).then_inc(rm_ready, 1)
            for u in range(4):
                hp, half = u // 2, u % 2
                c0 = 512 * half
                if u >= 2:
                    pool.wait_ge(sc_done, 8 * (u - 1))
                for lv in range(HL):
                    pool.wait_ge(e_ready, 7 * u + (1 if lv == 0 else 2 + lv))
                    sl = 1 if lv == 0 else (lv + 1) % 3
                    nc.gpsimd.tensor_tensor(KE[u % 2][:, lv], KK[:, hp, META + c0:META + c0 + 512], DE[:, sl], ALU.mult).then_inc(ke_done, 1)

        def act_hgrn(act, link):
            f = nc.scalar.activation
            act.wait_ge(lb_dve, 1)
            f(LBE, LBD, ACT.Exp).then_inc(lb_act, 1)
            act.wait_ge(s5_done, 4)
            link(f(CU, HF, ACT.Abs))
            link(f(CU, CU, ACT.Exp, scale=-1.0))
            f(CU, CU, ACT.Ln, bias=1.0).then_inc(zl_ready, 1)
            act.wait_ge(lb_dve, 2)
            f(LFL, LBF, ACT.Ln, scale=float(2.0 ** 64)).then_inc(lb_act, 1)
            f(L1P, OML, ACT.Ln).then_inc(lb_act, 1)
            act.wait_ge(ls_ready, 1)
            f(KK, KK, ACT.Exp).then_inc(ksig_ready, 1)
            act.wait_ge(gap_ready, 1)
            link(f(CU, CU, ACT.Abs))
            link(f(CU, CU, ACT.Exp, scale=-1.0))
            f(CU, CU, ACT.Ln, bias=1.0).then_inc(gapl_ready, 1)
            for hp in range(2):
                act.wait_ge(cum_ready, 1)
                if hp:
                    act.wait_ge(o_added, 4)
                f(QC, CU[:, hp, META:], ACT.Exp).then_inc(qdec_ready, 1)
                act.wait_ge(kd_ready, hp + 1)
                f(KP, KP, ACT.Exp).then_inc(kdec_ready, 1)
                f(DEC[:, 0:1], CU[:, hp, META - 1:META], ACT.Exp)
                f(DEC[:, 1:17], CU[:, hp, META + HC - 1::HC], ACT.Exp).then_inc(kdec_ready, 1)
                for b in range(3):
                    act.wait_ge(kt_turned, 3 * hp + b + 1)
                    if b == 0:
                        ins = nc.scalar.copy(KT[0:META, 0], ps[0:META, 4, 0:P])
                    else:
                        ins = nc.scalar.copy(KT[:, 4 * b - 3:4 * b + 1], ps[:, 4 + b, :].rearrange("p (t c) -> p t c", t=4))
                    ins.then_inc(kt_copied, 1)
                for half in range(2):
                    u = 2 * hp + half
                    act.wait_ge(d_ready, 6 * u + 1)
                    f(DE[:, 1], DE[:, 0], ACT.Exp, scale=-1.0).then_inc(e_ready, 1)
                    f(DE[:, 0], DE[:, 0], ACT.Exp).then_inc(e_ready, 1)
                    for lv in range(1, HL):
                        act.wait_ge(d_ready, 6 * u + lv + 1)
                        sl = (lv + 1) % 3
                        f(DE[:, sl], DE[:, sl], ACT.Exp).then_inc(e_ready, 1)
                for half in range(2):
                    u = 2 * hp + half
                    act.wait_ge(o_done, 8 * u + 8)
                    for r in range(2):
                        R = slice(64 * r, 64 * r + 64)
                        for h in range(2):
                            ins = nc.scalar.copy(OH[R, 4 * half:4 * half + 4, P * hp + 64 * h:P * hp + 64 * h + 64],
                                                 ps[R, 6 + r, 256 * h:256 * h + 256].rearrange("p (t v) -> p t v", t=4))
                    ins.then_inc(o1_copied, 1)
            act.wait_ge(o_added, 8)
            f(OSQ, OH, ACT.Square).then_inc(osq_ready, 1)
            act.wait_ge(oms_ready, 1)
            f(OSD, OMS, ACT.Sqrt).then_inc(osd_ready, 1)
            for n in range(4):
                k, h = n // 2, n % 2
                act.wait_ge(ot_done, n + 1)
                nc.scalar.copy(mix(2 + k)[:, 512 * h:512 * h + 512], ps[:, n, :]).then_inc(hgrn_done, 1)

        def dve_hgrn_bounds(dve, link):
            tt, ts = nc.vector.tensor_tensor, nc.vector.tensor_scalar
            lb = par[:, P_LB:P_LB + 2]
            tt(LBD, lb, lb, ALU.subtract).then_inc(lb_dve, 1)
            dve.wait_ge(lb_act, 1)
            link(nc.vector.reciprocal(LBW, LBE))
            link(tt(LBW, LBW, LBE, ALU.mult))
            link(tt(LBV, LBW, LBW, ALU.subtract))
            link(ts(LBF, LBV, 1e-30, None, ALU.max))
            link(tt(LC0, LBV, LBF, ALU.subtract))
            ts(OML, LBV, -1.0, 1.0, ALU.mult, ALU.add).then_inc(lb_dve, 1)

        def dve_hgrn(dve, link):
            tt, ts, stt = nc.vector.tensor_tensor, nc.vector.tensor_scalar, nc.vector.scalar_tensor_tensor
            dve.wait_ge(zl_ready, 1)
            link(stt(LF, HF, 0.0, CU, ALU.min, ALU.subtract))
            tt(KK, LF, HF, ALU.subtract).then_inc(ls_ready, 1)
            dve.wait_ge(lb_act, 3)
            link(ts(LFL, LFL, -LN2_64, None, ALU.add))
            for m in range(2):
                link(ts(LF[:, m], LF[:, m], L1P[:, m:m + 1], None, ALU.add))
                ins = ts(CU[:, m], LF[:, m], LFL[:, m:m + 1], None, ALU.subtract)
            ins.then_inc(gap_ready, 1)
            dve.wait_ge(ksig_ready, 1)
            for m in range(2):
                link(ts(KK[:, m], KK[:, m], OML[:, m:m + 1], LC0[:, m:m + 1], ALU.mult, ALU.add))
            dve.wait_ge(gapl_ready, 1)
            for m in range(2):
                link(stt(LF[:, m], LF[:, m], LFL[:, m:m + 1], CU[:, m], ALU.max, ALU.add))
            dve.wait_ge(rm_ready, 1)
            for m in range(2):
                ins = nc.vector.tensor_tensor_scan(CU[:, m], RM, LF[:, m], 0.0, ALU.mult, ALU.add)
            ins.then_inc(cum_ready, 1)
            dve.wait_ge(cum_ready, 1)
            for hp in range(2):
                if hp:
                    dve.wait_ge(qdec_ready, 2)
                for lo, n, w in ((0, 1, META), (META, 16, HC)):
                    cu = CU[:, hp, lo:lo + n * w].rearrange("p (n w) -> p n w", n=n)
                    ins = tt(KP[:, lo:lo + n * w].rearrange("p (n w) -> p n w", n=n),
                             cu[:, :, w - 1:w].to_broadcast([P, n, w]), cu, ALU.subtract)
                ins.then_inc(kd_ready, 1)
                dve.wait_ge(silu_ready, 1)
                dve.wait_ge(qdec_ready, hp + 1)
                tt(QC, QC, HQ[:, hp], ALU.mult).then_inc(qc_ready, 1)
                dve.wait_ge(kdec_ready, 2 * hp + 1)
                tt(KP, KP, KK[:, hp], ALU.mult).then_inc(kp_ready, 1)
                for half in range(2):
                    dve_levels(dve, 2 * hp + half)
                dve.wait_ge(u_done, hp + 1)
                dve.wait_ge(kdec_ready, 2 * hp + 2)
                for c in range(16):
                    uc = u_bank(c)
                    if c == 0:
                        ins = nc.vector.tensor_copy(SH[:, 0], uc)
                    else:
                        ins = stt(SH[:, c], SH[:, c - 1], DEC[:, c:c + 1], uc, ALU.mult, ALU.add)
                    if c < 15:
                        link(ins)
                ins.then_inc(state_ready, 1)
                for half in range(2):
                    dve_scores(dve, 2 * hp + half)
            dve.wait_ge(osq_ready, 1)
            dve.wait_ge(o_added, 8)
            link(nc.vector.tensor_reduce(OMS, OSQ.rearrange("p t (h v) -> p (t h) v", h=4), AX.X, ALU.add))
            ts(OMS, OMS, 1.0 / 64, EPS, ALU.mult, ALU.add).then_inc(oms_ready, 1)
            dve.wait_ge(osd_ready, 1)
            link(nc.vector.reciprocal(ORS, OSD))
            dve.wait_ge(gains_loaded, 32)
            o4 = OH.rearrange("p t (h v) -> p (t h) v", h=4)
            link(tt(o4, o4, ORS.unsqueeze(2).to_broadcast([P, 32, 64]), ALU.mult))
            link(tt(o4, o4, GN.unsqueeze(1).to_broadcast([P, 32, 64]), ALU.mult))
            tt(OH, OH, V[:, 1:9, 256:512], ALU.mult).then_inc(oh_ready, 1)

        def dve_levels(dve, u):
            tt = nc.vector.tensor_tensor
            hp, half = u // 2, u % 2
            lo = META + 512 * half

            def gaps(lv):
                B = 2 << lv
                sl = 0 if lv == 0 else (lv + 1) % 3
                if lv < 2 and u or lv in (2, 4, 5):
                    dve.wait_ge(qe_done, 6 * u + (0, 0, 1, 0, 2, 3)[lv])
                if lv == 0:
                    if u:
                        dve.wait_ge(ke_done, 6 * u)
                elif lv >= 3:
                    dve.wait_ge(ke_done, 6 * u + lv - 2)
                cu = CU[:, hp, lo:lo + 512].rearrange("p (n b) -> p n b", b=B)
                de = DE[:, sl].rearrange("p (n b) -> p n b", b=B)
                if lv == 0:
                    tt(de, cu, cu[:, :, 0:1].to_broadcast([P, 512 // B, B]), ALU.subtract).then_inc(d_ready, 1)
                else:
                    h = B // 2
                    ref = cu[:, :, h - 1:h].to_broadcast([P, 512 // B, h])
                    tt(de[:, :, 0:h], ref, cu[:, :, 0:h], ALU.subtract)
                    tt(de[:, :, h:B], cu[:, :, h:B], ref, ALU.subtract).then_inc(d_ready, 1)

            def queries(lv):
                sl = 0 if lv == 0 else (lv + 1) % 3
                dve.wait_ge(e_ready, 7 * u + 2 + lv)
                tt(QE[u % 2][:, lv], HQ[:, hp, lo - META:lo - META + 512], DE[:, sl], ALU.mult).then_inc(qe_done, 1)

            if u >= 2:
                dve.wait_ge(sc_done, 8 * (u - 1))
            gaps(0)
            gaps(1)
            for lv in range(HL):
                queries(lv)
                if lv + 2 < HL:
                    gaps(lv + 2)

        def dve_scores(dve, u):
            hm = con[:, C_HM:C_HM + HL * HC]
            hp, half = u // 2, u % 2
            for j in range(8):
                n = 8 * u + j
                dve.wait_ge(sc_done, n + 1)
                nc.vector.tensor_tensor(TM[:, n % 2], ps[:, n % 4, 0:HL * HC], hm, ALU.mult).then_inc(sc_masked, 1)
                dve.wait_ge(sc_masked, n + 1)
                if n >= 2:
                    dve.wait_ge(o_done, n - 1)
                nc.vector.tensor_reduce(PB[:, n % 2], TM[:, n % 2].rearrange("p (l t) -> p t l", l=HL), AX.X, ALU.add).then_inc(p_ready, 1)
            dve.wait_ge(o_done, 8 * u + 8)
            dve.wait_ge(o1_copied, u + 1)
            for h in range(2):
                o = OH[:, 4 * half:4 * half + 4, P * hp + 64 * h:P * hp + 64 * h + 64]
                nc.vector.tensor_tensor(o, o, ps[:, 4 + h, 0:256].rearrange("p (t v) -> p t v", t=4), ALU.add).then_inc(o_added, 1)

        def u_bank(c):
            i = (c + 1) // 2 if c % 2 or c == 0 else (c - 2) // 2
            b = (i // 4) if c % 2 or c == 0 else (3, 7)[i // 4]
            return ps[:, b, (i % 4) * P:(i % 4 + 1) * P]

        def pe_hgrn(pe):
            pe.wait_ge(s5_done, 4)
            for hp in range(2):
                pe.wait_ge(kp_ready, hp + 1)
                pe.wait_ge(qc_ready, hp + 1)
                if hp:
                    pe.wait_ge(o_added, 4)
                mm = nc.tensor.transpose(ps[0:META, 4, 0:P], KP[:, 0:META], ident)
                mm.then_inc(kt_turned, 1)
                for t in range(8):
                    mm = nc.tensor.transpose(ps[:, 5 + t // 4, (t % 4) * P:(t % 4 + 1) * P], KP[:, META + P * t:META + P * (t + 1)], ident)
                    if t % 4 == 3:
                        mm.then_inc(kt_turned, 1)
                pe.wait_ge(kt_copied, 3 * hp + 3)
                for c in range(16):
                    if c == 0:
                        rr, t = slice(0, META), 0
                    else:
                        rr, t = slice(64 * ((c - 1) % 2), 64 * ((c - 1) % 2) + 64), 1 + (c - 1) // 2
                    mm = nc.tensor.matmul(u_bank(c), KT[rr, t], V[rr, t, P * hp:P * hp + P], start=True, stop=True)
                mm.then_inc(u_done, 1)
                pe.wait_ge(state_ready, hp + 1)
                for half in range(2):
                    u = 2 * hp + half
                    pe.wait_ge(qe_done, 6 * u + 6)
                    pe.wait_ge(ke_done, 6 * u + 6)
                    if half:
                        pe.wait_ge(o_added, 2 * u)
                    for j in range(9):
                        if j < 8:
                            scores(pe, u, j)
                        if j >= 1:
                            outputs(pe, u, j - 1)
            pe.wait_ge(oh_ready, 1)
            for n in range(4):
                k, h = n // 2, n % 2
                for t in range(4):
                    mm = nc.tensor.transpose(ps[:, n, P * t:P * t + P], OH[:, 4 * h + t, P * k:P * k + P], ident)
                mm.then_inc(ot_done, 1)

        def scores(pe, u, j):
            tl, h = j // 2, j % 2
            n = 8 * u + j
            if n >= 4:
                pe.wait_ge(sc_masked, n - 3)
            R = slice(64 * h, 64 * h + 64)
            for c in range(2):
                cc = slice(P * tl + 64 * c, P * tl + 64 * c + 64)
                for lv in range(HL):
                    mm = nc.tensor.matmul(ps[64 * c:64 * c + 64, n % 4, HC * lv:HC * lv + HC], KE[u % 2][R, lv, cc], QE[u % 2][R, lv, cc],
                                          start=True, stop=True)
            mm.then_inc(sc_done, 1)

        def outputs(pe, u, j):
            tl, h = j // 2, j % 2
            hp, half = u // 2, u % 2
            n = 8 * u + j
            t = 4 * half + tl
            R = slice(64 * h, 64 * h + 64)
            for c in range(2):
                nc.tensor.matmul(ps[64 * c:64 * c + 64, 4 + h, 64 * tl:64 * tl + 64], QC[R, P * t + 64 * c:P * t + 64 * c + 64],
                                 SH[R, 2 * t + c, 64 * h:64 * h + 64], start=True, stop=True)
            pe.wait_ge(p_ready, n + 1)
            for c in range(2):
                S = slice(64 * c, 64 * c + 64)
                mm = nc.tensor.matmul(ps[S, 6 + c, 256 * h + 64 * tl:256 * h + 64 * tl + 64], PB[S, n % 2],
                                      V[S, 1 + t, P * hp + 64 * h:P * hp + 64 * h + 64], start=True, stop=True)
            mm.then_inc(o_done, 1)

        oS = oC
        ROT = [take(L + X) for _ in range(2)]
        PR_ = [take(2, L) for _ in range(2)]
        AT = [take(9, P) for _ in range(2)]
        OA = take(NT, 512)
        WO = take(KD, 1024)
        OSQA = take(512)
        assert oS <= 48420
        PRD, LAME, NLAM, GS8 = sml[:, 380:382], sml[:, 382:384], sml[:, 384:385], sml[:, 104:232]
        NMX, SUM, R0, R1, RW = (sml[:, 390 + 4 * i:394 + 4 * i] for i in range(5))
        ASS, HALF, ARS = sml[:, 412:416], sml[:, 416:420], sml[:, 420:424]
        rot_loaded = [sem("rot_loaded0"), sem("rot_loaded1")]
        roped, prd_ready, lam_sum, lame_ready, nlam_ready, half_ready = (
            sem(n) for n in ("roped", "prd_ready", "lam_sum", "lame_ready", "nlam_ready", "half_ready"))
        qk_done, max_ready, exp_done, a_ready, ring_ready, ring_free = (
            sem(n) for n in ("qk_done", "max_ready", "exp_done", "a_ready", "ring_ready", "ring_free"))
        asq_ready, ams_ready, oa_ready = sem("asq_ready"), sem("ams_ready"), sem("oa_ready")
        NJOB = 4 * NT

        def groups(i):
            x = list(range(i + 1))
            g = [x[b:b + 4] for b in range(0, i + 1, 4)]
            if len(g[-1]) < 4:
                g[-1].append("meta")
            else:
                g.append(["meta"])
            return g

        def step_of(kind, n):
            return n + 1 if kind == "t" else n + 2 if kind == "o" else min(4 * n + 7, NJOB + 5)

        ring = []
        for step in range(NJOB + 6):
            ring += [("t", n, g) for n in range(NJOB) if step_of("t", n) == step for g in groups(n // 4)]
            ring += [("o", n, None) for n in range(NJOB) if step_of("o", n) == step]
            ring += [("m", n, None) for n in range(NT) if step_of("m", n) == step]
        at_ready = {}
        for r, (kind, n, g) in enumerate(ring):
            if kind == "t":
                at_ready[n] = r + 1
        out_at = {n: r + 1 for r, (kind, n, g) in enumerate(ring) if kind == "o"}
        mix_at = {n: r + 1 for r, (kind, n, g) in enumerate(ring) if kind == "m"}

        def sp_attention(sp):
            sp.wait_ge(oh_ready, 1)
            sp.wait_ge(hgrn_done, 4)
            for h in range(4):
                if h >= 2:
                    sp.wait_ge(roped, h - 1)
                for b in range(4):
                    d, s = slice(32 * b, 32 * b + 32), slice(32 * (b ^ 1), 32 * (b ^ 1) + 32)
                    sp.dma_start(ROT[h % 2][d, 0:L], AK[s, h]).then_inc(rot_loaded[h % 2], 16)
                    sp.dma_start(ROT[h % 2][d, L:], AQ[s, h]).then_inc(rot_loaded[h % 2], 16)
            sp.dma_start(WO, a["w_out"].rearrange("(k p) n -> p k n", p=P)).then_inc(late_loaded, 16)

        def pool_attention(pool, link):
            nc.gpsimd.memset(HALF, -0.5).then_inc(half_ready, 1)
            pool.wait_ge(half_ready, 1)
            pool.wait_ge(gains_loaded, 32)
            link(nc.gpsimd.tensor_scalar(GS8, GS8, 1.0 - LAM_INIT, None, ALU.mult))
            for i in range(NT):
                pool.wait_ge(ams_ready, i + 1)
                link(nc.gpsimd.tensor_tensor(ARS, ASS, HALF, ALU.pow))
                o = OA[:, i].rearrange("p (h v) -> p h v", h=4)
                link(nc.gpsimd.tensor_tensor(o, o, ARS.unsqueeze(2).to_broadcast([P, 4, P]), ALU.mult))
                nc.gpsimd.tensor_tensor(o, o, GS8.unsqueeze(1).to_broadcast([P, 4, P]), ALU.mult).then_inc(oa_ready, 1)

        def dve_lambda(dve, link):
            tt = nc.vector.tensor_tensor
            v = par[0:64, P_LAM:P_LAM + 4].rearrange("p (a b) -> p a b", b=2)
            tt(PRD[0:64], v[:, :, 0], v[:, :, 1], ALU.mult).then_inc(prd_ready, 1)
            dve.wait_ge(lame_ready, 1)
            link(tt(NLAM, LAME[:, 1:2], LAME[:, 0:1], ALU.subtract))
            nc.vector.tensor_scalar(NLAM, NLAM, -LAM_INIT, None, ALU.add).then_inc(nlam_ready, 1)

        def dve_rope(dve, link, h):
            tt, stt = nc.vector.tensor_tensor, nc.vector.scalar_tensor_tensor
            cos, sin = con[:, C_COS:C_COS + L], con[:, C_SIN:C_SIN + L]
            dve.wait_ge(rot_loaded[h % 2], 128 * (h // 2 + 1))
            rk, rq = ROT[h % 2][:, 0:L], ROT[h % 2][:, L:]
            link(tt(rk, rk, sin, ALU.mult))
            link(tt(AK[:, h], AK[:, h], cos, ALU.mult))
            link(tt(AK[:, h], AK[:, h], rk, ALU.add))
            link(stt(rq, rq, SCALE, sin[:, META:], ALU.mult, ALU.mult))
            link(stt(AQ[:, h], AQ[:, h], SCALE, cos[:, META:], ALU.mult, ALU.mult))
            tt(AQ[:, h], AQ[:, h], rq, ALU.add).then_inc(roped, 1)

        def logits(c):
            return ps[:, 3 * c:3 * c + 3, :].rearrange("p b n -> p (b n)")

        def dve_attention(dve, link):
            stt = nc.vector.scalar_tensor_tensor
            dve_lambda(dve, link)
            dve.wait_ge(nlam_ready, 1)
            for n in range(NJOB + 1):
                if n < 4:
                    dve_rope(dve, link, n)
                if n < NJOB:
                    i = n // 4
                    nk = META + P * (i + 1)
                    for c in range(2):
                        dve.wait_ge(qk_done, 2 * n + c + 1)
                        s = logits(c)
                        link(nc.vector.tensor_tensor(s[:, nk - P:nk], s[:, nk - P:nk], con[:, C_MASK:C_MASK + P], ALU.add))
                        if n >= 2:
                            dve.wait_ge(exp_done, 2 * (n - 2) + c + 1)
                        nc.vector.tensor_reduce(NMX[:, 2 * (n % 2) + c:2 * (n % 2) + c + 1], s[:, 0:nk], AX.X, ALU.max,
                                                negate=True).then_inc(max_ready, 1)
                if n >= 1:
                    j = n - 1
                    o = 2 * (j % 2)
                    nk = META + P * (j // 4 + 1)
                    dve.wait_ge(exp_done, 2 * j + 2)
                    if j >= 2:
                        dve.wait_ge(ring_free, out_at[j - 2])
                    link(nc.vector.reciprocal(R1[:, o:o + 2], SUM[:, o:o + 2]))
                    link(stt(RW[:, j % 2:j % 2 + 1], SUM[:, o:o + 1], NLAM, R1[:, o + 1:o + 2], ALU.mult, ALU.mult))
                    A = PR_[j % 2]
                    stt(A[:, 0, 0:nk], A[:, 1, 0:nk], RW[:, j % 2:j % 2 + 1], A[:, 0, 0:nk], ALU.mult, ALU.add).then_inc(a_ready, 1)
                    if j % 4 == 1 and j >= 5:
                        dve_means(dve, link, j // 4 - 1)
            dve_means(dve, link, NT - 1)

        def dve_means(dve, link, i):
            dve.wait_ge(asq_ready, i + 1)
            if i:
                dve.wait_ge(oa_ready, i)
            link(nc.vector.tensor_reduce(ASS, OSQA.rearrange("p (h v) -> p h v", h=4), AX.X, ALU.add))
            nc.vector.tensor_scalar(ASS, ASS, 1.0 / P, EPS, ALU.mult, ALU.add).then_inc(ams_ready, 1)

        def act_attention(act, link):
            f = nc.scalar.activation
            act.wait_ge(lam_sum, 1)
            f(LAME, ps[:, 7, 0:2], ACT.Exp).then_inc(lame_ready, 1)
            r = 0
            for n in range(NJOB + 6):
                if n < NJOB:
                    nk = META + P * (n // 4 + 1)
                    for c in range(2):
                        act.wait_ge(max_ready, 2 * n + c + 1)
                        if n >= 2:
                            act.wait_ge(a_ready, n - 1)
                            act.wait_ge(ring_ready, at_ready[n - 2])
                        o = 2 * (n % 2) + c
                        f(PR_[n % 2][:, c, 0:nk], logits(c)[:, 0:nk], ACT.Exp, bias=NMX[:, o:o + 1],
                          accum_out=SUM[:, o:o + 1]).then_inc(exp_done, 1)
                while r < len(ring) and step_of(*ring[r][:2]) <= n:
                    act_ring(act, link, r)
                    r += 1

        def act_ring(act, link, r):
            kind, n, g = ring[r]
            f = nc.scalar.activation
            act.wait_ge(ring_ready, r + 1)
            b = ps[:, 6 + r % 2, :]
            if kind == "t":
                x = [v for v in g if v != "meta"]
                ins = None
                if x:
                    ins = nc.scalar.copy(AT[n % 2][:, x[0]:x[-1] + 1], b[:, 0:P * len(x)].rearrange("p (k q) -> p k q", q=P))
                if "meta" in g:
                    ins = nc.scalar.copy(AT[n % 2][0:META, 8], b[0:META, P * len(x):P * len(x) + P])
                ins.then_inc(ring_free, 1)
            elif kind == "o":
                i, h = n // 4, n % 4
                f(OA[:, i, P * h:P * h + P], b[:, 0:P], ACT.Identity, scale=R1[:, 2 * (n % 2):2 * (n % 2) + 1]).then_inc(ring_free, 1)
                if h == 3:
                    act.wait_ge(ring_free, r + 1)
                    if i:
                        act.wait_ge(ams_ready, i)
                    f(OSQA, OA[:, i], ACT.Square).then_inc(asq_ready, 1)
            else:
                nc.scalar.copy(AQ[:, :, P * n:P * n + P], b.rearrange("p (h q) -> p h q", h=4)).then_inc(ring_free, 1)

        def pe_attention(pe):
            pe.wait_ge(hgrn_done, 4)
            pe.wait_ge(prd_ready, 1)
            nc.tensor.matmul(ps[:, 7, 0:2], con[0:64, C_ONES:C_ONES + P], PRD[0:64], start=True, stop=True).then_inc(lam_sum, 1)
            pe.wait_ge(lame_ready, 1)
            r = 0
            for n in range(NJOB + 6):
                if n < NJOB:
                    pe_logits(pe, n)
                while r < len(ring) and step_of(*ring[r][:2]) <= n:
                    pe_ring(pe, r)
                    r += 1

        def pe_logits(pe, n):
            i, h = n // 4, n % 4
            nk = META + P * (i + 1)
            if n < 4:
                pe.wait_ge(roped, n + 1)
            for c in range(2):
                R = slice(64 * c, 64 * c + 64)
                if n >= 1:
                    pe.wait_ge(exp_done, 2 * (n - 1) + c + 1)
                for k in range(0, nk, 512):
                    w = min(512, nk - k)
                    mm = nc.tensor.matmul(logits(c)[:, k:k + w], AQ[R, h, P * i:P * i + P], AK[R, h, k:k + w], start=True, stop=True)
                mm.then_inc(qk_done, 1)

        def pe_ring(pe, r):
            kind, n, g = ring[r]
            if r >= 2:
                pe.wait_ge(ring_free, r - 1)
            b = ps[:, 6 + r % 2, :]
            if kind == "t":
                pe.wait_ge(a_ready, n + 1)
                A = PR_[n % 2][:, 0]
                for j, v in enumerate(g):
                    if v == "meta":
                        mm = nc.tensor.transpose(b[0:META, P * j:P * j + P], A[:, 0:META], ident)
                    else:
                        mm = nc.tensor.transpose(b[:, P * j:P * j + P], A[:, META + P * v:META + P * v + P], ident)
            elif kind == "o":
                i, h = n // 4, n % 4
                pe.wait_ge(ring_free, at_ready[n])
                vc = slice(512 + P * h, 512 + P * h + P)
                for k in range(i + 1):
                    nc.tensor.matmul(b[:, 0:P], AT[n % 2][:, k], V[:, 1 + k, vc], start=(k == 0), stop=False)
                mm = nc.tensor.matmul(b[:, 0:P], AT[n % 2][0:META, 8], V[0:META, 0, vc], start=False, stop=True)
            else:
                pe.wait_ge(oa_ready, n + 1)
                for h in range(4):
                    mm = nc.tensor.transpose(b[:, P * h:P * h + P], OA[:, n, P * h:P * h + P], ident)
            mm.then_inc(ring_ready, 1)

        H1 = view(oV, NT, D)
        XB, XN2 = view(oAK, 2, D), view(oAK + 2 * D, 2, D)
        XT2 = view(oAK + 4 * D, 2, KD, P)
        GF, WRT = view(oC + 22880, D), view(oC + 22880 + D, KD, 20)
        SS2, VA2, SD2, RS2 = (sml[:, 8 * i:8 * i + 8] for i in range(4))
        BR = sml[:, 430:450]
        xn_d = nc.dram_tensor("xn_d", (X, D), F32, kind="Internal").ap()
        ffn_loaded, xb_loaded = sem("ffn_loaded"), [sem("xb_loaded0"), sem("xb_loaded1")]
        out_done, h1_ready, ss2_ready, va2_ready, sd2_ready, xn2_ready = (
            sem(n) for n in ("out_done", "h1_ready", "ss2_ready", "va2_ready", "sd2_ready", "xn2_ready"))
        xn2_stored, xt2_ready, xt2_copied, log_done = (
            [sem("xn2_stored0"), sem("xn2_stored1")], sem("xt2_ready"), sem("xt2_copied"), sem("log_done"))

        def sp_out(sp):
            sp.wait_ge(ring_free, len(ring))
            sp.dma_start(GF, a["norm_ffn_g"].to_broadcast([P, D])).then_inc(ffn_loaded, 16)
            sp.dma_start(WRT, a["w_router"].rearrange("(k p) n -> p k n", p=P)).then_inc(ffn_loaded, 16)
            sp.dma_start(BR, a["b_router"].to_broadcast([P, 20])).then_inc(ffn_loaded, 16)
            for t in range(NT + 1):
                if t < NT:
                    if t >= 2:
                        sp.wait_ge(h1_ready, t - 1)
                    sp.dma_start(XB[:, t % 2], a["x"][P * t:P * t + P, :]).then_inc(xb_loaded[t % 2], 16)
                if t >= 1:
                    sp.wait_ge(xn2_ready, t)
                    sp.dma_start(xn_d[P * (t - 1):P * t, :], XN2[:, (t - 1) % 2]).then_inc(xn2_stored[(t - 1) % 2], 16)

        def act_out(act, link):
            for t in range(NT + 1):
                if t < NT:
                    act.wait_ge(h1_ready, t + 1)
                    nc.scalar.activation(OA.rearrange("p t n -> p (t n)")[:, 0:D], H1[:, t], ACT.Square,
                                         accum_out=SS2[:, t:t + 1]).then_inc(ss2_ready, 1)
                    act.wait_ge(va2_ready, t + 1)
                    nc.scalar.activation(SD2[:, t:t + 1], VA2[:, t:t + 1], ACT.Sqrt).then_inc(sd2_ready, 1)
                if t >= 1:
                    for j in range(2):
                        act.wait_ge(xt2_ready, 2 * (t - 1) + j + 1)
                        nc.scalar.copy(XT2[:, (t - 1) % 2, 4 * j:4 * j + 4],
                                       ps[:, 4 + j, :].rearrange("p (k q) -> p k q", k=4)).then_inc(xt2_copied, 1)

        def dve_out(dve, link):
            for t in range(NT):
                dve.wait_ge(out_done, t + 1)
                dve.wait_ge(xb_loaded[t % 2], 16 * (t // 2 + 1))
                if t == 0:
                    dve.wait_ge(ring_free, len(ring))
                nc.vector.tensor_tensor(H1[:, t], ps[:, 2 * (t % 2):2 * (t % 2) + 2, :].rearrange("p b n -> p (b n)"),
                                        XB[:, t % 2], ALU.add).then_inc(h1_ready, 1)
                dve.wait_ge(ss2_ready, t + 1)
                nc.vector.tensor_scalar(VA2[:, t:t + 1], SS2[:, t:t + 1], 1.0 / D, EPS, ALU.mult, ALU.add).then_inc(va2_ready, 1)
                dve.wait_ge(sd2_ready, t + 1)
                link(nc.vector.reciprocal(RS2[:, t:t + 1], SD2[:, t:t + 1]))
                if t >= 2:
                    dve.wait_ge(xn2_stored[t % 2], 16 * (t // 2))
                    dve.wait_ge(xt2_ready, 2 * (t - 1))
                if t == 0:
                    dve.wait_ge(ffn_loaded, 48)
                nc.vector.scalar_tensor_tensor(XN2[:, t % 2], H1[:, t], RS2[:, t:t + 1], GF, ALU.mult, ALU.mult).then_inc(xn2_ready, 1)

        def pe_out(pe):
            pe.wait_ge(ring_free, len(ring))
            pe.wait_ge(late_loaded, 32)
            for t in range(NT + 2):
                if t < NT:
                    if t >= 2:
                        pe.wait_ge(h1_ready, t - 1)
                    for h in range(2):
                        for k in range(KD):
                            mm = nc.tensor.matmul(ps[:, 2 * (t % 2) + h, :], mix(k)[:, P * t:P * t + P], WO[:, k, 512 * h:512 * h + 512],
                                                  start=(k == 0), stop=(k == KD - 1))
                    mm.then_inc(out_done, 1)
                if 1 <= t <= NT:
                    s = t - 1
                    pe.wait_ge(xn2_ready, s + 1)
                    for j in range(2):
                        if s:
                            pe.wait_ge(xt2_copied, 2 * s - 1 + j)
                        for k in range(4):
                            mm = nc.tensor.transpose(ps[:, 4 + j, P * k:P * k + P], XN2[:, s % 2, P * (4 * j + k):P * (4 * j + k) + P], ident)
                        mm.then_inc(xt2_ready, 1)
                if t >= 2:
                    s = t - 2
                    pe.wait_ge(xt2_copied, 2 * s + 2)
                    if s == 0:
                        pe.wait_ge(ffn_loaded, 48)
                    for k in range(KD):
                        mm = nc.tensor.matmul(ps[:, 6, 20 * s:20 * s + 20], XT2[:, s % 2, k], WRT[:, k], start=(k == 0), stop=(k == KD - 1))
                    mm.then_inc(log_done, 1)

        oS = oU
        LG = take(NT, 20)
        GM, GX, GS_, GP = take(NT), take(NT, 4), take(NT), take(NT)
        OHG, VAL, MX = take(NT, 4), take(NT, 4), take(NT)
        IG, M1, O1, M2, O2, E2 = take(NT, 4), take(NT), take(NT, 4), take(NT), take(NT, 4), take(NT)
        EXO = take(NT, 4, 4)
        OK1, OK2, OKS = take(NT, NE), take(NT, NE), take(NT, NE)
        RK, TOT, PRE = take(NT, NE), take(NT, NE), take(NT, NE)
        CNT, BLK, CB, BASE, BCMP, ECMP = take(NE), take(NE), take(NE), take(NE), take(NE, 8), take(NB, NE)
        SLF, EBF, TOKF = take(2, NT), take(NB), take(NT)
        assert oS <= oC
        W12 = sml[:, 460:476].rearrange("p (k t) -> p k t", k=2)
        slots = sml[:, 480:496].bitcast(I32).rearrange("p (k t) -> p k t", k=2)
        toks, ixb = sml[:, 496:504].bitcast(I32), sml[:, 504:506].bitcast(I32)
        eblk, zeros = sml[:, 510:510 + NB].bitcast(I32), sml[:, 545:545 + NB].bitcast(I32)
        idx_d = nc.dram_tensor("idx_d", (NB * P, 1), I32, kind="Internal").ap()
        ye_d = nc.dram_tensor("ye_d", (NB * P, D), F32, kind="Internal").ap()
        rt_gap, rt_exp, onehot_ready, rank_done, slots_ready, idx_zeroed, idx_stored = (
            sem(n) for n in ("rt_gap", "rt_exp", "onehot_ready", "rank_done", "slots_ready", "idx_zeroed", "idx_stored"))
        zeros_ready = sem("zeros_ready")

        def act_route(act, link):
            act.wait_ge(rt_gap, 1)
            nc.scalar.activation(GX, GX, ACT.Exp).then_inc(rt_exp, 1)
            act.wait_ge(rt_gap, 2)
            nc.scalar.activation(E2, E2, ACT.Exp).then_inc(rt_exp, 1)

        def pe_route(pe):
            pe.wait_ge(onehot_ready, 1)
            f = OKS.rearrange("p t e -> p (t e)")
            nc.tensor.matmul(ps[:, 0, 0:P], con[:, C_TRI:C_TRI + P], f, start=True, stop=True)
            nc.tensor.matmul(ps[:, 0, P:2 * P], con[:, C_ONES:C_ONES + P], f, start=True, stop=True).then_inc(rank_done, 1)

        def pool_route(pool, link):
            nc.gpsimd.memset(zeros[:, :], 0).then_inc(zeros_ready, 1)
            pool.wait_ge(zeros_ready, 1)
            pool.dma_start(idx_d.rearrange("(p b) o -> p (b o)", p=P), zeros[:, :]).then_inc(idx_zeroed, 16)
            pool.wait_ge(idx_zeroed, 16)
            pool.wait_ge(slots_ready, 1)
            for k in range(2):
                for t in range(NT):
                    pool.indirect_dma_start(idx_d, bass.IndirectOffsetOnAxis(ap=slots[:, k, t:t + 1], axis=0),
                                            toks[:, t:t + 1], None).then_inc(idx_stored, 16)
            pool.wait_ge(idx_stored, 16 * 2 * NT)
            for t in range(2):
                pool.wait_ge(xn2_stored[t], 16 * NT // 2)

        def dve_route(dve, link):
            tt, ts, stt, red = (nc.vector.tensor_tensor, nc.vector.tensor_scalar, nc.vector.scalar_tensor_tensor,
                                nc.vector.tensor_reduce)
            s4 = [P, NT, 4]

            def b4(v):
                return v.unsqueeze(2).to_broadcast(s4)

            def first_of_max(oh, x, m):
                link(red(m, x, AX.X, ALU.max))
                link(tt(oh, x, b4(m), ALU.is_equal))
                link(tt(VAL, oh, con[:, C_DESC4:C_DESC4 + 4].unsqueeze(1).to_broadcast(s4), ALU.mult))
                link(red(MX, VAL, AX.X, ALU.max))
                link(tt(oh, VAL, b4(MX), ALU.is_equal))

            dve.wait_ge(log_done, NT)
            link(tt(LG, ps[:, 6, 0:20 * NT].rearrange("p (t n) -> p t n", t=NT), BR.unsqueeze(1).to_broadcast([P, NT, 20]), ALU.add))
            gl = LG[:, :, 0:4]
            first_of_max(OHG, gl, GM)
            tt(GX, gl, b4(GM), ALU.subtract).then_inc(rt_gap, 1)
            link(tt(EXO, LG[:, :, 4:20].rearrange("p t (g e) -> p t g e", g=4), OHG.unsqueeze(3).to_broadcast([P, NT, 4, 4]), ALU.mult))
            link(red(IG, EXO.rearrange("p t g e -> p t e g"), AX.X, ALU.add))
            first_of_max(O1, IG, M1)
            link(stt(IG, O1, -3.0e38, IG, ALU.mult, ALU.add))
            first_of_max(O2, IG, M2)
            tt(E2, M2, M1, ALU.subtract).then_inc(rt_gap, 1)
            for o, oh in ((OK1, O1), (OK2, O2)):
                link(tt(o.rearrange("p t (g e) -> p t g e", g=4), OHG.unsqueeze(3).to_broadcast([P, NT, 4, 4]),
                        oh.unsqueeze(2).to_broadcast([P, NT, 4, 4]), ALU.mult))
            tt(OKS, OK1, OK2, ALU.add).then_inc(onehot_ready, 1)
            dve.wait_ge(rt_exp, 2)
            link(red(GS_, GX, AX.X, ALU.add))
            link(nc.vector.reciprocal(GP, GS_))
            link(ts(M1, E2, 1.0, None, ALU.add))
            link(nc.vector.reciprocal(M1, M1))
            link(tt(W12[:, 0], M1, GP, ALU.mult))
            link(tt(W12[:, 1], W12[:, 0], E2, ALU.mult))
            dve.wait_ge(rank_done, 1)
            link(nc.vector.tensor_copy(TOT, ps[:, 0, P:2 * P].rearrange("p (t e) -> p t e", t=NT)))
            link(nc.vector.memset(PRE[:, 0], 0.0))
            for t in range(1, NT):
                link(tt(PRE[:, t], PRE[:, t - 1], TOT[:, t - 1], ALU.add))
            link(tt(CNT, PRE[:, NT - 1], TOT[:, NT - 1], ALU.add))
            link(tt(RK, ps[:, 0, 0:P].rearrange("p (t e) -> p t e", t=NT), PRE, ALU.add))
            link(tt(BCMP, CNT.unsqueeze(2).to_broadcast([P, NE, 8]), con[:, C_128J:C_128J + 8].unsqueeze(1).to_broadcast([P, NE, 8]), ALU.is_gt))
            link(red(BLK, BCMP, AX.X, ALU.add))
            link(nc.vector.tensor_tensor_scan(CB, con[:, C_ONES:C_ONES + NE], BLK, 0.0, ALU.mult, ALU.add))
            link(tt(BASE, CB, BLK, ALU.subtract))
            link(ts(BASE, BASE, float(P), None, ALU.mult))
            link(tt(RK, RK, BASE.unsqueeze(1).to_broadcast([P, NT, NE]), ALU.add))
            for k, o in enumerate((OK1, OK2)):
                link(tt(o, o, RK, ALU.mult))
                link(red(SLF[:, k], o, AX.X, ALU.add))
            link(tt(ECMP, CB.unsqueeze(1).to_broadcast([P, NB, NE]), con[:, C_IOTAB:C_IOTAB + NB].unsqueeze(2).to_broadcast([P, NB, NE]), ALU.is_le))
            link(red(EBF, ECMP, AX.X, ALU.add))
            link(ts(EBF, EBF, float(NE - 1), None, ALU.min))
            link(nc.vector.tensor_copy(eblk[:, :], EBF))
            link(nc.vector.tensor_copy(toks[:, :], con[:, C_TOK:C_TOK + NT]))
            nc.vector.tensor_copy(slots[:, :, :], SLF).then_inc(slots_ready, 1)

        WGU = [view(oC + 12288 * i, 2, KD, FF) for i in range(2)]
        WDN = [view(oC + 12288 * i + 8192, FF // P, D) for i in range(2)]
        oS = oAK
        XG, XGT, YE = take(2, D), take(2, KD, P), take(2, D)
        SG, HE, HET = take(2, FF), take(2, FF), take(2, FF // P, P)
        Y12 = [take(2, D) for _ in range(2)]
        assert oS <= oC
        GFN = view(oC, D)
        OUTB = view(oC + D, 2, D)
        wgu_loaded, wdn_loaded = [sem(f"wgu_loaded{i}") for i in range(2)], [sem(f"wdn_loaded{i}") for i in range(2)]
        ix_loaded, xg_loaded = [sem(f"ix_loaded{i}") for i in range(2)], [sem(f"xg_loaded{i}") for i in range(2)]
        xgt_ready, xgt_copied, gu_done, sg_ready, he_ready, het_ready, het_copied, ye_done, ye_copied = (
            sem(n) for n in ("xgt_ready", "xgt_copied", "gu_done", "sg_ready", "he_ready", "het_ready", "het_copied", "ye_done", "ye_copied"))
        ix_seen = sem("ix_seen")
        ye_stored = [sem(f"ye_stored{i}") for i in range(2)]

        def blocks(eng, body):
            body(0, 0, True)
            body(1, 1, True)
            with eng.Fori(1, NB // 2 - 1) as j:
                for par in range(2):
                    body(2 * j + par, par, False)
            for b in range(2 * (NB // 2 - 1), NB):
                body(b, b % 2, False)

        def has(b, ahead):
            return not isinstance(b, int) or b + ahead < NB

        def loads(b, par):
            return b // 2 + 1 if isinstance(b, int) else (b - par) // 2 + 1

        def sp_experts(sp):
            sp.wait_ge(slots_ready, 1)

            def body(b, par, first):
                e = sp.value_load(eblk[0:1, bass.ds(b, 1)], min_val=0, max_val=NE - 1)
                if not first:
                    sp.wait_ge(gu_done, b - 1)
                for i, w in enumerate(("w_gate", "w_up")):
                    sp.dma_start(WGU[par][:, i], a[w][bass.ds(e, 1)].rearrange("a (k p) n -> p (a k) n", p=P)).then_inc(wgu_loaded[par], 16)
                if not first:
                    sp.wait_ge(ye_done, b - 1)
                sp.dma_start(WDN[par], a["w_down"][bass.ds(e, 1)].rearrange("a (k p) n -> p (a k) n", p=P)).then_inc(wdn_loaded[par], 16)

            blocks(sp, body)

        def pool_experts(pool):
            def body(b, par, first):
                if not first:
                    pool.wait_ge(xgt_ready, 2 * b - 2)
                pool.dma_start(ixb[:, par:par + 1], idx_d[bass.ds(b * P, P), :]).then_inc(ix_loaded[par], 16)
                pool.wait_ge(ix_loaded[par], 16 * loads(b, par))
                pool.sem_inc(ix_seen, 1)
                pool.indirect_dma_start(XG[:, par], None, xn_d, bass.IndirectOffsetOnAxis(ap=ixb[:, par:par + 1], axis=0)).then_inc(xg_loaded[par], 16)

            blocks(pool, body)

        def pe_experts(pe):
            def turn_x(b, par):
                pe.wait_ge(xg_loaded[par], 16 * loads(b, par))
                for j in range(2):
                    for k in range(4):
                        mm = nc.tensor.transpose(ps[:, 6 + j, P * k:P * k + P], XG[:, par, P * (4 * j + k):P * (4 * j + k) + P], ident)
                    mm.then_inc(xgt_ready, 1)

            def gate_up(b, par):
                pe.wait_ge(wgu_loaded[par], 32 * loads(b, par))
                pe.wait_ge(xgt_copied, 2 * b + 2)
                for i in range(2):
                    for k in range(KD):
                        mm = nc.tensor.matmul(ps[:, 2 * par + i, :], XGT[:, par, k], WGU[par][:, i, k], start=(k == 0), stop=(k == KD - 1))
                mm.then_inc(gu_done, 1)

            pe.wait_ge(slots_ready, 1)
            turn_x(0, 0)
            gate_up(0, 0)
            pe.wait_ge(xgt_copied, 2)
            turn_x(1, 1)

            def body(b, par, first):
                pe.wait_ge(he_ready, b + 1)
                pe.wait_ge(xgt_copied, 2 * b + 4 if has(b, 1) else 2 * NB)
                for k in range(FF // P):
                    mm = nc.tensor.transpose(ps[:, 6, P * k:P * k + P], HE[:, par, P * k:P * k + P], ident)
                mm.then_inc(het_ready, 1)
                if has(b, 1):
                    gate_up(b + 1, 1 - par)
                pe.wait_ge(het_copied, b + 1)
                if has(b, 2):
                    turn_x(b + 2, par)
                if not (isinstance(b, int) and b == 0):
                    pe.wait_ge(ye_copied, 2 * b)
                pe.wait_ge(wdn_loaded[par], 16 * loads(b, par))
                for h in range(2):
                    for k in range(FF // P):
                        mm = nc.tensor.matmul(ps[:, 4 + h, :], HET[:, par, k], WDN[par][:, k, 512 * h:512 * h + 512], start=(k == 0), stop=(k == 3))
                mm.then_inc(ye_done, 1)

            blocks(pe, body)

        def act_experts(act):
            def copy_x(b, par):
                for j in range(2):
                    act.wait_ge(xgt_ready, 2 * b + 1 + j)
                    nc.scalar.copy(XGT[:, par, 4 * j:4 * j + 4], ps[:, 6 + j, :].rearrange("p (k q) -> p k q", k=4)).then_inc(xgt_copied, 1)

            def silu(b, par):
                act.wait_ge(gu_done, b + 1)
                nc.scalar.activation(SG[:, par], ps[:, 2 * par, :], ACT.Silu).then_inc(sg_ready, 1)

            copy_x(0, 0)
            silu(0, 0)
            copy_x(1, 1)

            def body(b, par, first):
                act.wait_ge(het_ready, b + 1)
                nc.scalar.copy(HET[:, par], ps[:, 6, :].rearrange("p (k q) -> p k q", k=4)).then_inc(het_copied, 1)
                if has(b, 1):
                    silu(b + 1, 1 - par)
                if has(b, 2):
                    copy_x(b + 2, par)
                act.wait_ge(ye_copied, 2 * b + 2)
                act.dma_start(ye_d[bass.ds(b * P, P), :], YE[:, par]).then_inc(ye_stored[par], 16)

            blocks(act, body)

        def dve_experts(dve):
            def hidden(b, par):
                dve.wait_ge(sg_ready, b + 1)
                nc.vector.tensor_tensor(HE[:, par], SG[:, par], ps[:, 2 * par + 1, :], ALU.mult).then_inc(he_ready, 1)

            hidden(0, 0)

            def body(b, par, first):
                if has(b, 1):
                    hidden(b + 1, 1 - par)
                dve.wait_ge(ye_done, b + 1)
                if not first:
                    dve.wait_ge(ye_stored[par], 16 * (loads(b, par) - 1))
                for h in range(2):
                    nc.vector.tensor_copy(YE[:, par, 512 * h:512 * h + 512], ps[:, 4 + h, :]).then_inc(ye_copied, 1)

            blocks(dve, body)

        y_gathered = [sem(f"y_gathered{i}") for i in range(2)]
        y_added, ob_ready = sem("y_added"), sem("ob_ready")
        out_stored = [sem("out_stored0"), sem("out_stored1")]

        def sp_final(sp):
            sp.wait_ge(ye_copied, 2 * NB)
            sp.dma_start(GFN, a["final_norm_g"].to_broadcast([P, D])).then_inc(late_loaded, 16)
            for t in range(NT):
                sp.wait_ge(ob_ready, t + 1)
                sp.dma_start(out[P * t:P * t + P, :], OUTB[:, t % 2]).then_inc(out_stored[t % 2], 16)
            for i in range(2):
                sp.wait_ge(out_stored[i], 16 * NT // 2)

        def pool_final(pool):
            for i in range(2):
                pool.wait_ge(ye_stored[i], 16 * ((NB + 1 - i) // 2))
            for t in range(NT):
                if t >= 2:
                    pool.wait_ge(y_added, 2 * (t - 1))
                for k in range(2):
                    pool.indirect_dma_start(Y12[t % 2][:, k], None, ye_d,
                                            bass.IndirectOffsetOnAxis(ap=slots[:, k, t:t + 1], axis=0)).then_inc(y_gathered[t % 2], 16)

        def act_final(act):
            for t in range(NT):
                act.wait_ge(y_added, 2 * t + 2)
                nc.scalar.activation(SG.rearrange("p a b -> p (a b)"), H1[:, t], ACT.Square, accum_out=SS2[:, t:t + 1]).then_inc(ss2_ready, 1)
                act.wait_ge(va2_ready, NT + t + 1)
                nc.scalar.activation(SD2[:, t:t + 1], VA2[:, t:t + 1], ACT.Sqrt).then_inc(sd2_ready, 1)

        def dve_final(dve, link):
            dve.wait_ge(late_loaded, 48)
            for t in range(NT):
                dve.wait_ge(y_gathered[t % 2], 32 * (t // 2 + 1))
                for k in range(2):
                    nc.vector.scalar_tensor_tensor(H1[:, t], Y12[t % 2][:, k], W12[:, k, t:t + 1], H1[:, t], ALU.mult, ALU.add).then_inc(y_added, 1)
                    dve.wait_ge(y_added, 2 * t + k + 1)
                dve.wait_ge(ss2_ready, NT + t + 1)
                nc.vector.tensor_scalar(VA2[:, t:t + 1], SS2[:, t:t + 1], 1.0 / D, EPS, ALU.mult, ALU.add).then_inc(va2_ready, 1)
                dve.wait_ge(sd2_ready, NT + t + 1)
                link(nc.vector.reciprocal(RS2[:, t:t + 1], SD2[:, t:t + 1]))
                if t >= 2:
                    dve.wait_ge(out_stored[t % 2], 16 * (t // 2))
                nc.vector.scalar_tensor_tensor(OUTB[:, t % 2], H1[:, t], RS2[:, t:t + 1], GFN, ALU.mult, ALU.mult).then_inc(ob_ready, 1)

        def sp_rest(sp):
            sp_s5(sp)
            sp_hgrn(sp)
            sp_attention(sp)
            sp_out(sp)
            sp_experts(sp)
            sp_final(sp)

        def act_silu(act):
            for s, v in projected:
                act.wait_ge(s, v)
            nc.scalar.activation(HQ, HQ, ACT.Silu)
            nc.scalar.activation(V[:, 1:9, 256:512], V[:, 1:9, 256:512], ACT.Silu).then_inc(silu_ready, 1)

        def act_rest(act, link):
            act_silu(act)
            act_s5(act, link)
            act_hgrn(act, link)
            act_attention(act, link)
            act_out(act, link)
            act_route(act, link)
            act_experts(act)
            act_final(act)

        def dve_rest(dve, link):
            dve_s5(dve, link)
            dve_hgrn_bounds(dve, link)
            dve_hgrn(dve, link)
            dve_attention(dve, link)
            dve_out(dve, link)
            dve_route(dve, link)
            dve_experts(dve)
            dve_final(dve, link)

        def pe_rest(pe):
            pe_s5(pe)
            pe_hgrn(pe)
            pe_attention(pe)
            pe_out(pe)
            pe_route(pe)
            pe_experts(pe)

        def pool_rest(pool, link):
            pool_s5(pool, link)
            pool_hgrn(pool, link)
            pool_attention(pool, link)
            pool_route(pool, link)
            pool_experts(pool)
            pool_final(pool)


        with nc.Block() as block:
            @block.sync
            def _(sp):
                sp_project(sp)
                if stage < 2:
                    sp.wait_ge(proj_evac[0], 27)
                    sp.wait_ge(proj_evac[1], 27)
                    return
                sp_rest(sp)

            @block.scalar
            def _(act):
                link = Chain(act, act_chain)
                act_project(act)
                if stage >= 2:
                    act_rest(act, link)

            @block.vector
            def _(dve):
                link = Chain(dve, dve_chain)
                dve_project(dve, link)
                if stage >= 2:
                    dve_rest(dve, link)

            @block.tensor
            def _(pe):
                pe_project(pe)
                if stage >= 2:
                    pe_rest(pe)

            @block.gpsimd
            def _(pool):
                link = Chain(pool, pool_chain)
                if stage >= 2:
                    pool_rest(pool, link)


def layout(inputs):
    g = {k: np.asarray(v) for k, v in inputs.items()}
    par = np.zeros((P, P_END), np.float32)
    par[:, P_GMIX:P_GMIX + 8] = g["norm_mix_g"].reshape(8, P).T
    for j, name in enumerate(("s5_lambda_re", "s5_lambda_im")):
        par[:, P_S5 + 16 * j:P_S5 + 16 * j + 16] = np.concatenate([g[name][0].T] * 2)
    par[:, P_S5 + 32:P_S5 + 48] = g["s5_log_dt"][0][None, :]
    par[:, P_D:P_D + 2] = g["s5_d"].reshape(2, P).T
    par[:, P_LB:P_LB + 2] = g["hgrn_lower_bounds"].reshape(2, P).T
    for j, name in enumerate(("diff_lambda_q1", "diff_lambda_k1", "diff_lambda_q2", "diff_lambda_k2")):
        par[0:64, P_LAM + j] = g[name][0]
    b = [g["s5_b_re"][0].transpose(1, 0, 2).reshape(64, 256), g["s5_b_im"][0].transpose(1, 0, 2).reshape(64, 256)]
    c = [g["s5_c_re"][0].transpose(2, 0, 1).reshape(64, 256), g["s5_c_im"][0].transpose(2, 0, 1).reshape(64, 256)]
    par[:, P_B1:P_B1 + 256], par[:, P_B2:P_B2 + 256] = np.concatenate(b), np.concatenate(b[::-1])
    par[:, P_C1:P_C1 + 256], par[:, P_C2:P_C2 + 256] = np.concatenate(c), np.concatenate(c[::-1])
    router = np.concatenate([g["moe_w_group"][0], g["moe_w_expert"][0]], axis=1)
    return {
        "consts": constants(), "params": par, "x": g["x"][0], "meta_tokens": g["meta_tokens"],
        "w_in": g["w_in"][0], "w_glu": g["s5_w_glu"][0], "w_out": g["w_out"][0],
        "hgrn_norm_g": g["hgrn_norm_g"], "subln_g": g["diff_subln_g"], "norm_ffn_g": g["norm_ffn_g"],
        "final_norm_g": g["final_norm_g"][None], "w_router": router,
        "b_router": np.concatenate([g["moe_b_group"], g["moe_b_expert"]], axis=1),
        "w_gate": g["moe_w_gate"][0], "w_up": g["moe_w_up"][0], "w_down": g["moe_w_down"][0],
    }


def kernel(_stage=99, **inputs):
    import concourse.bacc as bacc
    from concourse.bass_utils import run_bass_kernel_spmd

    nc = bacc.Bacc("TRN2", target_bir_lowering=False, num_devices=1)
    arrays = {f"in_{k}": np.ascontiguousarray(v) for k, v in layout(inputs).items()}
    a = {k[3:]: nc.dram_tensor(k, v.shape, mybir.dt.from_np(v.dtype), kind="ExternalInput").ap() for k, v in arrays.items()}
    out = nc.dram_tensor("out", (X, D), F32, kind="ExternalOutput").ap()
    build(nc, a, out, _stage)
    r = run_bass_kernel_spmd(nc, [arrays], core_ids=[0])
    return np.asarray(r.results[0]["out"]).reshape(1, X, D)
```

```python
from contextlib import ExitStack

import numpy as np

import concourse.bass as bass
from concourse import mybir

F32 = mybir.dt.float32
I32 = mybir.dt.int32
ACT = mybir.ActivationFunctionType
ALU = mybir.AluOpType
AX = mybir.AxisListType

P = 128
D = 1024
KD = D // P
META = 16
X = 1024
L = META + X
NT = X // P
EPS = 1e-6

S5_G, S5_C, S5_N = 16, 16, 64
S5_T = P // S5_C
S5_K = L // S5_T
S5_KM = META // S5_T

HC = 64
HL = 6
NH = 4
LAM_INIT = 0.8 - 0.6 * 1.0
SCALE = 64 ** -0.5

NG, NPG, NE, FF = 4, 4, 16, 512
SLOTS = X * 2
NB = (SLOTS + NE * (P - 1)) // P
LEAST = SLOTS // P
NB += NB % 2

C_ID, C_MASK, C_TRI, C_ONES, C_HM = 0, 128, 256, 384, 512
C_TOK, C_DESC4, C_J9, C_128J, C_SG, C_IOTAB = 896, 912, 916, 928, 936, 937
C_COS = 976
C_SIN = C_COS + L
C_END = C_SIN + L
C_SWAP = C_END
P_GMIX, P_S5, P_D, P_LB, P_LAM = 0, 8, 56, 58, 60
P_B1, P_B2, P_C1, P_C2 = 64, 64 + 256, 64 + 512, 64 + 768
P_END = 64 + 1024

MEM = 48432


def constants():
    c = np.zeros((P, C_END + P), np.float32)
    i = np.arange(P)
    c[:, C_ID:C_ID + P] = np.eye(P)
    c[:, C_MASK:C_MASK + P] = np.where(i[None, :] <= i[:, None], 0.0, -1e30)
    c[:, C_TRI:C_TRI + P] = i[:, None] < i[None, :]
    c[:, C_ONES:C_ONES + P] = 1.0
    s, t = (i % HC)[:, None], np.arange(HC)[None, :]
    for lv in range(HL):
        if lv == 0:
            m = (s // 2 == t // 2) & (s <= t)
        else:
            b = 2 << lv
            m = (s // b == t // b) & (s % b < b // 2) & (t % b >= b // 2)
        c[:, C_HM + lv * HC:C_HM + (lv + 1) * HC] = m
    c[:, C_TOK:C_TOK + NT] = P * np.arange(NT)[None, :] + i[:, None]
    c[:, C_DESC4:C_DESC4 + 4] = [4, 3, 2, 1]
    c[:, C_J9:C_J9 + 9] = np.arange(9)
    c[:, C_128J:C_128J + 8] = 128 * np.arange(8)
    c[:, C_SG] = np.where(i < 64, -1.0, 1.0)
    c[:, C_IOTAB:C_IOTAB + NB] = np.arange(NB)
    c[i ^ 32, C_SWAP + i] = 1.0
    inv = (np.float32(1.0) / (np.float32(10000.0) ** (np.arange(0, 64, 2, dtype=np.float32) / np.float32(64)))).astype(np.float32)
    ang = (np.arange(L, dtype=np.float32)[:, None] * inv[None, :]).astype(np.float32)
    cos, sin = np.cos(ang).T, np.sin(ang).T
    c[:, C_COS:C_COS + L] = np.concatenate([cos] * 4)
    c[:, C_SIN:C_SIN + L] = np.concatenate([-sin, sin, -sin, sin])
    return c


class Chain:

    def __init__(self, eng, sem):
        self.eng, self.sem, self.n = eng, sem, 0

    def __call__(self, ins):
        self.n += 1
        ins.then_inc(self.sem, 1)
        self.eng.wait_ge(self.sem, self.n)


def build(nc, a, out, stage=99):
    ctx = ExitStack()
    with ctx:
        def sem(name):
            return ctx.enter_context(nc.semaphore(name))

        con = ctx.enter_context(nc.sbuf_tensor("con", [P, C_END], F32))
        par = ctx.enter_context(nc.sbuf_tensor("par", [P, P_END], F32))
        mem = ctx.enter_context(nc.sbuf_tensor("mem", [P, MEM], F32))
        sml = ctx.enter_context(nc.sbuf_tensor("sml", [P, 604], F32))
        ps = ctx.enter_context(nc.psum_tensor("ps", [P, 8, 512], F32))

        def view(off, *shape):
            n = int(np.prod(shape))
            v = mem[:, off:off + n]
            if len(shape) == 2:
                v = v.rearrange("p (a b) -> p a b", a=shape[0])
            if len(shape) == 3:
                v = v.rearrange("p (a b c) -> p a b c", a=shape[0], b=shape[1])
            return v

        ident = con[:, C_ID:C_ID + P]
        SWAP = con[:, C_MASK:C_MASK + P]

        oV = 0
        oAK = oV + 9 * 1024
        oHF = oAK + 4 * L
        oU = oHF + 2 * L
        oHQ = oU + 2 * L
        oAQ = oHQ + 2 * X
        oC = oAQ + 4 * X
        V = view(oV, 9, 1024)
        AK, HF, AQ, HQ = view(oAK, 4, L), view(oHF, 2, L), view(oAQ, 4, X), view(oHQ, 2, X)
        UP = view(oU, 2, S5_T, S5_K)
        XT = view(oC, KD, L)
        oW = oC + KD * L
        oW1 = oW + 2 * L + S5_G * P
        WR = [view(o, KD, 512) for o in (oW, oW1)]
        oX = oW1 + 4096
        XN = view(oX, 3, 1024)
        JUNK = view(oX + 3072, 1024)
        SSQ, VAR, SD, RSTD = (sml[:, i * 9:i * 9 + 9] for i in range(4))

        params_loaded = sem("params_loaded")
        x_loaded = [sem(f"x_loaded{i}") for i in range(3)]
        w_loaded = [sem(f"w_loaded{i}") for i in range(6)]
        ssq_ready, var_ready, sd_ready, xn_ready = sem("ssq_ready"), sem("var_ready"), sem("sd_ready"), sem("xn_ready")
        xt_ready, xt_copied = sem("xt_ready"), sem("xt_copied")
        proj_done, zero_ready = sem("proj_done"), sem("zero_ready")
        proj_evac = sem("proj_evac")
        tables_loaded, swapped, roped, up_loaded = sem("tables_loaded"), sem("swapped"), sem("roped"), sem("up_loaded")
        dve_chain, act_chain, pool_chain = sem("dve_chain"), sem("act_chain"), sem("pool_chain")

        SECT = [(0, 512, 0), (512, 768, 1), (768, 1280, 0), (2304, 2816, 1), (1280, 1792, 0), (1792, 2304, 1)]
        CH = [(0, META), (META, META + 512), (META + 512, L)]
        jobs = []
        for m in range(2):
            for c in range(3):
                jobs.append((0, "u", m, c))
        for m in range(2):
            for c in (1, 2):
                jobs.append((0, "hq", m, c))
        for m in range(2):
            for c in range(3):
                jobs.append((1, "hf", m, c))
        for t in range(9):
            jobs.append((2, "vl", 0, t))
        for t in range(9):
            jobs.append((3, "vr", 0, t))
        for m in range(4):
            for c in (1, 2):
                jobs.append((4, "aq", m, c))
        for m in range(4):
            for c in range(3):
                jobs.append((5, "ak", m, c))
        last_of = {j[0]: n + 1 for n, j in enumerate(jobs)}
        first_of = {}
        for n, j in enumerate(jobs):
            first_of.setdefault(j[0], n)

        PREP = {12 + r: r for r in range(12)}
        GATES = {26 + i: i for i in range(3)}
        TURNS = [n for n, j in enumerate(jobs) if j[1] in ("aq", "ak")]
        NTQ = sum(j[1] == "aq" for j in jobs)

        def rows(t):
            return META if t == 0 else P

        def cols(t):
            return (0, META) if t == 0 else (META + P * (t - 1), META + P * t)

        ye_d = nc.dram_tensor("ye_d", (NB * P, D), F32, kind="Internal").ap()
        ye_zeroed, zero_tile = sem("ye_zeroed"), V[:, 1:3, 512:1024]
        ZEROED = NB - LEAST

        def pool_project(pool, link):
            nc.gpsimd.memset(zero_tile, 0.0).then_inc(zero_ready, 1)
            pool.wait_ge(zero_ready, 1)
            pool.wait_ge(xt_ready, 18)
            for b in range(NB - ZEROED, NB):
                pool.dma_start(ye_d[P * b:P * b + P, :].rearrange("p (a n) -> p a n", a=2), zero_tile).then_inc(ye_zeroed, 16)
            pool.wait_ge(up_stored, 32)
            nc.gpsimd.memset(TO, 0.0).then_inc(to_zeroed, 1)
            pool.wait_ge(prep_done, 8)
            link(nc.gpsimd.memset(RM, 1.0))
            link(nc.gpsimd.memset(RM[:, 0:1], 0.0))
            nc.gpsimd.memset(RM[:, META::HC], 0.0).then_inc(rm_ready, 1)

        def sp_project(sp):
            sp.dma_start(par[:, :], a["params"]).then_inc(params_loaded, 16)
            for lo, hi in ((0, C_MASK), (C_TRI, C_COS)):
                sp.dma_start(con[:, lo:hi], a["consts"][:, lo:hi]).then_inc(params_loaded, 16)
            for t in range(9):
                if t >= 3:
                    sp.wait_ge(xt_ready, 2 * (t - 2))
                src = a["meta_tokens"] if t == 0 else a["x"][P * (t - 1):P * t, :]
                sp.dma_start(XN[0:rows(t), t % 3, :], src).then_inc(x_loaded[t % 3], 16)
            sp.dma_start(con[:, C_COS:C_END], a["consts"][:, C_COS:C_END]).then_inc(tables_loaded, 16)
            sp.dma_start(SWAP, a["consts"][:, C_SWAP:C_SWAP + P]).then_inc(tables_loaded, 16)
            for s in range(2, 6):
                lo, hi, slot = SECT[s]
                sp.wait_ge(proj_done, last_of[s - 2])
                sp.dma_start(WR[slot][:, :, 0:hi - lo],
                             a["w_in"].rearrange("(k p) n -> p k n", p=P)[:, :, lo:hi]).then_inc(w_loaded[s], 16)
                if s == 3:
                    sp_s5_up(sp)
                if s == 4:
                    sp_s5_toeplitz(sp)

        def act_project(act, link):
            for s in range(2):
                lo, hi, slot = SECT[s]
                act.dma_start(WR[slot][:, :, 0:hi - lo],
                              a["w_in"].rearrange("(k p) n -> p k n", p=P)[:, :, lo:hi]).then_inc(w_loaded[s], 16)
            for t in range(9):
                R = rows(t)
                act.wait_ge(x_loaded[t % 3], 16 * (t // 3 + 1))
                nc.scalar.activation(JUNK[0:R, :], XN[0:R, t % 3, :], ACT.Square,
                                     accum_out=SSQ[0:R, t:t + 1]).then_inc(ssq_ready, 1)
                act.wait_ge(var_ready, t + 1)
                nc.scalar.activation(SD[0:R, t:t + 1], VAR[0:R, t:t + 1], ACT.Sqrt).then_inc(sd_ready, 1)
            act_s5_angles(act)
            for n in range(len(jobs)):
                evacuate(act, n)
                if n in PREP:
                    act_s5_prep(act, PREP[n])
                if n in GATES:
                    act_gates(act, link, GATES[n])
                if n + 1 == last_of[2]:
                    act.wait_ge(proj_evac, n + 1)
                    nc.scalar.activation(HQ, HQ, ACT.Silu)
                    nc.scalar.activation(V[:, 1:9, 256:512], V[:, 1:9, 256:512], ACT.Silu).then_inc(silu_ready, 1)

        def dve_norm(dve, link, t):
            R = rows(t)
            dve.wait_ge(ssq_ready, t + 1)
            nc.vector.tensor_scalar(VAR[0:R, t:t + 1], SSQ[0:R, t:t + 1], 1.0 / D, EPS, ALU.mult, ALU.add).then_inc(var_ready, 1)
            dve.wait_ge(sd_ready, t + 1)
            link(nc.vector.reciprocal(RSTD[0:R, t:t + 1], SD[0:R, t:t + 1]))
            nc.vector.tensor_scalar(XN[0:R, t % 3, :], XN[0:R, t % 3, :], RSTD[0:R, t:t + 1], None, ALU.mult).then_inc(xn_ready, 1)

        def dve_gain(dve, t):
            R = rows(t)
            lo, hi = cols(t)
            for j in range(2):
                dve.wait_ge(xt_ready, 2 * t + j + 1)
                nc.vector.tensor_tensor(XT[:, 4 * j:4 * j + 4, lo:hi],
                                        ps[:, 6 + j, 0:4 * R].rearrange("p (k t) -> p k t", k=4),
                                        par[:, P_GMIX + 4 * j:P_GMIX + 4 * j + 4].unsqueeze(2).to_broadcast([P, 4, R]),
                                        ALU.mult).then_inc(xt_copied, 1)

        def dve_project(dve, link):
            dve.wait_ge(params_loaded, 48)
            for t in range(10):
                if t < 9:
                    dve_norm(dve, link, t)
                if t >= 1:
                    dve_gain(dve, t - 1)
            dve_s5_phasors(dve, link)
            dve_s5_maps(dve, link)

        def evacuate(act, n):
            s, kind, m, c = jobs[n]
            copy = nc.scalar.copy
            act.wait_ge(proj_done, n + 1)
            b = ps[:, n % 6, :]
            if n == first_of[3]:
                act.wait_ge(ye_zeroed, 16 * ZEROED)
            if n == first_of[4]:
                act.wait_ge(cum_ready, 1)
            if n == first_of[5]:
                act.wait_ge(kk_moved, 1)
            if kind in ("vl", "vr"):
                R = rows(c)
                w = 256 if (kind == "vl" and c == 0) else 512
                o = 0 if kind == "vl" else 512
                ins = copy(V[0:R, c, o:o + w], b[0:R, 0:w])
            elif kind == "u":
                lo, hi = CH[c]
                ins = copy(UP[:, m, :, lo // S5_T:hi // S5_T], b[:, 0:hi - lo].rearrange("p (k s) -> p s k", s=S5_T))
            else:
                lo, hi = CH[c]
                dst = {"hq": HQ, "hf": HF, "ak": AK, "aq": AQ}[kind]
                sh = META if kind in ("hq", "aq") else 0
                ins = copy(dst[:, m, lo - sh:hi - sh], b[:, 0:hi - lo])
            ins.then_inc(proj_evac, 1)

        def pe_project(pe):
            pe.wait_ge(params_loaded, 48)
            for t in range(9):
                R = rows(t)
                pe.wait_ge(xn_ready, t + 1)
                for j in range(2):
                    if t >= 1:
                        pe.wait_ge(xt_copied, 2 * t + j - 1)
                    for k in range(4):
                        mm = nc.tensor.transpose(ps[:, 6 + j, k * R:(k + 1) * R], XN[0:R, t % 3, (4 * j + k) * P:(4 * j + k + 1) * P],
                                                 ident[0:R, 0:R])
                    mm.then_inc(xt_ready, 1)
            pe.wait_ge(xt_copied, 18)
            for n, (s, kind, m, c) in enumerate(jobs):
                if first_of[s] == n:
                    pe.wait_ge(w_loaded[s], 16)
                if n >= 6:
                    pe.wait_ge(proj_evac, n - 5)
                W = WR[SECT[s][2]]
                for k in range(KD):
                    if kind in ("vl", "vr"):
                        R = rows(c)
                        lo, hi = cols(c)
                        w = 256 if (kind == "vl" and c == 0) else 512
                        mm = nc.tensor.matmul(ps[0:R, n % 6, 0:w], XT[:, k, lo:hi], W[:, k, 0:w], start=(k == 0), stop=(k == KD - 1))
                    else:
                        lo, hi = CH[c]
                        m0 = m + (2 if kind == "hq" else 0)
                        mm = nc.tensor.matmul(ps[:, n % 6, 0:hi - lo], W[:, k, m0 * P:(m0 + 1) * P], XT[:, k, lo:hi],
                                              start=(k == 0), stop=(k == KD - 1))
                mm.then_inc(proj_done, 1)
                if n in PREP:
                    pe_s5_prep(pe, PREP[n])
                if n - 1 in TURNS:
                    pe_turn(pe, TURNS.index(n - 1))
            pe_turn(pe, len(TURNS) - 1)

        def turned(r):
            _, kind, m, c = jobs[TURNS[r]]
            lo, hi = CH[c]
            return (AQ[:, m, lo - META:hi - META] if kind == "aq" else AK[:, m, lo:hi]), slice(lo, hi)

        def pe_turn(pe, r):
            pe.wait_ge(proj_evac, TURNS[r] + 1)
            if r >= 2:
                pe.wait_ge(roped, r - 1)
            x, _ = turned(r)
            if r == 0:
                pe.wait_ge(tables_loaded, 32)
            nc.tensor.matmul(ps[:, 6 + r % 2, 0:x.shape[-1]], SWAP, x, start=True, stop=True).then_inc(swapped, 1)

        def dve_rope(dve, link, r):
            tt, stt = nc.vector.tensor_tensor, nc.vector.scalar_tensor_tensor
            x, cols_ = turned(r)
            b = ps[:, 6 + r % 2, 0:x.shape[-1]]
            cos, sin = con[:, C_COS:C_COS + L][:, cols_], con[:, C_SIN:C_SIN + L][:, cols_]
            dve.wait_ge(swapped, r + 1)
            if r < NTQ:
                link(stt(b, b, SCALE, sin, ALU.mult, ALU.mult))
                link(stt(x, x, SCALE, cos, ALU.mult, ALU.mult))
            else:
                link(tt(b, b, sin, ALU.mult))
                link(tt(x, x, cos, ALU.mult))
            tt(x, x, b, ALU.add).then_inc(roped, 1)

        NJ = len(jobs)
        projected = [(proj_evac, NJ)]

        oS = oX
        def take(*shape):
            nonlocal oS
            v = view(oS, *shape)
            oS += int(np.prod(shape))
            return v
        WIN = [take(S5_G, P), take(S5_G, P)]
        L1 = take(S5_G, S5_T + 1, S5_C)
        UC, UI, MJ, PR, PI, SPR, SPI = (take(S5_T + 1, S5_G) for _ in range(7))
        BX2 = mem[:, oS:oS + 2 * S5_G * S5_C]
        BB, BX = take(S5_G, S5_C), take(S5_G, S5_C)
        q = [take(S5_G) for _ in range(14)]
        SNI, SN = take(2, S5_G), take(2, S5_G)
        assert oS <= MEM
        TO = view(oU, S5_G, P)
        TA, TB = view(oAK, 2080), view(oAK + 2080, 2080)
        G3 = TA[:, 0:2048].rearrange("p (g s c) -> p g s c", g=S5_G, s=S5_T)
        H3 = TB[:, 0:2048].rearrange("p (g s c) -> p g s c", g=S5_G, s=S5_T)
        GW = [view(oAQ + i * S5_G * P, S5_G, P) for i in range(2)]
        GA, GB = (v.rearrange("p g (s c) -> p g s c", s=S5_T) for v in GW)
        HS = TA[0:S5_C, 0:2048].rearrange("p (g n) -> p g n", g=S5_G)
        KK, L2 = view(oW, 2, L), view(oW + 2 * L, S5_G, S5_T, S5_C)
        oS = oC
        COS, SIN = take(S5_G, S5_K), take(S5_G, S5_K)
        T1, T2 = take(S5_G * S5_K), take(S5_G * S5_K)
        assert oS <= oW
        oS = oW1
        US = take(S5_G, S5_K)
        WGLU = take(2, 512)
        assert oS <= oX
        XR = T1.rearrange("p (g k) -> p g k", g=S5_G)
        XS = T2.rearrange("p (g k) -> p g k", g=S5_G)
        YO = T1[:, 0:2048].rearrange("p (g k) -> p g k", g=S5_G)
        YT = WIN[0].rearrange("p (m t) k -> p m t k", m=2)
        GT = WIN[1].rearrange("p (m t) k -> p m (t k)", m=2)
        SGM = T2[:, 0:2048].rearrange("p (m t) -> p m t", m=2)
        MIX = [view(oU, 2, X), HQ, AQ]

        def mix(k):
            return MIX[0][:, k, :] if k < 2 else MIX[1][:, k - 2, :] if k < 4 else MIX[2][:, k - 4, :]

        up_d = nc.dram_tensor("up_d", (2 * P, S5_T, S5_K), F32, kind="Internal").ap()
        y_d = nc.dram_tensor("y_d", (2 * P, S5_T, P), F32, kind="Internal").ap()
        dt_ready, phase_ready, sin_ready = sem("dt_ready"), sem("phase_ready"), sem("sin_ready")
        mag_ready, g_ready = sem("mag_ready"), sem("g_ready")
        l_ready, prep_done, prep_copied = sem("l_ready"), sem("prep_done"), sem("prep_copied")
        to_zeroed, to_loaded, up_stored, us_loaded = sem("to_zeroed"), sem("to_loaded"), sem("up_stored"), sem("us_loaded")
        x_done, x_turned, w_ready = sem("x_done"), sem("x_turned"), sem("w_ready")
        y_done, y_copied, y_stored, y_loaded = sem("y_done"), sem("y_copied"), sem("y_stored"), sem("y_loaded")
        yu_ready, gelu_ready, glu_done, glu_gate, s5_done = sem("yu_ready"), sem("gelu_ready"), sem("glu_done"), sem("glu_gate"), sem("s5_done")
        late_loaded = sem("late_loaded")
        UNITS = [(g, min(g + 3, S5_G)) for g in range(0, S5_G, 3)]

        def sp_s5_up(sp):
            sp.wait_ge(proj_evac, 6)
            for m in range(2):
                sp.dma_start(up_d[m * P:(m + 1) * P], UP[:, m]).then_inc(up_stored, 16)

        def sp_s5_toeplitz(sp):
            sp.wait_ge(to_zeroed, 1)
            sp.wait_ge(prep_copied, 12)
            for s in range(S5_T):
                sp.dma_start(TO[S5_C * s:S5_C * (s + 1), :, S5_C * s:], HS[:, :, 0:P - S5_C * s]).then_inc(to_loaded, 16)

        def sp_s5(sp):
            sp.wait_ge(proj_done, NJ)
            sp.wait_ge(up_stored, 32)
            src = up_d.rearrange("(g c) s k -> s c g k", c=S5_C)
            for s in range(S5_T):
                sp.dma_start(US[S5_C * s:S5_C * (s + 1)], src[s]).then_inc(us_loaded, 16)
            sp.dma_start(WGLU, a["w_glu"].rearrange("(k p) n -> p k n", p=P)).then_inc(late_loaded, 16)
            sp.wait_ge(y_done, 4)
            for m in range(2):
                sp.dma_start(UP[:, m], up_d[m * P:(m + 1) * P]).then_inc(up_loaded, 16)
            sp.wait_ge(y_copied, 4)
            dst = y_d.rearrange("(g c) t k -> t c g k", c=S5_C)
            for t in range(S5_T):
                sp.dma_start(dst[t], YO[S5_C * t:S5_C * (t + 1)]).then_inc(y_stored, 16)
            sp.wait_ge(y_stored, 16 * S5_T)
            for m in range(2):
                sp.dma_start(YT[:, m], y_d[m * P:(m + 1) * P]).then_inc(y_loaded, 16)

        def act_s5_angles(act):
            act.wait_ge(params_loaded, 48)
            nc.scalar.activation(q[0], par[:, P_S5 + 32:P_S5 + 48], ACT.Exp).then_inc(dt_ready, 1)
            act.wait_ge(phase_ready, 1)
            nc.scalar.activation(q[8], q[1], ACT.Exp).then_inc(mag_ready, 1)
            act.wait_ge(phase_ready, 2)
            nc.scalar.activation(SN, SNI, ACT.Sin).then_inc(sin_ready, 1)

        def act_s5_prep(act, r):
            act.wait_ge(prep_done, r + 1)
            b = ps[:, 6 + r % 2, :]
            if r < 8:
                ins = nc.scalar.copy(WIN[r // 4][:, 4 * (r % 4):4 * (r % 4) + 4, :], b.rearrange("p (g n) -> p g n", g=4))
            else:
                ins = nc.scalar.copy(HS[:, 4 * (r - 8):4 * (r - 8) + 4, :], b[0:S5_C].rearrange("p (g n) -> p g n", g=4))
            ins.then_inc(prep_copied, 1)

        def act_s5(act, link):
            for b in range(4):
                act.wait_ge(y_done, b + 1)
                nc.scalar.copy(YO[:, 4 * b:4 * b + 4, :], ps[:, b, :].rearrange("p (g n) -> p g n", g=4)).then_inc(y_copied, 1)
            for m in range(2):
                act.wait_ge(yu_ready, m + 1)
                nc.scalar.activation(GT[:, m], YT[:, m].rearrange("p t k -> p (t k)"), ACT.Gelu_apprx_tanh).then_inc(gelu_ready, 1)
            for m in range(2):
                for h in range(2):
                    act.wait_ge(glu_done, 2 * m + h + 1)
                    nc.scalar.activation(SGM[:, m, 512 * h:512 * h + 512], ps[:, 2 * m + h, :], ACT.Sigmoid).then_inc(glu_gate, 1)

        def dve_s5_phasors(dve, link):
            lr, li = par[:, P_S5:P_S5 + 16], par[:, P_S5 + 16:P_S5 + 32]
            sg = con[:, C_SG:C_SG + 1]
            tt, ts, stt = nc.vector.tensor_tensor, nc.vector.tensor_scalar, nc.vector.scalar_tensor_tensor
            dt_, lrdt, th, kf, em, e2, zr, den, mag, t0, t1, fr, fi, sfi = q[:14]
            dve.wait_ge(dt_ready, 1)
            tt(lrdt, lr, dt_, ALU.mult).then_inc(phase_ready, 1)
            link(tt(th, li, dt_, ALU.mult))
            MAGIC = 12582912.0
            link(ts(kf, th, float(1 / (2 * np.pi)), MAGIC, ALU.mult, ALU.add))
            link(ts(kf, kf, -MAGIC, None, ALU.add))
            for part in (6.28125, 0.0019350051879882812, 3.0199157e-07):
                link(stt(th, kf, -part, th, ALU.mult, ALU.add))
            link(ts(SNI[:, 0], th, 3.1415925, -3.1415925, ALU.min, ALU.max))
            ts(SNI[:, 1], th, 0.5, None, ALU.mult).then_inc(phase_ready, 1)
            dve.wait_ge(phase_ready, 1)
            link(ts(t0, lrdt, 1.0 / 8, 1.0, ALU.mult, ALU.add))
            for j in range(7, 1, -1):
                link(tt(t0, t0, lrdt, ALU.mult))
                link(ts(t0, t0, 1.0 / j, 1.0, ALU.mult, ALU.add))
            link(tt(em, t0, lrdt, ALU.mult))
            link(tt(t1, lrdt, lrdt, ALU.mult))
            link(ts(t1, t1, 0.16, None, ALU.is_gt))
            dve.wait_ge(mag_ready, 1)
            link(ts(e2, mag, -1.0, None, ALU.add))
            link(nc.vector.copy_predicated(em, t1.bitcast(I32), e2))
            link(ts(MJ[:, 1], em, 1.0, None, ALU.add))
            link(nc.vector.memset(MJ[:, 0], 1.0))
            dve.wait_ge(sin_ready, 1)
            link(nc.vector.memset(UC[:, 0], 1.0))
            link(nc.vector.memset(UI[:, 0], 0.0))
            link(nc.vector.tensor_copy(UI[:, 1], SN[:, 0]))
            link(tt(t0, SN[:, 1], SN[:, 1], ALU.mult))
            link(ts(t1, t0, -2.0, None, ALU.mult))
            link(ts(UC[:, 1], t1, 1.0, None, ALU.add))

            def cmul(oc, os_, ac, as_, bc, bs, shape):
                n = int(np.prod(shape[1:]))
                pa, pb = TA[:, 0:n], TA[:, 1040:1040 + n]
                if len(shape) == 3:
                    pa, pb = (v.rearrange("p (a b) -> p a b", a=shape[1]) for v in (pa, pb))
                link(tt(pa, ac, bc, ALU.mult))
                link(tt(pb, as_, bs, ALU.mult))
                link(tt(oc, pa, pb, ALU.subtract))
                link(tt(pa, ac, bs, ALU.mult))
                link(tt(pb, as_, bc, ALU.mult))
                link(tt(os_, pa, pb, ALU.add))

            for m in (1, 2, 4):
                sh = [P, m, S5_G]
                b = [v[:, m:m + 1].to_broadcast(sh) for v in (UC, UI, MJ)]
                cmul(UC[:, m + 1:2 * m + 1], UI[:, m + 1:2 * m + 1], UC[:, 1:m + 1], UI[:, 1:m + 1], b[0], b[1], sh)
                link(tt(MJ[:, m + 1:2 * m + 1], MJ[:, 1:m + 1], b[2], ALU.mult))
            link(tt(PR, MJ, UC, ALU.mult))
            link(tt(PI, MJ, UI, ALU.mult))
            link(ts(SPR, PR, sg, None, ALU.mult))
            link(ts(SPI, PI, sg, None, ALU.mult))
            link(tt(t0, em, UC[:, 1], ALU.mult))
            link(tt(zr, t0, t1, ALU.add))
            link(tt(den, lr, lr, ALU.mult))
            link(tt(t0, li, li, ALU.mult))
            link(tt(den, den, t0, ALU.add))
            link(nc.vector.reciprocal(den, den))
            link(tt(t0, zr, lr, ALU.mult))
            link(tt(t1, PI[:, 1], li, ALU.mult))
            link(tt(t0, t0, t1, ALU.add))
            link(tt(fr, t0, den, ALU.mult))
            link(tt(t0, PI[:, 1], lr, ALU.mult))
            link(tt(t1, zr, li, ALU.mult))
            link(tt(t0, t0, t1, ALU.subtract))
            link(tt(fi, t0, den, ALU.mult))
            link(ts(sfi, fi, sg, None, ALU.mult))

        def dve_s5_maps(dve, link):
            tt, ts = nc.vector.tensor_tensor, nc.vector.tensor_scalar
            sg, fr, sfi = con[:, C_SG:C_SG + 1], q[11], q[13]
            B1, B2, C1, C2 = (par[:, o:o + 256].rearrange("p (g c) -> p g c", g=S5_G) for o in (P_B1, P_B2, P_C1, P_C2))
            g2 = [P, S5_G, S5_C]
            ta, tb = (TA[:, o:o + 256].rearrange("p (g c) -> p g c", g=S5_G) for o in (0, 256))
            bf, bs = fr.unsqueeze(2).to_broadcast(g2), sfi.unsqueeze(2).to_broadcast(g2)
            for o, u, v, op in ((BB, B1, B2, ALU.add), (BX, B2, B1, ALU.subtract)):
                link(tt(ta, u, bf, ALU.mult))
                link(tt(tb, v, bs, ALU.mult))
                link(tt(o, ta, tb, op))

            def powers(tab, lo, n, rev=False):
                v = tab[:, lo:lo + n].rearrange("p s g -> p g s")
                if rev:
                    v = v[:, :, ::-1]
                return v.unsqueeze(3).to_broadcast([P, S5_G, n, S5_C])

            def rep(v, n):
                return v.unsqueeze(2).to_broadcast([P, S5_G, n, S5_C])

            link(tt(G3, rep(BB, 8), powers(PR, 0, 8, True), ALU.mult))
            link(tt(H3, rep(BX, 8), powers(SPI, 0, 8, True), ALU.mult))
            tt(GA, G3, H3, ALU.add).then_inc(g_ready, 1)
            dve.wait_ge(g_ready, 1)
            link(tt(G3, rep(BB, 8), powers(PI, 0, 8, True), ALU.mult))
            link(tt(H3, rep(BX, 8), powers(SPR, 0, 8, True), ALU.mult))
            tt(GB, G3, H3, ALU.subtract).then_inc(g_ready, 1)
            link(tt(L1, rep(C1, 9), powers(SPR, 0, 9), ALU.mult))
            dve.wait_ge(g_ready, 2)
            for lo, n in ((0, 8), (8, 1)):
                t3 = TB[:, 0:256 * n].rearrange("p (g s c) -> p g s c", g=S5_G, s=n)
                link(tt(t3, rep(C2, n), powers(PI, lo, n), ALU.mult))
                ins = stt_neg(L1[:, :, lo:lo + n], t3)
                if lo == 8:
                    ins.then_inc(l_ready, 1)
                else:
                    link(ins)
            dve_hgrn_bounds(dve, link)
            dve_gates(dve, link)
            dve.wait_ge(tables_loaded, 32)
            for r in range(NTQ):
                dve_rope(dve, link, r)
            dve.wait_ge(proj_done, last_of[4])
            nc.vector.tensor_copy(KK, KT_).then_inc(kk_moved, 1)
            for lo in range(0, 8, 2):
                t3 = BX2.rearrange("p (g s c) -> p g s c", g=S5_G, s=2)
                l2 = L2[:, :, lo:lo + 2]
                link(tt(l2, rep(C1, 2), powers(SPI, lo + 1, 2), ALU.mult))
                link(tt(t3, rep(C2, 2), powers(PR, lo + 1, 2), ALU.mult))
                link(tt(l2, l2, t3, ALU.subtract))
            for r in range(NTQ, len(TURNS)):
                dve_rope(dve, link, r)

        def dve_s5(dve, link):
            tt, stt = nc.vector.tensor_tensor, nc.vector.scalar_tensor_tensor
            dve.wait_ge(proj_done, NJ)
            link(nc.vector.memset(COS[:, :, 0], 1.0))
            link(nc.vector.memset(SIN[:, :, 0], 0.0))
            link(nc.vector.tensor_copy(COS[:, :, 1], UC[:, 8]))
            link(nc.vector.tensor_copy(SIN[:, :, 1], UI[:, 8]))
            for m in (1, 2, 4, 8, 16, 32, 64, 128):
                w = min(m, S5_K - 1 - m)
                sh = [P, S5_G, w]
                n = S5_G * w
                pa, pb = (T2[:, o:o + n].rearrange("p (g k) -> p g k", g=S5_G) for o in (0, 1040))
                bc, bs = (v[:, :, m:m + 1].to_broadcast(sh) for v in (COS, SIN))
                ac, as_, oc, os_ = COS[:, :, 1:w + 1], SIN[:, :, 1:w + 1], COS[:, :, m + 1:m + 1 + w], SIN[:, :, m + 1:m + 1 + w]
                link(tt(pa, ac, bc, ALU.mult))
                link(tt(pb, as_, bs, ALU.mult))
                link(tt(oc, pa, pb, ALU.subtract))
                link(tt(pa, ac, bs, ALU.mult))
                link(tt(pb, as_, bc, ALU.mult))
                link(tt(os_, pa, pb, ALU.add))
            for n, (lo, hi) in enumerate(UNITS):
                b = 2 * (n % 4)
                w = (hi - lo) * S5_K
                dve.wait_ge(x_done, n + 1)
                link(tt(XR[:, lo:hi], ps[:, b, 0:w].rearrange("p (g k) -> p g k", k=S5_K), COS[:, lo:hi], ALU.mult))
                tt(XS[:, lo:hi], ps[:, b + 1, 0:w].rearrange("p (g k) -> p g k", k=S5_K), SIN[:, lo:hi], ALU.mult).then_inc(x_turned, 1)
                dve.wait_ge(x_turned, n + 1)
                link(tt(XR[:, lo:hi], XR[:, lo:hi], XS[:, lo:hi], ALU.add))
            for g in range(S5_G):
                ins = nc.vector.tensor_tensor_scan(XS[:, g], MJ[:, 8, g:g + 1].to_broadcast([P, S5_K]), XR[:, g], 0.0, ALU.mult, ALU.add)
            link(ins)
            tt(COS, COS, XS, ALU.mult).then_inc(w_ready, 1)
            tt(SIN, SIN, XS, ALU.mult).then_inc(w_ready, 1)
            for m in range(2):
                dve.wait_ge(y_loaded, 32)
                dve.wait_ge(up_loaded, 32)
                stt(YT[:, m], UP[:, m, :, S5_KM:], par[:, P_D + m:P_D + m + 1], YT[:, m], ALU.mult, ALU.add).then_inc(yu_ready, 1)
            for m in range(2):
                for h in range(2):
                    dve.wait_ge(glu_done, 4 + 2 * m + h + 1)
                    dve.wait_ge(glu_gate, 2 * m + h + 1)
                    tt(mix(m).rearrange("p (k t) -> p t k", t=S5_T)[:, 4 * h:4 * h + 4],
                       ps[:, 4 + 2 * m + h, :].rearrange("p (t k) -> p t k", t=4),
                       SGM[:, m, 512 * h:512 * h + 512].rearrange("p (t k) -> p t k", t=4), ALU.mult).then_inc(s5_done, 1)

        def stt_neg(x, y):
            return nc.vector.scalar_tensor_tensor(x, x, -1.0, y, ALU.mult, ALU.subtract)

        def pe_s5_prep(pe, r):
            if r >= 2:
                pe.wait_ge(prep_copied, r - 1)
            if r < 8:
                pe.wait_ge(g_ready, r // 4 + 1)
            else:
                pe.wait_ge(l_ready, 1)
            for j in range(4):
                g = 4 * (r % 4) + j
                o = ps[:, 6 + r % 2, j * P:(j + 1) * P]
                if r < 8:
                    mm = nc.tensor.transpose(o, GW[r // 4][:, g], ident)
                else:
                    mm = nc.tensor.matmul(o[0:S5_C], BB[:, g], L1[:, g, 0:S5_T].rearrange("p t c -> p (t c)"), start=True, stop=True)
            mm.then_inc(prep_done, 1)

        def pe_s5(pe):
            for s, v in projected:
                pe.wait_ge(s, v)
            pe.wait_ge(roped, len(TURNS))
            pe.wait_ge(us_loaded, 16 * S5_T)
            pe.wait_ge(prep_copied, 12)
            for n, (lo, hi) in enumerate(UNITS):
                b = 2 * (n % 4)
                if n >= 4:
                    pe.wait_ge(x_turned, n - 3)
                for g in range(lo, hi):
                    for w in range(2):
                        mm = nc.tensor.matmul(ps[:, b + w, (g - lo) * S5_K:(g - lo + 1) * S5_K], WIN[w][:, g], US[:, g], start=True, stop=True)
                mm.then_inc(x_done, 1)
            pe.wait_ge(x_turned, len(UNITS))
            pe.wait_ge(to_loaded, 16 * S5_T)
            pe.wait_ge(w_ready, 2)
            for g in range(S5_G):
                o = ps[:, g // 4, (g % 4) * P:(g % 4 + 1) * P]
                nc.tensor.matmul(o, TO[:, g], US[:, g, S5_KM:], start=True, stop=False)
                nc.tensor.matmul(o, L1[:, g, 1:].rearrange("p t c -> p (t c)"), COS[:, g, S5_KM - 1:S5_K - 1], start=False, stop=False)
                mm = nc.tensor.matmul(o, L2[:, g].rearrange("p t c -> p (t c)"), SIN[:, g, S5_KM - 1:S5_K - 1], start=False, stop=True)
                if g % 4 == 3:
                    mm.then_inc(y_done, 1)
            pe.wait_ge(late_loaded, 16)
            pe.wait_ge(gelu_ready, 2)
            pe.wait_ge(y_copied, 4)
            for n, m in enumerate((2, 3, 0, 1)):
                for h in range(2):
                    for k in range(2):
                        mm = nc.tensor.matmul(ps[:, 2 * n + h, :], WGLU[:, k, m * P:(m + 1) * P], GT[:, k, 512 * h:512 * h + 512],
                                              start=(k == 0), stop=(k == 1))
                    mm.then_inc(glu_done, 1)

        CU = HF
        ZT, KT_ = view(oAK, 2, L), view(oAK + 2 * L, 2, L)
        RM = view(oAQ, L)
        oS = oC
        QC, KP, OH = take(X), take(L), take(NT, 256)
        DE = take(3, 512)
        KT = take(9, P)
        TM = take(2, HL * HC)
        PB = take(2, HC)
        assert oS <= oW
        oS = oW + 2 * L
        QE, KE = [take(HL, 512) for _ in range(2)], [take(HL, 512) for _ in range(2)]
        SH = take(X // HC, P)
        assert oS <= MEM
        OSQ = QE[0].rearrange("p a b -> p (a b)")[:, 0:2048].rearrange("p (t c) -> p t c", t=NT)
        GN, GS = sml[:, 40:104], sml[:, 104:232]
        LBD, LBE, LBW, LBV, LBF, LFL, OML, L1P, LC0 = (sml[:, 240 + 2 * i:242 + 2 * i] for i in range(9))
        DEC, OMS, OSD, ORS = sml[:, 260:277], sml[:, 280:312], sml[:, 312:344], sml[:, 344:376]
        gains_loaded = sem("gains_loaded")
        lb_dve, lb_act = sem("lb_dve"), sem("lb_act")
        silu_ready = sem("silu_ready")
        zl_ready, ls_ready, ksig_ready, gap_ready, gapl_ready, lf_ready = (
            sem(n) for n in ("zl_ready", "ls_ready", "ksig_ready", "gap_ready", "gapl_ready", "lf_ready"))
        rm_ready, kk_moved, cum_ready, qdec_ready, kd_ready, kdec_ready, qc_ready, kp_ready = (
            sem(n) for n in ("rm_ready", "kk_moved", "cum_ready", "qdec_ready", "kd_ready", "kdec_ready", "qc_ready", "kp_ready"))
        kt_turned, kt_copied, u_done, state_ready = sem("kt_turned"), sem("kt_copied"), sem("u_done"), sem("state_ready")
        d_ready, e_ready, qe_done, ke_done = sem("d_ready"), sem("e_ready"), sem("qe_done"), sem("ke_done")
        sc_done, sc_masked, p_ready, o_done, o1_copied, o_added = (
            sem(n) for n in ("sc_done", "sc_masked", "p_ready", "o_done", "o1_copied", "o_added"))
        osq_ready, oms_ready, osd_ready, oh_ready, ot_done, hgrn_done = (
            sem(n) for n in ("osq_ready", "oms_ready", "osd_ready", "oh_ready", "ot_done", "hgrn_done"))
        LN2_64 = float(64 * np.log(2.0))

        def sp_hgrn(sp):
            sp.dma_start(GN, a["hgrn_norm_g"].to_broadcast([P, 64])).then_inc(gains_loaded, 16)
            sp.dma_start(GS, a["subln_g"].to_broadcast([P, P])).then_inc(gains_loaded, 16)
            sp.wait_ge(swapped, len(TURNS))
            sp.dma_start(con[:, C_MASK:C_MASK + P], a["consts"][:, C_MASK:C_MASK + P]).then_inc(gains_loaded, 16)

        def pool_hgrn(pool, link):
            pool.wait_ge(s5_done, 4)
            for u in range(4):
                hp, half = u // 2, u % 2
                c0 = 512 * half
                if u >= 2:
                    pool.wait_ge(sc_done, 8 * (u - 1))
                for lv in range(HL):
                    pool.wait_ge(e_ready, 7 * u + (1 if lv == 0 else 2 + lv))
                    sl = 1 if lv == 0 else (lv + 1) % 3
                    nc.gpsimd.tensor_tensor(KE[u % 2][:, lv], KK[:, hp, META + c0:META + c0 + 512], DE[:, sl], ALU.mult).then_inc(ke_done, 1)

        def act_gates(act, link, step):
            f = nc.scalar.activation
            if step == 0:
                act.wait_ge(lb_dve, 1)
                f(LBE, LBD, ACT.Exp).then_inc(lb_act, 1)
                act.wait_ge(to_loaded, 16 * S5_T)
                act.wait_ge(proj_evac, last_of[1])
                link(f(ZT, HF, ACT.Abs))
                link(f(ZT, ZT, ACT.Exp, scale=-1.0))
                f(ZT, ZT, ACT.Ln, bias=1.0).then_inc(zl_ready, 1)
                act.wait_ge(lb_dve, 2)
                f(LFL, LBF, ACT.Ln, scale=float(2.0 ** 64)).then_inc(lb_act, 1)
                f(L1P, OML, ACT.Ln).then_inc(lb_act, 1)
            elif step == 1:
                act.wait_ge(ls_ready, 1)
                f(KT_, KT_, ACT.Exp).then_inc(ksig_ready, 1)
            else:
                act.wait_ge(gap_ready, 1)
                link(f(ZT, ZT, ACT.Abs))
                link(f(ZT, ZT, ACT.Exp, scale=-1.0))
                f(ZT, ZT, ACT.Ln, bias=1.0).then_inc(gapl_ready, 1)

        def act_hgrn(act, link):
            f = nc.scalar.activation
            act.wait_ge(s5_done, 4)
            for hp in range(2):
                act.wait_ge(cum_ready, 1)
                if hp:
                    act.wait_ge(o_added, 4)
                f(QC, CU[:, hp, META:], ACT.Exp).then_inc(qdec_ready, 1)
                act.wait_ge(kd_ready, hp + 1)
                f(KP, KP, ACT.Exp).then_inc(kdec_ready, 1)
                f(DEC[:, 0:1], CU[:, hp, META - 1:META], ACT.Exp)
                f(DEC[:, 1:17], CU[:, hp, META + HC - 1::HC], ACT.Exp).then_inc(kdec_ready, 1)
                for b in range(3):
                    act.wait_ge(kt_turned, 3 * hp + b + 1)
                    if b == 0:
                        ins = nc.scalar.copy(KT[0:META, 0], ps[0:META, 4, 0:P])
                    else:
                        ins = nc.scalar.copy(KT[:, 4 * b - 3:4 * b + 1], ps[:, 4 + b, :].rearrange("p (t c) -> p t c", t=4))
                    ins.then_inc(kt_copied, 1)
                if hp == 0:
                    act_levels(act, 0)
                for half in range(2):
                    u = 2 * hp + half
                    if u < 3:
                        act_levels(act, u + 1)
                    act.wait_ge(o_done, 8 * u + 8)
                    for r in range(2):
                        R = slice(64 * r, 64 * r + 64)
                        for h in range(2):
                            ins = nc.scalar.copy(OH[R, 4 * half:4 * half + 4, P * hp + 64 * h:P * hp + 64 * h + 64],
                                                 ps[R, 6 + r, 256 * h:256 * h + 256].rearrange("p (t v) -> p t v", t=4))
                    ins.then_inc(o1_copied, 1)
            act.wait_ge(o_added, 8)
            f(OSQ, OH, ACT.Square).then_inc(osq_ready, 1)
            act.wait_ge(oms_ready, 1)
            f(OSD, OMS, ACT.Sqrt).then_inc(osd_ready, 1)
            for n in range(4):
                k, h = n // 2, n % 2
                act.wait_ge(ot_done, n + 1)
                nc.scalar.copy(mix(2 + k)[:, 512 * h:512 * h + 512], ps[:, n, :]).then_inc(hgrn_done, 1)

        def act_levels(act, u):
            f = nc.scalar.activation
            act.wait_ge(d_ready, 6 * u + 1)
            f(DE[:, 1], DE[:, 0], ACT.Exp, scale=-1.0).then_inc(e_ready, 1)
            f(DE[:, 0], DE[:, 0], ACT.Exp).then_inc(e_ready, 1)
            for lv in range(1, HL):
                act.wait_ge(d_ready, 6 * u + lv + 1)
                sl = (lv + 1) % 3
                f(DE[:, sl], DE[:, sl], ACT.Exp).then_inc(e_ready, 1)

        def dve_hgrn_bounds(dve, link):
            tt, ts = nc.vector.tensor_tensor, nc.vector.tensor_scalar
            lb = par[:, P_LB:P_LB + 2]
            tt(LBD, lb, lb, ALU.subtract).then_inc(lb_dve, 1)
            dve.wait_ge(lb_act, 1)
            link(nc.vector.reciprocal(LBW, LBE))
            link(tt(LBW, LBW, LBE, ALU.mult))
            link(tt(LBV, LBW, LBW, ALU.subtract))
            link(ts(LBF, LBV, 1e-30, None, ALU.max))
            link(tt(LC0, LBV, LBF, ALU.subtract))
            ts(OML, LBV, -1.0, 1.0, ALU.mult, ALU.add).then_inc(lb_dve, 1)

        def dve_gates(dve, link):
            ts, stt = nc.vector.tensor_scalar, nc.vector.scalar_tensor_tensor
            dve.wait_ge(zl_ready, 1)
            link(stt(KT_, HF, 0.0, ZT, ALU.max, ALU.add))
            ts(KT_, KT_, -1.0, None, ALU.mult).then_inc(ls_ready, 1)
            link(stt(HF, HF, 0.0, ZT, ALU.min, ALU.subtract))
            dve.wait_ge(lb_act, 3)
            link(ts(LFL, LFL, -LN2_64, None, ALU.add))
            for m in range(2):
                link(ts(HF[:, m], HF[:, m], L1P[:, m:m + 1], None, ALU.add))
                ins = ts(ZT[:, m], HF[:, m], LFL[:, m:m + 1], None, ALU.subtract)
            ins.then_inc(gap_ready, 1)
            dve.wait_ge(ksig_ready, 1)
            for m in range(2):
                link(ts(KT_[:, m], KT_[:, m], OML[:, m:m + 1], LC0[:, m:m + 1], ALU.mult, ALU.add))
            dve.wait_ge(gapl_ready, 1)
            for m in range(2):
                link(stt(HF[:, m], HF[:, m], LFL[:, m:m + 1], ZT[:, m], ALU.max, ALU.add))
            dve.wait_ge(rm_ready, 1)
            for m in range(2):
                ins = nc.vector.tensor_tensor_scan(HF[:, m], RM, HF[:, m], 0.0, ALU.mult, ALU.add)
            ins.then_inc(cum_ready, 1)
            dve.wait_ge(cum_ready, 1)

        def dve_hgrn(dve, link):
            tt, ts, stt = nc.vector.tensor_tensor, nc.vector.tensor_scalar, nc.vector.scalar_tensor_tensor
            for hp in range(2):
                if hp:
                    dve.wait_ge(qdec_ready, 2)
                for lo, n, w in ((0, 1, META), (META, 16, HC)):
                    cu = CU[:, hp, lo:lo + n * w].rearrange("p (n w) -> p n w", n=n)
                    ins = tt(KP[:, lo:lo + n * w].rearrange("p (n w) -> p n w", n=n),
                             cu[:, :, w - 1:w].to_broadcast([P, n, w]), cu, ALU.subtract)
                ins.then_inc(kd_ready, 1)
                dve.wait_ge(silu_ready, 1)
                dve.wait_ge(qdec_ready, hp + 1)
                tt(QC, QC, HQ[:, hp], ALU.mult).then_inc(qc_ready, 1)
                dve.wait_ge(kdec_ready, 2 * hp + 1)
                tt(KP, KP, KK[:, hp], ALU.mult).then_inc(kp_ready, 1)
                if hp == 0:
                    for n in range(len(LEVEL_STEPS)):
                        dve_level_step(dve, 0, n)
                dve.wait_ge(u_done, hp + 1)
                dve.wait_ge(kdec_ready, 2 * hp + 2)
                for c in range(16):
                    uc = u_bank(c)
                    if c == 0:
                        ins = nc.vector.tensor_copy(SH[:, 0], uc)
                    else:
                        ins = stt(SH[:, c], SH[:, c - 1], DEC[:, c:c + 1], uc, ALU.mult, ALU.add)
                    if c < 15:
                        link(ins)
                ins.then_inc(state_ready, 1)
                for half in range(2):
                    dve_scores(dve, 2 * hp + half)
            dve.wait_ge(osq_ready, 1)
            dve.wait_ge(o_added, 8)
            link(nc.vector.tensor_reduce(OMS, OSQ.rearrange("p t (h v) -> p (t h) v", h=4), AX.X, ALU.add))
            ts(OMS, OMS, 1.0 / 64, EPS, ALU.mult, ALU.add).then_inc(oms_ready, 1)
            dve.wait_ge(osd_ready, 1)
            link(nc.vector.reciprocal(ORS, OSD))
            dve.wait_ge(gains_loaded, 48)
            o4 = OH.rearrange("p t (h v) -> p (t h) v", h=4)
            link(tt(o4, o4, ORS.unsqueeze(2).to_broadcast([P, 32, 64]), ALU.mult))
            link(tt(o4, o4, GN.unsqueeze(1).to_broadcast([P, 32, 64]), ALU.mult))
            tt(OH, OH, V[:, 1:9, 256:512], ALU.mult).then_inc(oh_ready, 1)

        LEVEL_STEPS = [("gaps", 0), ("gaps", 1)]
        for lv in range(HL):
            LEVEL_STEPS += [("queries", lv)] + [("gaps", lv + 2)] * (lv + 2 < HL)

        def dve_level_step(dve, u, n):
            tt = nc.vector.tensor_tensor
            hp, half = u // 2, u % 2
            lo = META + 512 * half
            what, lv = LEVEL_STEPS[n]
            sl = 0 if lv == 0 else (lv + 1) % 3
            if n == 0 and u >= 2:
                dve.wait_ge(sc_done, 8 * (u - 1))
            if what == "queries":
                dve.wait_ge(e_ready, 7 * u + 2 + lv)
                tt(QE[u % 2][:, lv], HQ[:, hp, lo - META:lo - META + 512], DE[:, sl], ALU.mult).then_inc(qe_done, 1)
                return
            B = 2 << lv
            if lv < 2 and u or lv in (2, 4, 5):
                dve.wait_ge(qe_done, 6 * u + (0, 0, 1, 0, 2, 3)[lv])
            if lv == 0:
                if u:
                    dve.wait_ge(ke_done, 6 * u)
            elif lv >= 3:
                dve.wait_ge(ke_done, 6 * u + lv - 2)
            cu = CU[:, hp, lo:lo + 512].rearrange("p (n b) -> p n b", b=B)
            de = DE[:, sl].rearrange("p (n b) -> p n b", b=B)
            if lv == 0:
                tt(de, cu, cu[:, :, 0:1].to_broadcast([P, 512 // B, B]), ALU.subtract).then_inc(d_ready, 1)
            else:
                h = B // 2
                ref = cu[:, :, h - 1:h].to_broadcast([P, 512 // B, h])
                tt(de[:, :, 0:h], ref, cu[:, :, 0:h], ALU.subtract)
                tt(de[:, :, h:B], cu[:, :, h:B], ref, ALU.subtract).then_inc(d_ready, 1)

        def dve_scores(dve, u):
            hm = con[:, C_HM:C_HM + HL * HC]
            hp, half = u // 2, u % 2
            for j in range(8):
                n = 8 * u + j
                dve.wait_ge(sc_done, n + 1)
                nc.vector.tensor_tensor(TM[:, n % 2], ps[:, n % 4, 0:HL * HC], hm, ALU.mult).then_inc(sc_masked, 1)
                dve.wait_ge(sc_masked, n + 1)
                if n >= 2:
                    dve.wait_ge(o_done, n - 1)
                nc.vector.tensor_reduce(PB[:, n % 2], TM[:, n % 2].rearrange("p (l t) -> p t l", l=HL), AX.X, ALU.add).then_inc(p_ready, 1)
                if u < 3:
                    for k in range(len(LEVEL_STEPS) * j // 8, len(LEVEL_STEPS) * (j + 1) // 8):
                        dve_level_step(dve, u + 1, k)
            dve.wait_ge(o_done, 8 * u + 8)
            dve.wait_ge(o1_copied, u + 1)
            for h in range(2):
                o = OH[:, 4 * half:4 * half + 4, P * hp + 64 * h:P * hp + 64 * h + 64]
                nc.vector.tensor_tensor(o, o, ps[:, 4 + h, 0:256].rearrange("p (t v) -> p t v", t=4), ALU.add).then_inc(o_added, 1)

        def u_bank(c):
            i = (c + 1) // 2 if c % 2 or c == 0 else (c - 2) // 2
            b = (i // 4) if c % 2 or c == 0 else (3, 7)[i // 4]
            return ps[:, b, (i % 4) * P:(i % 4 + 1) * P]

        def pe_hgrn(pe):
            pe.wait_ge(s5_done, 4)
            for hp in range(2):
                pe.wait_ge(kp_ready, hp + 1)
                pe.wait_ge(qc_ready, hp + 1)
                if hp:
                    pe.wait_ge(o_added, 4)
                mm = nc.tensor.transpose(ps[0:META, 4, 0:P], KP[:, 0:META], ident)
                mm.then_inc(kt_turned, 1)
                for t in range(8):
                    mm = nc.tensor.transpose(ps[:, 5 + t // 4, (t % 4) * P:(t % 4 + 1) * P], KP[:, META + P * t:META + P * (t + 1)], ident)
                    if t % 4 == 3:
                        mm.then_inc(kt_turned, 1)
                pe.wait_ge(kt_copied, 3 * hp + 3)
                for c in range(16):
                    if c == 0:
                        rr, t = slice(0, META), 0
                    else:
                        rr, t = slice(64 * ((c - 1) % 2), 64 * ((c - 1) % 2) + 64), 1 + (c - 1) // 2
                    mm = nc.tensor.matmul(u_bank(c), KT[rr, t], V[rr, t, P * hp:P * hp + P], start=True, stop=True)
                mm.then_inc(u_done, 1)
                pe.wait_ge(state_ready, hp + 1)
                for half in range(2):
                    u = 2 * hp + half
                    pe.wait_ge(qe_done, 6 * u + 6)
                    pe.wait_ge(ke_done, 6 * u + 6)
                    if half:
                        pe.wait_ge(o_added, 2 * u)
                    for j in range(9):
                        if j < 8:
                            scores(pe, u, j)
                        if j >= 1:
                            outputs(pe, u, j - 1)
            pe.wait_ge(oh_ready, 1)
            for n in range(4):
                k, h = n // 2, n % 2
                for t in range(4):
                    mm = nc.tensor.transpose(ps[:, n, P * t:P * t + P], OH[:, 4 * h + t, P * k:P * k + P], ident)
                mm.then_inc(ot_done, 1)

        def scores(pe, u, j):
            tl, h = j // 2, j % 2
            n = 8 * u + j
            if n >= 4:
                pe.wait_ge(sc_masked, n - 3)
            R = slice(64 * h, 64 * h + 64)
            for c in range(2):
                cc = slice(P * tl + 64 * c, P * tl + 64 * c + 64)
                for lv in range(HL):
                    mm = nc.tensor.matmul(ps[64 * c:64 * c + 64, n % 4, HC * lv:HC * lv + HC], KE[u % 2][R, lv, cc], QE[u % 2][R, lv, cc],
                                          start=True, stop=True)
            mm.then_inc(sc_done, 1)

        def outputs(pe, u, j):
            tl, h = j // 2, j % 2
            hp, half = u // 2, u % 2
            n = 8 * u + j
            t = 4 * half + tl
            R = slice(64 * h, 64 * h + 64)
            for c in range(2):
                nc.tensor.matmul(ps[64 * c:64 * c + 64, 4 + h, 64 * tl:64 * tl + 64], QC[R, P * t + 64 * c:P * t + 64 * c + 64],
                                 SH[R, 2 * t + c, 64 * h:64 * h + 64], start=True, stop=True)
            pe.wait_ge(p_ready, n + 1)
            for c in range(2):
                S = slice(64 * c, 64 * c + 64)
                mm = nc.tensor.matmul(ps[S, 6 + c, 256 * h + 64 * tl:256 * h + 64 * tl + 64], PB[S, n % 2],
                                      V[S, 1 + t, P * hp + 64 * h:P * hp + 64 * h + 64], start=True, stop=True)
            mm.then_inc(o_done, 1)

        oS = oC
        PR_ = [take(2, L) for _ in range(2)]
        AT = [take(9, P) for _ in range(2)]
        OA = take(NT, 512)
        WO = take(KD, 1024)
        OSQA = take(512)
        assert oS <= MEM
        PRD, LAME, NLAM, GS8 = sml[:, 380:382], sml[:, 382:384], sml[:, 384:385], sml[:, 104:232]
        NMX, SUM, R0, R1, RW = (sml[:, 390 + 4 * i:394 + 4 * i] for i in range(5))
        ASS, HALF, ARS = sml[:, 412:416], sml[:, 416:420], sml[:, 420:424]
        prd_ready, lam_sum, lame_ready, nlam_ready, half_ready = (
            sem(n) for n in ("prd_ready", "lam_sum", "lame_ready", "nlam_ready", "half_ready"))
        qk_done, max_ready, exp_done, a_ready, ring_ready, ring_free = (
            sem(n) for n in ("qk_done", "max_ready", "exp_done", "a_ready", "ring_ready", "ring_free"))
        asq_ready, ams_ready, oa_ready = sem("asq_ready"), sem("ams_ready"), sem("oa_ready")
        NJOB = 4 * NT

        def groups(i):
            x = list(range(i + 1))
            g = [x[b:b + 4] for b in range(0, i + 1, 4)]
            if len(g[-1]) < 4:
                g[-1].append("meta")
            else:
                g.append(["meta"])
            return g

        def step_of(kind, n):
            return n + 1 if kind == "t" else n + 2 if kind == "o" else min(4 * n + 7, NJOB + 5)

        ring = []
        for step in range(NJOB + 6):
            ring += [("t", n, g) for n in range(NJOB) if step_of("t", n) == step for g in groups(n // 4)]
            ring += [("o", n, None) for n in range(NJOB) if step_of("o", n) == step]
            ring += [("m", n, None) for n in range(NT) if step_of("m", n) == step]
        at_ready = {}
        for r, (kind, n, g) in enumerate(ring):
            if kind == "t":
                at_ready[n] = r + 1
        out_at = {n: r + 1 for r, (kind, n, g) in enumerate(ring) if kind == "o"}
        mix_at = {n: r + 1 for r, (kind, n, g) in enumerate(ring) if kind == "m"}

        def sp_attention(sp):
            sp.wait_ge(oh_ready, 1)
            sp.wait_ge(hgrn_done, 4)
            sp.dma_start(WO, a["w_out"].rearrange("(k p) n -> p k n", p=P)).then_inc(late_loaded, 16)

        def pool_attention(pool, link):
            nc.gpsimd.memset(HALF, -0.5).then_inc(half_ready, 1)
            pool.wait_ge(half_ready, 1)
            pool.wait_ge(gains_loaded, 48)
            link(nc.gpsimd.tensor_scalar(GS8, GS8, 1.0 - LAM_INIT, None, ALU.mult))
            for i in range(NT):
                pool.wait_ge(ams_ready, i + 1)
                link(nc.gpsimd.tensor_tensor(ARS, ASS, HALF, ALU.pow))
                o = OA[:, i].rearrange("p (h v) -> p h v", h=4)
                link(nc.gpsimd.tensor_tensor(o, o, ARS.unsqueeze(2).to_broadcast([P, 4, P]), ALU.mult))
                nc.gpsimd.tensor_tensor(o, o, GS8.unsqueeze(1).to_broadcast([P, 4, P]), ALU.mult).then_inc(oa_ready, 1)

        def dve_lambda(dve, link):
            tt = nc.vector.tensor_tensor
            v = par[0:64, P_LAM:P_LAM + 4].rearrange("p (a b) -> p a b", b=2)
            tt(PRD[0:64], v[:, :, 0], v[:, :, 1], ALU.mult).then_inc(prd_ready, 1)
            dve.wait_ge(lame_ready, 1)
            link(tt(NLAM, LAME[:, 1:2], LAME[:, 0:1], ALU.subtract))
            nc.vector.tensor_scalar(NLAM, NLAM, -LAM_INIT, None, ALU.add).then_inc(nlam_ready, 1)

        def logits(c):
            return ps[:, 3 * c:3 * c + 3, :].rearrange("p b n -> p (b n)")

        def dve_attention(dve, link):
            dve_lambda(dve, link)
            dve.wait_ge(nlam_ready, 1)
            for n in range(NJOB + 1):
                if n < NJOB:
                    dve_maximum(dve, n, 0)
                if n >= 1:
                    dve_combine(dve, link, n - 1)
                if n < NJOB:
                    dve_maximum(dve, n, 1)
            dve_means(dve, link, NT - 1)

        def dve_maximum(dve, n, c):
            dve.wait_ge(qk_done, 2 * n + c + 1)
            if n >= 2:
                dve.wait_ge(exp_done, 2 * (n - 2) + c + 1)
            nc.vector.tensor_reduce(NMX[:, 2 * (n % 2) + c:2 * (n % 2) + c + 1], logits(c)[:, 0:META + P * (n // 4 + 1)], AX.X, ALU.max,
                                    negate=True).then_inc(max_ready, 1)

        def dve_combine(dve, link, j):
            stt = nc.vector.scalar_tensor_tensor
            o = 2 * (j % 2)
            nk = META + P * (j // 4 + 1)
            dve.wait_ge(exp_done, 2 * j + 2)
            if j >= 2:
                dve.wait_ge(ring_free, out_at[j - 2])
            link(nc.vector.reciprocal(R1[:, o:o + 2], SUM[:, o:o + 2]))
            link(stt(RW[:, j % 2:j % 2 + 1], SUM[:, o:o + 1], NLAM, R1[:, o + 1:o + 2], ALU.mult, ALU.mult))
            A = PR_[j % 2]
            stt(A[:, 0, 0:nk], A[:, 1, 0:nk], RW[:, j % 2:j % 2 + 1], A[:, 0, 0:nk], ALU.mult, ALU.add).then_inc(a_ready, 1)
            if j % 4 == 1 and j >= 5:
                dve_means(dve, link, j // 4 - 1)

        def dve_means(dve, link, i):
            dve.wait_ge(asq_ready, i + 1)
            if i:
                dve.wait_ge(oa_ready, i)
            link(nc.vector.tensor_reduce(ASS, OSQA.rearrange("p (h v) -> p h v", h=4), AX.X, ALU.add))
            nc.vector.tensor_scalar(ASS, ASS, 1.0 / P, EPS, ALU.mult, ALU.add).then_inc(ams_ready, 1)

        def act_attention(act, link):
            f = nc.scalar.activation
            act.wait_ge(lam_sum, 1)
            f(LAME, ps[:, 7, 0:2], ACT.Exp).then_inc(lame_ready, 1)
            r = 0
            for n in range(NJOB + 6):
                if n < NJOB:
                    nk = META + P * (n // 4 + 1)
                    for c in range(2):
                        while c == 1 and r < len(ring) and ring[r][0] == "t" and step_of(*ring[r][:2]) <= n:
                            act_ring(act, link, r)
                            r += 1
                        act.wait_ge(max_ready, 2 * n + c + 1)
                        if n >= 2:
                            act.wait_ge(a_ready, n - 1)
                            act.wait_ge(ring_ready, at_ready[n - 2])
                        o = 2 * (n % 2) + c
                        f(PR_[n % 2][:, c, 0:nk], logits(c)[:, 0:nk], ACT.Exp, bias=NMX[:, o:o + 1],
                          accum_out=SUM[:, o:o + 1]).then_inc(exp_done, 1)
                while r < len(ring) and step_of(*ring[r][:2]) <= n:
                    act_ring(act, link, r)
                    r += 1

        def act_ring(act, link, r):
            kind, n, g = ring[r]
            f = nc.scalar.activation
            act.wait_ge(ring_ready, r + 1)
            b = ps[:, 6 + r % 2, :]
            if kind == "t":
                x = [v for v in g if v != "meta"]
                ins = None
                if x:
                    ins = nc.scalar.copy(AT[n % 2][:, x[0]:x[-1] + 1], b[:, 0:P * len(x)].rearrange("p (k q) -> p k q", q=P))
                if "meta" in g:
                    ins = nc.scalar.copy(AT[n % 2][0:META, 8], b[0:META, P * len(x):P * len(x) + P])
                ins.then_inc(ring_free, 1)
            elif kind == "o":
                i, h = n // 4, n % 4
                f(OA[:, i, P * h:P * h + P], b[:, 0:P], ACT.Identity, scale=R1[:, 2 * (n % 2):2 * (n % 2) + 1]).then_inc(ring_free, 1)
                if h == 3:
                    act.wait_ge(ring_free, r + 1)
                    if i:
                        act.wait_ge(ams_ready, i)
                    f(OSQA, OA[:, i], ACT.Square).then_inc(asq_ready, 1)
            else:
                nc.scalar.copy(AQ[:, :, P * n:P * n + P], b.rearrange("p (h q) -> p h q", h=4)).then_inc(ring_free, 1)

        def pe_attention(pe):
            pe.wait_ge(hgrn_done, 4)
            pe.wait_ge(prd_ready, 1)
            nc.tensor.matmul(ps[:, 7, 0:2], con[0:64, C_ONES:C_ONES + P], PRD[0:64], start=True, stop=True).then_inc(lam_sum, 1)
            pe.wait_ge(lame_ready, 1)
            r = 0
            for n in range(NJOB + 6):
                if n < NJOB:
                    pe_logits(pe, n)
                while r < len(ring) and step_of(*ring[r][:2]) <= n:
                    pe_ring(pe, r)
                    r += 1

        def pe_logits(pe, n):
            i, h = n // 4, n % 4
            nk = META + P * (i + 1)
            if n == 0:
                pe.wait_ge(roped, len(TURNS))
                pe.wait_ge(gains_loaded, 48)
            for c in range(2):
                R = slice(64 * c, 64 * c + 64)
                if n >= 1:
                    pe.wait_ge(exp_done, 2 * (n - 1) + c + 1)
                for k in range(0, nk, 512):
                    w = min(512, nk - k)
                    m = max(nk - P, k)
                    masked = m < k + w
                    mm = nc.tensor.matmul(logits(c)[:, k:k + w], AQ[R, h, P * i:P * i + P], AK[R, h, k:k + w], start=True, stop=not masked)
                    if masked:
                        mm = nc.tensor.matmul(logits(c)[:, m:k + w], ident, con[:, C_MASK + m - (nk - P):C_MASK + k + w - (nk - P)],
                                              start=False, stop=True)
                mm.then_inc(qk_done, 1)

        def pe_ring(pe, r):
            kind, n, g = ring[r]
            if r >= 2:
                pe.wait_ge(ring_free, r - 1)
            b = ps[:, 6 + r % 2, :]
            if kind == "t":
                pe.wait_ge(a_ready, n + 1)
                A = PR_[n % 2][:, 0]
                for j, v in enumerate(g):
                    if v == "meta":
                        mm = nc.tensor.transpose(b[0:META, P * j:P * j + P], A[:, 0:META], ident)
                    else:
                        mm = nc.tensor.transpose(b[:, P * j:P * j + P], A[:, META + P * v:META + P * v + P], ident)
            elif kind == "o":
                i, h = n // 4, n % 4
                pe.wait_ge(ring_free, at_ready[n])
                vc = slice(512 + P * h, 512 + P * h + P)
                for k in range(i + 1):
                    nc.tensor.matmul(b[:, 0:P], AT[n % 2][:, k], V[:, 1 + k, vc], start=(k == 0), stop=False)
                mm = nc.tensor.matmul(b[:, 0:P], AT[n % 2][0:META, 8], V[0:META, 0, vc], start=False, stop=True)
            else:
                pe.wait_ge(oa_ready, n + 1)
                for h in range(4):
                    mm = nc.tensor.transpose(b[:, P * h:P * h + P], OA[:, n, P * h:P * h + P], ident)
            mm.then_inc(ring_ready, 1)

        H1 = view(oV, NT, D)
        XB, XN2 = view(oAK, 2, D), view(oAK + 2 * D, 2, D)
        XT2 = view(oAK + 4 * D, 2, KD, P)
        GF, WRT = view(oC + 22880, D), view(oC + 22880 + D, KD, 20)
        SS2, VA2, SD2, RS2 = (sml[:, 8 * i:8 * i + 8] for i in range(4))
        BR = sml[:, 430:450]
        xn_d = nc.dram_tensor("xn_d", (X, D), F32, kind="Internal").ap()
        ffn_loaded, xb_loaded = sem("ffn_loaded"), [sem("xb_loaded0"), sem("xb_loaded1")]
        out_done, h1_ready, ss2_ready, va2_ready, sd2_ready, xn2_ready = (
            sem(n) for n in ("out_done", "h1_ready", "ss2_ready", "va2_ready", "sd2_ready", "xn2_ready"))
        xn2_stored, xt2_ready, xt2_copied, log_done = (
            [sem("xn2_stored0"), sem("xn2_stored1")], sem("xt2_ready"), sem("xt2_copied"), sem("log_done"))

        def sp_out(sp):
            sp.wait_ge(ring_free, len(ring))
            sp.dma_start(GF, a["norm_ffn_g"].to_broadcast([P, D])).then_inc(ffn_loaded, 16)
            sp.dma_start(WRT, a["w_router"].rearrange("(k p) n -> p k n", p=P)).then_inc(ffn_loaded, 16)
            sp.dma_start(BR, a["b_router"].to_broadcast([P, 20])).then_inc(ffn_loaded, 16)
            for t in range(NT + 1):
                if t < NT:
                    if t >= 2:
                        sp.wait_ge(h1_ready, t - 1)
                    sp.dma_start(XB[:, t % 2], a["x"][P * t:P * t + P, :]).then_inc(xb_loaded[t % 2], 16)
                if t >= 1:
                    sp.wait_ge(xn2_ready, t)
                    sp.dma_start(xn_d[P * (t - 1):P * t, :], XN2[:, (t - 1) % 2]).then_inc(xn2_stored[(t - 1) % 2], 16)

        def act_out(act, link):
            for t in range(NT + 1):
                if t < NT:
                    act.wait_ge(h1_ready, t + 1)
                    nc.scalar.activation(OA.rearrange("p t n -> p (t n)")[:, 0:D], H1[:, t], ACT.Square,
                                         accum_out=SS2[:, t:t + 1]).then_inc(ss2_ready, 1)
                    act.wait_ge(va2_ready, t + 1)
                    nc.scalar.activation(SD2[:, t:t + 1], VA2[:, t:t + 1], ACT.Sqrt).then_inc(sd2_ready, 1)
                if t >= 1:
                    for j in range(2):
                        act.wait_ge(xt2_ready, 2 * (t - 1) + j + 1)
                        nc.scalar.copy(XT2[:, (t - 1) % 2, 4 * j:4 * j + 4],
                                       ps[:, 4 + j, :].rearrange("p (k q) -> p k q", k=4)).then_inc(xt2_copied, 1)

        def dve_out(dve, link):
            for t in range(NT):
                dve.wait_ge(out_done, t + 1)
                dve.wait_ge(xb_loaded[t % 2], 16 * (t // 2 + 1))
                if t == 0:
                    dve.wait_ge(ring_free, len(ring))
                nc.vector.tensor_tensor(H1[:, t], ps[:, 2 * (t % 2):2 * (t % 2) + 2, :].rearrange("p b n -> p (b n)"),
                                        XB[:, t % 2], ALU.add).then_inc(h1_ready, 1)
                dve.wait_ge(ss2_ready, t + 1)
                nc.vector.tensor_scalar(VA2[:, t:t + 1], SS2[:, t:t + 1], 1.0 / D, EPS, ALU.mult, ALU.add).then_inc(va2_ready, 1)
                dve.wait_ge(sd2_ready, t + 1)
                link(nc.vector.reciprocal(RS2[:, t:t + 1], SD2[:, t:t + 1]))
                if t >= 2:
                    dve.wait_ge(xn2_stored[t % 2], 16 * (t // 2))
                    dve.wait_ge(xt2_ready, 2 * (t - 1))
                if t == 0:
                    dve.wait_ge(ffn_loaded, 48)
                nc.vector.scalar_tensor_tensor(XN2[:, t % 2], H1[:, t], RS2[:, t:t + 1], GF, ALU.mult, ALU.mult).then_inc(xn2_ready, 1)

        def pe_out(pe):
            pe.wait_ge(ring_free, len(ring))
            pe.wait_ge(late_loaded, 32)
            for t in range(NT + 2):
                if t < NT:
                    if t >= 2:
                        pe.wait_ge(h1_ready, t - 1)
                    for h in range(2):
                        for k in range(KD):
                            mm = nc.tensor.matmul(ps[:, 2 * (t % 2) + h, :], mix(k)[:, P * t:P * t + P], WO[:, k, 512 * h:512 * h + 512],
                                                  start=(k == 0), stop=(k == KD - 1))
                    mm.then_inc(out_done, 1)
                if 1 <= t <= NT:
                    s = t - 1
                    pe.wait_ge(xn2_ready, s + 1)
                    for j in range(2):
                        if s:
                            pe.wait_ge(xt2_copied, 2 * s - 1 + j)
                        for k in range(4):
                            mm = nc.tensor.transpose(ps[:, 4 + j, P * k:P * k + P], XN2[:, s % 2, P * (4 * j + k):P * (4 * j + k) + P], ident)
                        mm.then_inc(xt2_ready, 1)
                if t >= 2:
                    s = t - 2
                    pe.wait_ge(xt2_copied, 2 * s + 2)
                    if s == 0:
                        pe.wait_ge(ffn_loaded, 48)
                    for k in range(KD):
                        mm = nc.tensor.matmul(ps[:, 6, 20 * s:20 * s + 20], XT2[:, s % 2, k], WRT[:, k], start=(k == 0), stop=(k == KD - 1))
                    mm.then_inc(log_done, 1)

        oS = oU
        LG = take(NT, 20)
        GM, GX, GS_, GP = take(NT), take(NT, 4), take(NT), take(NT)
        OHG, VAL, MX = take(NT, 4), take(NT, 4), take(NT)
        IG, M1, O1, M2, O2, E2 = take(NT, 4), take(NT), take(NT, 4), take(NT), take(NT, 4), take(NT)
        EXO = take(NT, 4, 4)
        OK1, OK2, OKS = take(NT, NE), take(NT, NE), take(NT, NE)
        RK, TOT, PRE = take(NT, NE), take(NT, NE), take(NT, NE)
        CNT, BLK, CB, BASE, BCMP, ECMP = take(NE), take(NE), take(NE), take(NE), take(NE, 8), take(NB, NE)
        SLF, EBF = take(2, NT), take(NB)
        NEW, OLD, RUN, PRV, BUF, NHALF, NPR = take(NB), take(NB), take(NB), take(NB), take(NB), take(1), take(1)
        PCMP = take(NB // 2)
        BLKF, REM, HOTR, HOTB = take(2, NT), take(2, NT), take(2 * NT, P), take(2 * NT, NB)
        IOTAP = ps[:, 2, 0:P]
        assert oS <= oC
        W12 = sml[:, 460:476].rearrange("p (k t) -> p k t", k=2)
        slots = sml[:, 480:496].bitcast(I32).rearrange("p (k t) -> p k t", k=2)
        ixb, ixc = sml[:, 538:538 + NB].bitcast(I32), sml[:, 602:604].bitcast(I32)
        eblk, ebuf, enew = (sml[:, o:o + NB].bitcast(I32) for o in (506, 570, 398))
        efree, npair = sml[:, 366:366 + NB].bitcast(I32), sml[:, 504:505].bitcast(I32)
        rt_gap, rt_exp, onehot_ready, rank_done, slots_ready, tables_ready, slot_hot_ready, idx_done = (
            sem(n) for n in ("rt_gap", "rt_exp", "onehot_ready", "rank_done", "slots_ready", "tables_ready", "slot_hot_ready", "idx_done"))

        def act_route(act, link):
            act.wait_ge(rt_gap, 1)
            nc.scalar.activation(GX, GX, ACT.Exp).then_inc(rt_exp, 1)
            act.wait_ge(rt_gap, 2)
            nc.scalar.activation(E2, E2, ACT.Exp).then_inc(rt_exp, 1)

        def pe_route(pe):
            pe.wait_ge(onehot_ready, 1)
            nc.tensor.matmul(IOTAP, con[:, C_ONES:C_ONES + P], con[:, C_TRI:C_TRI + P], start=True, stop=True)
            f = OKS.rearrange("p t e -> p (t e)")
            nc.tensor.matmul(ps[:, 0, 0:P], con[:, C_TRI:C_TRI + P], f, start=True, stop=True)
            nc.tensor.matmul(ps[:, 0, P:2 * P], con[:, C_ONES:C_ONES + P], f, start=True, stop=True).then_inc(rank_done, 1)

            pe.wait_ge(slot_hot_ready, 1)
            for n in range(2 * NT):
                mm = nc.tensor.matmul(ps[:, 1, 0:NB], HOTR[:, n], HOTB[:, n], start=(n == 0), stop=(n == 2 * NT - 1))
            mm.then_inc(idx_done, 1)

        def dve_route(dve, link):
            tt, ts, stt, red = (nc.vector.tensor_tensor, nc.vector.tensor_scalar, nc.vector.scalar_tensor_tensor,
                                nc.vector.tensor_reduce)
            s4 = [P, NT, 4]

            def b4(v):
                return v.unsqueeze(2).to_broadcast(s4)

            def first_of_max(oh, x, m):
                link(red(m, x, AX.X, ALU.max))
                link(tt(oh, x, b4(m), ALU.is_equal))
                link(tt(VAL, oh, con[:, C_DESC4:C_DESC4 + 4].unsqueeze(1).to_broadcast(s4), ALU.mult))
                link(red(MX, VAL, AX.X, ALU.max))
                link(tt(oh, VAL, b4(MX), ALU.is_equal))

            dve.wait_ge(log_done, NT)
            link(tt(LG, ps[:, 6, 0:20 * NT].rearrange("p (t n) -> p t n", t=NT), BR.unsqueeze(1).to_broadcast([P, NT, 20]), ALU.add))
            gl = LG[:, :, 0:4]
            first_of_max(OHG, gl, GM)
            tt(GX, gl, b4(GM), ALU.subtract).then_inc(rt_gap, 1)
            link(tt(EXO, LG[:, :, 4:20].rearrange("p t (g e) -> p t g e", g=4), OHG.unsqueeze(3).to_broadcast([P, NT, 4, 4]), ALU.mult))
            link(red(IG, EXO.rearrange("p t g e -> p t e g"), AX.X, ALU.add))
            first_of_max(O1, IG, M1)
            link(stt(IG, O1, -3.0e38, IG, ALU.mult, ALU.add))
            first_of_max(O2, IG, M2)
            tt(E2, M2, M1, ALU.subtract).then_inc(rt_gap, 1)
            for o, oh in ((OK1, O1), (OK2, O2)):
                link(tt(o.rearrange("p t (g e) -> p t g e", g=4), OHG.unsqueeze(3).to_broadcast([P, NT, 4, 4]),
                        oh.unsqueeze(2).to_broadcast([P, NT, 4, 4]), ALU.mult))
            tt(OKS, OK1, OK2, ALU.add).then_inc(onehot_ready, 1)
            dve.wait_ge(rt_exp, 2)
            link(red(GS_, GX, AX.X, ALU.add))
            link(nc.vector.reciprocal(GP, GS_))
            link(ts(M1, E2, 1.0, None, ALU.add))
            link(nc.vector.reciprocal(M1, M1))
            link(tt(W12[:, 0], M1, GP, ALU.mult))
            link(tt(W12[:, 1], W12[:, 0], E2, ALU.mult))
            dve.wait_ge(rank_done, 1)
            link(nc.vector.tensor_copy(TOT, ps[:, 0, P:2 * P].rearrange("p (t e) -> p t e", t=NT)))
            link(nc.vector.memset(PRE[:, 0], 0.0))
            for t in range(1, NT):
                link(tt(PRE[:, t], PRE[:, t - 1], TOT[:, t - 1], ALU.add))
            link(tt(CNT, PRE[:, NT - 1], TOT[:, NT - 1], ALU.add))
            link(tt(RK, ps[:, 0, 0:P].rearrange("p (t e) -> p t e", t=NT), PRE, ALU.add))
            link(tt(BCMP, CNT.unsqueeze(2).to_broadcast([P, NE, 8]), con[:, C_128J:C_128J + 8].unsqueeze(1).to_broadcast([P, NE, 8]), ALU.is_gt))
            link(red(BLK, BCMP, AX.X, ALU.add))
            link(nc.vector.tensor_tensor_scan(CB, con[:, C_ONES:C_ONES + NE], BLK, 0.0, ALU.mult, ALU.add))
            link(tt(BASE, CB, BLK, ALU.subtract))
            link(ts(BASE, BASE, float(P), None, ALU.mult))
            link(tt(ECMP, CB.unsqueeze(1).to_broadcast([P, NB, NE]), con[:, C_IOTAB:C_IOTAB + NB].unsqueeze(2).to_broadcast([P, NB, NE]), ALU.is_le))
            link(red(EBF, ECMP, AX.X, ALU.add))
            link(ts(EBF, EBF, float(NE - 1), None, ALU.min))
            link(nc.vector.tensor_copy(eblk[:, :], EBF))
            scan = nc.vector.tensor_tensor_scan
            link(nc.vector.memset(NEW[:, 0:1], 1.0))
            link(tt(NEW[:, 1:NB], EBF[:, 1:NB], EBF[:, 0:NB - 1], ALU.not_equal))
            link(ts(OLD, NEW, -1.0, 1.0, ALU.mult, ALU.add))
            link(tt(PRV, NEW, con[:, C_IOTAB:C_IOTAB + NB], ALU.mult))
            link(scan(RUN, OLD, PRV, 0.0, ALU.mult, ALU.add))
            link(nc.vector.memset(PRV[:, 0:1], 0.0))
            link(tt(PRV[:, 1:NB], NEW[:, 1:NB], RUN[:, 0:NB - 1], ALU.mult))
            link(scan(BUF, OLD, PRV, 0.0, ALU.mult, ALU.add))
            link(ts(BUF, BUF, 1.0, None, ALU.add))
            link(nc.vector.tensor_copy(efree, BUF))
            link(tt(OLD, OLD, NEW, ALU.subtract))
            link(scan(BUF, OLD, NEW, 1.0, ALU.mult, ALU.add))
            link(nc.vector.tensor_copy(ebuf, BUF))
            link(nc.vector.tensor_copy(enew, NEW))
            link(ts(NHALF, CB[:, NE - 1:NE], 0.5, None, ALU.mult))
            link(tt(PCMP, NHALF.to_broadcast([P, NB // 2]), con[:, C_IOTAB:C_IOTAB + NB // 2], ALU.is_gt))
            link(red(NPR, PCMP, AX.X, ALU.add))
            link(ts(NPR, NPR, float(-(LEAST // 2)), None, ALU.add))
            nc.vector.tensor_copy(npair, NPR).then_inc(tables_ready, 1)
            link(tt(RK, RK, BASE.unsqueeze(1).to_broadcast([P, NT, NE]), ALU.add))
            for k, o in enumerate((OK1, OK2)):
                link(tt(o, o, RK, ALU.mult))
                link(red(SLF[:, k], o, AX.X, ALU.add))
            MAGIC = 12582912.0
            link(ts(BLKF, SLF, 1.0 / P, 0.5 / P - 0.5, ALU.mult, ALU.add))
            link(ts(BLKF, BLKF, MAGIC, None, ALU.add))
            link(ts(BLKF, BLKF, -MAGIC, None, ALU.add))
            link(stt(REM, BLKF, -float(P), SLF, ALU.mult, ALU.add))
            n2 = 2 * NT
            fl = [v.rearrange("p k t -> p (k t)").unsqueeze(2) for v in (REM, BLKF)]
            link(tt(HOTR, fl[0].to_broadcast([P, n2, P]), IOTAP.unsqueeze(1).to_broadcast([P, n2, P]), ALU.is_equal))
            link(tt(HOTB, fl[1].to_broadcast([P, n2, NB]), con[:, C_IOTAB:C_IOTAB + NB].unsqueeze(1).to_broadcast([P, n2, NB]), ALU.is_equal))
            for k in range(2):
                ins = tt(HOTB[:, NT * k:NT * k + NT], HOTB[:, NT * k:NT * k + NT], con[:, C_TOK:C_TOK + NT].unsqueeze(2).to_broadcast([P, NT, NB]), ALU.mult)
            ins.then_inc(slot_hot_ready, 1)
            nc.vector.tensor_copy(slots[:, :, :], SLF)
            dve.wait_ge(idx_done, 1)
            nc.vector.tensor_copy(ixb, ps[:, 1, 0:NB]).then_inc(slots_ready, 1)

        WGU = view(oC, 2 * 2 * KD, FF)
        WDN = view(oC + 2 * 2 * KD * FF, 2 * FF // P, D)
        oS = oAK
        XG, XGT, YE = take(2, D), take(2, KD, P), take(2, D)
        SG, HE, HET = take(2, FF), take(2, FF), take(2, FF // P, P)
        Y12 = [take(2, D) for _ in range(2)]
        assert oS <= oC
        GFN = view(oC, D)
        OUTB = view(oC + D, 2, D)
        w_loads, wdn_loaded = [sem("gate_loaded"), sem("up_w_loaded")], sem("wdn_loaded")
        ix_ready, xg_loaded = sem("ix_ready"), [sem(f"xg_loaded{i}") for i in range(2)]
        xgt_ready, xgt_copied, gu_done, sg_ready, he_ready, het_ready, het_copied, ye_done, ye_copied = (
            sem(n) for n in ("xgt_ready", "xgt_copied", "gu_done", "sg_ready", "he_ready", "het_ready", "het_copied", "ye_done", "ye_copied"))
        ix_seen = sem("ix_seen")
        ye_stored = [sem(f"ye_stored{i}") for i in range(2)]

        def blocks(eng, body):
            pairs = eng.value_load(npair[0:1, 0:1], min_val=0, max_val=(NB - LEAST) // 2) + LEAST // 2
            for par in range(2):
                body(0, par, True, False)
            with eng.Fori(1, pairs - 1) as j:
                for par in range(2):
                    body(j, par, False, False)
            for par in range(2):
                body(pairs - 1, par, False, True)
            return pairs

        def has(par, last, ahead):
            return not last or par + ahead < 2

        def sp_experts(sp):
            sp.wait_ge(out_done, NT)
            sp.wait_ge(log_done, NT)
            sp.wait_ge(tables_ready, 1)

            def body(j, par, first, last):
                b = 2 * j + par
                e, q, new, free = (sp.value_load(tab[0:1, bass.ds(b, 1)], min_val=0, max_val=hi)
                                   for tab, hi in ((eblk, NE - 1), (ebuf, 1), (enew, 1), (efree, NB)))
                if par or not first:
                    for i in range(2):
                        sp.wait_ge(w_loads[i], 16 * b)
                sp.wait_ge(gu_done, free)
                for i, w in enumerate(("w_gate", "w_up")):
                    sp.dma_start(WGU[:, bass.ds(q * (2 * KD) + i * KD, KD)], a[w][bass.ds(e, 1)].rearrange("a (k p) n -> p (a k) n", p=P),
                                 cond=new).then_inc(w_loads[i], 16)
                if par or not first:
                    sp.wait_ge(wdn_loaded, 16 * b)
                sp.wait_ge(ye_done, free)
                sp.dma_start(WDN[:, bass.ds(q * (FF // P), FF // P)], a["w_down"][bass.ds(e, 1)].rearrange("a (k p) n -> p (a k) n", p=P),
                             cond=new).then_inc(wdn_loaded, 16)

            return blocks(sp, body)

        def pool_experts(pool):
            pool.wait_ge(slots_ready, 1)
            for t in range(2):
                pool.wait_ge(xn2_stored[t], 16 * NT // 2)

            def body(j, par, first, last):
                b = 2 * j + par
                if not first:
                    pool.wait_ge(xgt_ready, 2 * b - 2)
                pool.sem_inc(ix_seen, 1)
                nc.gpsimd.tensor_copy(ixc[:, par:par + 1], ixb[:, bass.ds(b, 1)]).then_inc(ix_ready, 1)
                pool.wait_ge(ix_ready, b + 1)
                pool.sem_inc(ix_seen, 1)
                pool.indirect_dma_start(XG[:, par], None, xn_d, bass.IndirectOffsetOnAxis(ap=ixc[:, par:par + 1], axis=0)).then_inc(xg_loaded[par], 16)

            return blocks(pool, body)

        def pe_experts(pe):
            def turn_x(j, par):
                pe.wait_ge(xg_loaded[par], 16 * (j + 1))
                for h in range(2):
                    for k in range(4):
                        mm = nc.tensor.transpose(ps[:, 6 + h, P * k:P * k + P], XG[:, par, P * (4 * h + k):P * (4 * h + k) + P], ident)
                    mm.then_inc(xgt_ready, 1)

            def buffer_of(b):
                return pe.value_load(ebuf[0:1, bass.ds(b, 1)], min_val=0, max_val=1)

            def gate_up(b, par, q):
                pe.wait_ge(xgt_copied, 2 * b + 2)
                for i in range(2):
                    pe.wait_ge(w_loads[i], 16 * b + 16)
                    for k in range(KD):
                        mm = nc.tensor.matmul(ps[:, 2 * par + i, :], XGT[:, par, k], WGU[:, bass.ds(q * (2 * KD) + (i * KD + k), 1)], start=(k == 0), stop=(k == KD - 1))
                mm.then_inc(gu_done, 1)

            pe.wait_ge(slots_ready, 1)
            for s in (gu_done, ye_done):
                pe.sem_inc(s, 1)
            turn_x(0, 0)
            gate_up(0, 0, buffer_of(0))
            pe.wait_ge(xgt_copied, 2)
            turn_x(0, 1)

            def body(j, par, first, last):
                b = 2 * j + par
                q = buffer_of(b)
                q_next = buffer_of(b + 1) if has(par, last, 1) else None
                pe.wait_ge(he_ready, b + 1)
                pe.wait_ge(xgt_copied, 2 * b + (4 if has(par, last, 1) else 2))
                for k in range(FF // P):
                    mm = nc.tensor.transpose(ps[:, 6, P * k:P * k + P], HE[:, par, P * k:P * k + P], ident)
                mm.then_inc(het_ready, 1)
                if has(par, last, 1):
                    gate_up(b + 1, 1 - par, q_next)
                pe.wait_ge(het_copied, b + 1)
                if has(par, last, 2):
                    turn_x(j + 1, par)
                if par or not first:
                    pe.wait_ge(ye_copied, 2 * b)
                pe.wait_ge(wdn_loaded, 16 * b + 16)
                for h in range(2):
                    for k in range(FF // P):
                        mm = nc.tensor.matmul(ps[:, 4 + h, :], HET[:, par, k], WDN[:, bass.ds(q * (FF // P) + k, 1), 512 * h:512 * h + 512], start=(k == 0), stop=(k == 3))
                mm.then_inc(ye_done, 1)

            blocks(pe, body)

        def act_experts(act):
            act.wait_ge(slots_ready, 1)

            def copy_x(b, par):
                for j in range(2):
                    act.wait_ge(xgt_ready, 2 * b + 1 + j)
                    nc.scalar.copy(XGT[:, par, 4 * j:4 * j + 4], ps[:, 6 + j, :].rearrange("p (k q) -> p k q", k=4)).then_inc(xgt_copied, 1)

            def silu(b, par):
                act.wait_ge(gu_done, b + 2)
                nc.scalar.activation(SG[:, par], ps[:, 2 * par, :], ACT.Silu).then_inc(sg_ready, 1)

            copy_x(0, 0)
            silu(0, 0)
            copy_x(1, 1)

            def body(j, par, first, last):
                b = 2 * j + par
                act.wait_ge(het_ready, b + 1)
                nc.scalar.copy(HET[:, par], ps[:, 6, :].rearrange("p (k q) -> p k q", k=4)).then_inc(het_copied, 1)
                if has(par, last, 1):
                    silu(b + 1, 1 - par)
                if has(par, last, 2):
                    copy_x(b + 2, par)
                act.wait_ge(ye_copied, 2 * b + 2)
                act.dma_start(ye_d[bass.ds(b * P, P), :], YE[:, par]).then_inc(ye_stored[par], 16)

            blocks(act, body)

        def dve_experts(dve):
            def hidden(b, par):
                dve.wait_ge(sg_ready, b + 1)
                nc.vector.tensor_tensor(HE[:, par], SG[:, par], ps[:, 2 * par + 1, :], ALU.mult).then_inc(he_ready, 1)

            hidden(0, 0)

            def body(j, par, first, last):
                b = 2 * j + par
                if has(par, last, 1):
                    hidden(b + 1, 1 - par)
                dve.wait_ge(ye_done, b + 2)
                if not first:
                    dve.wait_ge(ye_stored[par], 16 * j)
                for h in range(2):
                    nc.vector.tensor_copy(YE[:, par, 512 * h:512 * h + 512], ps[:, 4 + h, :]).then_inc(ye_copied, 1)

            blocks(dve, body)

        y_gathered = [sem(f"y_gathered{i}") for i in range(2)]
        y_added, ob_ready = sem("y_added"), sem("ob_ready")
        out_stored = [sem("out_stored0"), sem("out_stored1")]

        def sp_final(sp, pairs):
            sp.wait_ge(ye_copied, 4 * pairs)
            sp.dma_start(GFN, a["final_norm_g"].to_broadcast([P, D])).then_inc(late_loaded, 16)
            for t in range(NT):
                sp.wait_ge(ob_ready, t + 1)
                sp.dma_start(out[P * t:P * t + P, :], OUTB[:, t % 2]).then_inc(out_stored[t % 2], 16)
            for i in range(2):
                sp.wait_ge(out_stored[i], 16 * NT // 2)

        def pool_final(pool, pairs):
            for i in range(2):
                pool.wait_ge(ye_stored[i], 16 * pairs)
            pool.sem_inc(ix_seen, 1)
            for t in range(NT):
                if t >= 2:
                    pool.wait_ge(y_added, 2 * (t - 1))
                for k in range(2):
                    pool.indirect_dma_start(Y12[t % 2][:, k], None, ye_d,
                                            bass.IndirectOffsetOnAxis(ap=slots[:, k, t:t + 1], axis=0)).then_inc(y_gathered[t % 2], 16)

        def act_final(act):
            for t in range(NT):
                act.wait_ge(y_added, 2 * t + 2)
                nc.scalar.activation(SG.rearrange("p a b -> p (a b)"), H1[:, t], ACT.Square, accum_out=SS2[:, t:t + 1]).then_inc(ss2_ready, 1)
                act.wait_ge(va2_ready, NT + t + 1)
                nc.scalar.activation(SD2[:, t:t + 1], VA2[:, t:t + 1], ACT.Sqrt).then_inc(sd2_ready, 1)

        def dve_final(dve, link):
            dve.wait_ge(late_loaded, 48)
            for t in range(NT + 1):
                if t < NT:
                    dve.wait_ge(y_gathered[t % 2], 32 * (t // 2 + 1))
                    for k in range(2):
                        nc.vector.scalar_tensor_tensor(H1[:, t], Y12[t % 2][:, k], W12[:, k, t:t + 1], H1[:, t], ALU.mult, ALU.add).then_inc(y_added, 1)
                        dve.wait_ge(y_added, 2 * t + k + 1)
                if t >= 1:
                    s = t - 1
                    dve.wait_ge(ss2_ready, NT + s + 1)
                    nc.vector.tensor_scalar(VA2[:, s:s + 1], SS2[:, s:s + 1], 1.0 / D, EPS, ALU.mult, ALU.add).then_inc(va2_ready, 1)
                    dve.wait_ge(sd2_ready, NT + s + 1)
                    link(nc.vector.reciprocal(RS2[:, s:s + 1], SD2[:, s:s + 1]))
                    if s >= 2:
                        dve.wait_ge(out_stored[s % 2], 16 * (s // 2))
                    nc.vector.scalar_tensor_tensor(OUTB[:, s % 2], H1[:, s], RS2[:, s:s + 1], GFN, ALU.mult, ALU.mult).then_inc(ob_ready, 1)

        def sp_rest(sp):
            sp_s5(sp)
            sp_hgrn(sp)
            sp_attention(sp)
            sp_out(sp)
            sp_final(sp, sp_experts(sp))

        def act_rest(act, link):
            act_s5(act, link)
            act_hgrn(act, link)
            act_attention(act, link)
            act_out(act, link)
            act_route(act, link)
            act_experts(act)
            act_final(act)

        def dve_rest(dve, link):
            dve_s5(dve, link)
            dve_hgrn(dve, link)
            dve_attention(dve, link)
            dve_out(dve, link)
            dve_route(dve, link)
            dve_experts(dve)
            dve_final(dve, link)

        def pe_rest(pe):
            pe_s5(pe)
            pe_hgrn(pe)
            pe_attention(pe)
            pe_out(pe)
            pe_route(pe)
            pe_experts(pe)

        def pool_rest(pool, link):
            pool_hgrn(pool, link)
            pool_attention(pool, link)
            pool_final(pool, pool_experts(pool))


        with nc.Block() as block:
            @block.sync
            def _(sp):
                sp_project(sp)
                sp_rest(sp)

            @block.scalar
            def _(act):
                link = Chain(act, act_chain)
                act_project(act, link)
                if stage >= 2:
                    act_rest(act, link)

            @block.vector
            def _(dve):
                link = Chain(dve, dve_chain)
                dve_project(dve, link)
                if stage >= 2:
                    dve_rest(dve, link)

            @block.tensor
            def _(pe):
                pe_project(pe)
                if stage >= 2:
                    pe_rest(pe)

            @block.gpsimd
            def _(pool):
                link = Chain(pool, pool_chain)
                pool_project(pool, link)
                if stage >= 2:
                    pool_rest(pool, link)


def layout(inputs):
    g = {k: np.asarray(v) for k, v in inputs.items()}
    par = np.zeros((P, P_END), np.float32)
    par[:, P_GMIX:P_GMIX + 8] = g["norm_mix_g"].reshape(8, P).T
    for j, name in enumerate(("s5_lambda_re", "s5_lambda_im")):
        par[:, P_S5 + 16 * j:P_S5 + 16 * j + 16] = np.concatenate([g[name][0].T] * 2)
    par[:, P_S5 + 32:P_S5 + 48] = g["s5_log_dt"][0][None, :]
    par[:, P_D:P_D + 2] = g["s5_d"].reshape(2, P).T
    par[:, P_LB:P_LB + 2] = g["hgrn_lower_bounds"].reshape(2, P).T
    for j, name in enumerate(("diff_lambda_q1", "diff_lambda_k1", "diff_lambda_q2", "diff_lambda_k2")):
        par[0:64, P_LAM + j] = g[name][0]
    b = [g["s5_b_re"][0].transpose(1, 0, 2).reshape(64, 256), g["s5_b_im"][0].transpose(1, 0, 2).reshape(64, 256)]
    c = [g["s5_c_re"][0].transpose(2, 0, 1).reshape(64, 256), g["s5_c_im"][0].transpose(2, 0, 1).reshape(64, 256)]
    par[:, P_B1:P_B1 + 256], par[:, P_B2:P_B2 + 256] = np.concatenate(b), np.concatenate(b[::-1])
    par[:, P_C1:P_C1 + 256], par[:, P_C2:P_C2 + 256] = np.concatenate(c), np.concatenate(c[::-1])
    router = np.concatenate([g["moe_w_group"][0], g["moe_w_expert"][0]], axis=1)
    return {
        "consts": constants(), "params": par, "x": g["x"][0], "meta_tokens": g["meta_tokens"],
        "w_in": g["w_in"][0], "w_glu": g["s5_w_glu"][0], "w_out": g["w_out"][0],
        "hgrn_norm_g": g["hgrn_norm_g"], "subln_g": g["diff_subln_g"], "norm_ffn_g": g["norm_ffn_g"],
        "final_norm_g": g["final_norm_g"][None], "w_router": router,
        "b_router": np.concatenate([g["moe_b_group"], g["moe_b_expert"]], axis=1),
        "w_gate": g["moe_w_gate"][0], "w_up": g["moe_w_up"][0], "w_down": g["moe_w_down"][0],
    }


def kernel(_stage=99, **inputs):
    import concourse.bacc as bacc
    from concourse.bass_utils import run_bass_kernel_spmd

    nc = bacc.Bacc("TRN2", target_bir_lowering=False, num_devices=1)
    arrays = {f"in_{k}": np.ascontiguousarray(v) for k, v in layout(inputs).items()}
    a = {k[3:]: nc.dram_tensor(k, v.shape, mybir.dt.from_np(v.dtype), kind="ExternalInput").ap() for k, v in arrays.items()}
    out = nc.dram_tensor("out", (X, D), F32, kind="ExternalOutput").ap()
    build(nc, a, out, _stage)
    r = run_bass_kernel_spmd(nc, [arrays], core_ids=[0])
    return np.asarray(r.results[0]["out"]).reshape(1, X, D)
```

```python
from contextlib import ExitStack

import numpy as np

import concourse.bass as bass
from concourse import mybir

F32 = mybir.dt.float32
F32R = mybir.dt.float32r
I32 = mybir.dt.int32
ACT = mybir.ActivationFunctionType
ALU = mybir.AluOpType
AX = mybir.AxisListType

P = 128
D = 1024
KD = D // P
META = 16
X = 1024
L = META + X
NT = X // P
EPS = 1e-6

S5_G, S5_C, S5_N = 16, 16, 64
S5_T = P // S5_C
S5_K = L // S5_T
S5_KM = META // S5_T

HC = 64
HL = 6
NH = 4
LAM_INIT = 0.8 - 0.6 * 1.0
SCALE = 64 ** -0.5

NG, NPG, NE, FF = 4, 4, 16, 512
SLOTS = X * 2
NB = (SLOTS + NE * (P - 1)) // P
LEAST = SLOTS // P
NB += NB % 2

C_ID, C_MASK, C_TRI, C_ONES, C_HM = 0, 128, 256, 384, 512
C_TOK, C_DESC4, C_128J, C_SG, C_IOTAB = 896, 912, 928, 936, 937
C_COS = 976
C_SIN = C_COS + L
C_END = C_SIN + L
C_SWAP = C_END
P_GMIX, P_S5, P_D, P_LB, P_LAM = 0, 8, 56, 58, 60
P_B1, P_B2, P_C1, P_C2 = 64, 64 + 256, 64 + 512, 64 + 768
P_END = 64 + 1024

MEM = 48432
RING = 4
O_C = 9 * 1024 + 8 * L + 6 * X
SPLIT = 5 * D + RING * 2 * D


def constants():
    c = np.zeros((P, C_END + P), np.float32)
    i = np.arange(P)
    c[:, C_ID:C_ID + P] = np.eye(P)
    c[:, C_MASK:C_MASK + P] = np.where(i[None, :] <= i[:, None], 0.0, -1e30)
    c[:, C_TRI:C_TRI + P] = i[:, None] < i[None, :]
    c[:, C_ONES:C_ONES + P] = 1.0
    s, t = (i % HC)[:, None], np.arange(HC)[None, :]
    for lv in range(HL):
        if lv == 0:
            m = (s // 2 == t // 2) & (s <= t)
        else:
            b = 2 << lv
            m = (s // b == t // b) & (s % b < b // 2) & (t % b >= b // 2)
        c[:, C_HM + lv * HC:C_HM + (lv + 1) * HC] = m
    c[:, C_TOK:C_TOK + NT] = P * np.arange(NT)[None, :] + i[:, None]
    c[:, C_DESC4:C_DESC4 + 4] = [4, 3, 2, 1]
    c[:, C_128J:C_128J + 8] = 128 * np.arange(8)
    c[:, C_SG] = np.where(i < 64, -1.0, 1.0)
    c[:, C_IOTAB:C_IOTAB + NB] = np.arange(NB)
    c[i ^ 32, C_SWAP + i] = 1.0
    inv = (np.float32(1.0) / (np.float32(10000.0) ** (np.arange(0, 64, 2, dtype=np.float32) / np.float32(64)))).astype(np.float32)
    ang = (np.arange(L, dtype=np.float32)[:, None] * inv[None, :]).astype(np.float32)
    cos, sin = np.cos(ang).T, np.sin(ang).T
    c[:, C_COS:C_COS + L] = np.concatenate([cos] * 4)
    c[:, C_SIN:C_SIN + L] = np.concatenate([-sin, sin, -sin, sin])
    return c


class Chain:

    def __init__(self, eng, sem):
        self.eng, self.sem, self.n = eng, sem, 0

    def __call__(self, ins):
        self.n += 1
        ins.then_inc(self.sem, 1)
        self.eng.wait_ge(self.sem, self.n)


def build(nc, a, out):
    ctx = ExitStack()
    with ctx:
        def sem(name):
            return ctx.enter_context(nc.semaphore(name))

        con = ctx.enter_context(nc.sbuf_tensor("con", [P, C_END], F32))
        par = ctx.enter_context(nc.sbuf_tensor("par", [P, P_END], F32))
        sml = ctx.enter_context(nc.sbuf_tensor("sml", [P, 604], F32))
        with (nc.sbuf_tensor("below_split", [P, NT * D], F32), nc.sbuf_tensor("split", [P, SPLIT], F32R) as split_tensor,
              nc.sbuf_tensor("below_weights", [P, O_C - NT * D - SPLIT], F32),
              nc.sbuf_tensor("weights", [P, 2 * 3 * D * FF // P], F32) as weights_tensor):
            split, weights = split_tensor, weights_tensor
        mem = ctx.enter_context(nc.sbuf_tensor("mem", [P, MEM], F32))
        ps = ctx.enter_context(nc.psum_tensor("ps", [P, 8, 512], F32))

        def view(off, *shape):
            n = int(np.prod(shape))
            v = mem[:, off:off + n]
            if len(shape) == 2:
                v = v.rearrange("p (a b) -> p a b", a=shape[0])
            if len(shape) == 3:
                v = v.rearrange("p (a b c) -> p a b c", a=shape[0], b=shape[1])
            return v

        ident = con[:, C_ID:C_ID + P]
        SWAP = con[:, C_MASK:C_MASK + P]

        oV = 0
        oAK = oV + 9 * 1024
        oHF = oAK + 4 * L
        oU = oHF + 2 * L
        oHQ = oU + 2 * L
        oAQ = oHQ + 2 * X
        oC = oAQ + 4 * X
        assert oC == O_C
        V = view(oV, 9, 1024)
        AK, HF, AQ, HQ = view(oAK, 4, L), view(oHF, 2, L), view(oAQ, 4, X), view(oHQ, 2, X)
        UP = view(oU, 2, S5_T, S5_K)
        XT = view(oC, KD, L)
        oW = oC + KD * L
        oW1 = oW + 2 * L + S5_G * P
        WR = [view(o, KD, 512) for o in (oW, oW1)]
        oX = oW1 + 4096
        XN = view(oX, 3, 1024)
        JUNK = view(oX + 3072, 1024)
        SSQ, VAR, SD, RSTD = (sml[:, i * 9:i * 9 + 9] for i in range(4))

        params_loaded = sem("params_loaded")
        x_loaded = [sem(f"x_loaded{i}") for i in range(3)]
        w_loaded = [sem(f"w_loaded{i}") for i in range(6)]
        ssq_ready, var_ready, sd_ready, xn_ready = sem("ssq_ready"), sem("var_ready"), sem("sd_ready"), sem("xn_ready")
        xt_ready, xt_copied = sem("xt_ready"), sem("xt_copied")
        proj_done, zero_ready = sem("proj_done"), sem("zero_ready")
        proj_evac = sem("proj_evac")
        tables_loaded, swapped, roped, up_loaded = sem("tables_loaded"), sem("swapped"), sem("roped"), sem("up_loaded")
        dve_chain, act_chain, pool_chain = sem("dve_chain"), sem("act_chain"), sem("pool_chain")

        SECT = [(0, 512, 0), (512, 768, 1), (768, 1280, 0), (2304, 2816, 1), (1280, 1792, 0), (1792, 2304, 1)]
        CH = [(0, META), (META, META + 512), (META + 512, L)]
        jobs = []
        for m in range(2):
            for c in range(3):
                jobs.append((0, "u", m, c))
        for m in range(2):
            for c in (1, 2):
                jobs.append((0, "hq", m, c))
        for m in range(2):
            for c in range(3):
                jobs.append((1, "hf", m, c))
        for t in range(9):
            jobs.append((2, "vl", 0, t))
        for t in range(9):
            jobs.append((3, "vr", 0, t))
        for m in range(4):
            for c in (1, 2):
                jobs.append((4, "aq", m, c))
        for m in range(4):
            for c in range(3):
                jobs.append((5, "ak", m, c))
        last_of = {j[0]: n + 1 for n, j in enumerate(jobs)}
        first_of = {}
        for n, j in enumerate(jobs):
            first_of.setdefault(j[0], n)

        PREP = {12 + r: r for r in range(12)}
        GATES = {26 + i: i for i in range(3)}
        TURNS = [n for n, j in enumerate(jobs) if j[1] in ("aq", "ak")]
        NTQ = sum(j[1] == "aq" for j in jobs)

        def rows(t):
            return META if t == 0 else P

        def cols(t):
            return (0, META) if t == 0 else (META + P * (t - 1), META + P * t)

        ye_d = nc.dram_tensor("ye_d", (NB * P, D), F32, kind="Internal").ap()
        ye_zeroed, zero_tile = sem("ye_zeroed"), V[:, 1:3, 512:1024]
        ZEROED = NB - LEAST

        def pool_project(pool, link):
            nc.gpsimd.memset(zero_tile, 0.0).then_inc(zero_ready, 1)
            pool.wait_ge(zero_ready, 1)
            pool.wait_ge(xt_ready, 18)
            for b in range(NB - ZEROED, NB):
                pool.dma_start(ye_d[P * b:P * b + P, :].rearrange("p (a n) -> p a n", a=2), zero_tile).then_inc(ye_zeroed, 16)
            pool.wait_ge(up_stored, 32)
            nc.gpsimd.memset(TO, 0.0).then_inc(to_zeroed, 1)
            pool.wait_ge(prep_done, 8)
            link(nc.gpsimd.memset(RM, 1.0))
            link(nc.gpsimd.memset(RM[:, 0:1], 0.0))
            nc.gpsimd.memset(RM[:, META::HC], 0.0).then_inc(rm_ready, 1)

        def sp_project(sp):
            sp.dma_start(par[:, :], a["params"]).then_inc(params_loaded, 16)
            for lo, hi in ((0, C_MASK), (C_TRI, C_COS)):
                sp.dma_start(con[:, lo:hi], a["consts"][:, lo:hi]).then_inc(params_loaded, 16)
            for t in range(9):
                if t >= 3:
                    sp.wait_ge(xt_ready, 2 * (t - 2))
                src = a["meta_tokens"] if t == 0 else a["x"][P * (t - 1):P * t, :]
                sp.dma_start(XN[0:rows(t), t % 3, :], src).then_inc(x_loaded[t % 3], 16)
            sp.dma_start(con[:, C_COS:C_END], a["consts"][:, C_COS:C_END]).then_inc(tables_loaded, 16)
            sp.dma_start(SWAP, a["consts"][:, C_SWAP:C_SWAP + P]).then_inc(tables_loaded, 16)
            for s in range(2, 6):
                lo, hi, slot = SECT[s]
                sp.wait_ge(proj_done, last_of[s - 2])
                sp.dma_start(WR[slot][:, :, 0:hi - lo],
                             a["w_in"].rearrange("(k p) n -> p k n", p=P)[:, :, lo:hi]).then_inc(w_loaded[s], 16)
                if s == 3:
                    sp_s5_up(sp)
                if s == 4:
                    sp_s5_toeplitz(sp)

        def act_project(act, link):
            for s in range(2):
                lo, hi, slot = SECT[s]
                act.dma_start(WR[slot][:, :, 0:hi - lo],
                              a["w_in"].rearrange("(k p) n -> p k n", p=P)[:, :, lo:hi]).then_inc(w_loaded[s], 16)
            for t in range(9):
                R = rows(t)
                act.wait_ge(x_loaded[t % 3], 16 * (t // 3 + 1))
                nc.scalar.activation(JUNK[0:R, :], XN[0:R, t % 3, :], ACT.Square,
                                     accum_out=SSQ[0:R, t:t + 1]).then_inc(ssq_ready, 1)
                act.wait_ge(var_ready, t + 1)
                nc.scalar.activation(SD[0:R, t:t + 1], VAR[0:R, t:t + 1], ACT.Sqrt).then_inc(sd_ready, 1)
            act_s5_angles(act)
            for n in range(len(jobs)):
                evacuate(act, n)
                if n in PREP:
                    act_s5_prep(act, PREP[n])
                if n in GATES:
                    act_gates(act, link, GATES[n])
                if n + 1 == last_of[2]:
                    act.wait_ge(proj_evac, n + 1)
                    nc.scalar.activation(HQ, HQ, ACT.Silu)
                    nc.scalar.activation(V[:, 1:9, 256:512], V[:, 1:9, 256:512], ACT.Silu).then_inc(silu_ready, 1)

        def dve_norm(dve, link, t):
            R = rows(t)
            dve.wait_ge(ssq_ready, t + 1)
            nc.vector.tensor_scalar(VAR[0:R, t:t + 1], SSQ[0:R, t:t + 1], 1.0 / D, EPS, ALU.mult, ALU.add).then_inc(var_ready, 1)
            dve.wait_ge(sd_ready, t + 1)
            link(nc.vector.reciprocal(RSTD[0:R, t:t + 1], SD[0:R, t:t + 1]))
            nc.vector.tensor_scalar(XN[0:R, t % 3, :], XN[0:R, t % 3, :], RSTD[0:R, t:t + 1], None, ALU.mult).then_inc(xn_ready, 1)

        def dve_gain(dve, t):
            R = rows(t)
            lo, hi = cols(t)
            for j in range(2):
                dve.wait_ge(xt_ready, 2 * t + j + 1)
                nc.vector.tensor_tensor(XT[:, 4 * j:4 * j + 4, lo:hi],
                                        ps[:, 6 + j, 0:4 * R].rearrange("p (k t) -> p k t", k=4),
                                        par[:, P_GMIX + 4 * j:P_GMIX + 4 * j + 4].unsqueeze(2).to_broadcast([P, 4, R]),
                                        ALU.mult).then_inc(xt_copied, 1)

        def dve_project(dve, link):
            dve.wait_ge(params_loaded, 48)
            for t in range(10):
                if t < 9:
                    dve_norm(dve, link, t)
                if t >= 1:
                    dve_gain(dve, t - 1)
            dve_s5_phasors(dve, link)
            dve_s5_maps(dve, link)

        def evacuate(act, n):
            s, kind, m, c = jobs[n]
            copy = nc.scalar.copy
            act.wait_ge(proj_done, n + 1)
            b = ps[:, n % 6, :]
            if n == first_of[3]:
                act.wait_ge(ye_zeroed, 16 * ZEROED)
            if n == first_of[4]:
                act.wait_ge(cum_ready, 1)
            if n == first_of[5]:
                act.wait_ge(kk_moved, 1)
            if kind in ("vl", "vr"):
                R = rows(c)
                w = 256 if (kind == "vl" and c == 0) else 512
                o = 0 if kind == "vl" else 512
                ins = copy(V[0:R, c, o:o + w], b[0:R, 0:w])
            elif kind == "u":
                lo, hi = CH[c]
                ins = copy(UP[:, m, :, lo // S5_T:hi // S5_T], b[:, 0:hi - lo].rearrange("p (k s) -> p s k", s=S5_T))
            else:
                lo, hi = CH[c]
                dst = {"hq": HQ, "hf": HF, "ak": AK, "aq": AQ}[kind]
                sh = META if kind in ("hq", "aq") else 0
                ins = copy(dst[:, m, lo - sh:hi - sh], b[:, 0:hi - lo])
            ins.then_inc(proj_evac, 1)

        def pe_project(pe):
            pe.wait_ge(params_loaded, 48)
            for t in range(9):
                R = rows(t)
                pe.wait_ge(xn_ready, t + 1)
                for j in range(2):
                    if t >= 1:
                        pe.wait_ge(xt_copied, 2 * t + j - 1)
                    for k in range(4):
                        mm = nc.tensor.transpose(ps[:, 6 + j, k * R:(k + 1) * R], XN[0:R, t % 3, (4 * j + k) * P:(4 * j + k + 1) * P],
                                                 ident[0:R, 0:R])
                    mm.then_inc(xt_ready, 1)
            pe.wait_ge(xt_copied, 18)
            for n, (s, kind, m, c) in enumerate(jobs):
                if first_of[s] == n:
                    pe.wait_ge(w_loaded[s], 16)
                if n >= 6:
                    pe.wait_ge(proj_evac, n - 5)
                W = WR[SECT[s][2]]
                for k in range(KD):
                    if kind in ("vl", "vr"):
                        R = rows(c)
                        lo, hi = cols(c)
                        w = 256 if (kind == "vl" and c == 0) else 512
                        mm = nc.tensor.matmul(ps[0:R, n % 6, 0:w], XT[:, k, lo:hi], W[:, k, 0:w], start=(k == 0), stop=(k == KD - 1))
                    else:
                        lo, hi = CH[c]
                        m0 = m + (2 if kind == "hq" else 0)
                        mm = nc.tensor.matmul(ps[:, n % 6, 0:hi - lo], W[:, k, m0 * P:(m0 + 1) * P], XT[:, k, lo:hi],
                                              start=(k == 0), stop=(k == KD - 1))
                mm.then_inc(proj_done, 1)
                if n in PREP:
                    pe_s5_prep(pe, PREP[n])
                if n - 1 in TURNS:
                    pe_turn(pe, TURNS.index(n - 1))
            pe_turn(pe, len(TURNS) - 1)

        def turned(r):
            _, kind, m, c = jobs[TURNS[r]]
            lo, hi = CH[c]
            return (AQ[:, m, lo - META:hi - META] if kind == "aq" else AK[:, m, lo:hi]), slice(lo, hi)

        def pe_turn(pe, r):
            pe.wait_ge(proj_evac, TURNS[r] + 1)
            if r >= 2:
                pe.wait_ge(roped, r - 1)
            x, _ = turned(r)
            if r == 0:
                pe.wait_ge(tables_loaded, 32)
            nc.tensor.matmul(ps[:, 6 + r % 2, 0:x.shape[-1]], SWAP, x, start=True, stop=True).then_inc(swapped, 1)

        def dve_rope(dve, link, r):
            tt, stt = nc.vector.tensor_tensor, nc.vector.scalar_tensor_tensor
            x, cols_ = turned(r)
            b = ps[:, 6 + r % 2, 0:x.shape[-1]]
            cos, sin = con[:, C_COS:C_COS + L][:, cols_], con[:, C_SIN:C_SIN + L][:, cols_]
            dve.wait_ge(swapped, r + 1)
            if r < NTQ:
                link(stt(b, b, SCALE, sin, ALU.mult, ALU.mult))
                link(stt(x, x, SCALE, cos, ALU.mult, ALU.mult))
            else:
                link(tt(b, b, sin, ALU.mult))
                link(tt(x, x, cos, ALU.mult))
            tt(x, x, b, ALU.add).then_inc(roped, 1)

        NJ = len(jobs)
        projected = [(proj_evac, NJ)]

        oS = oX
        def take(*shape):
            nonlocal oS
            v = view(oS, *shape)
            oS += int(np.prod(shape))
            return v
        WIN = [take(S5_G, P), take(S5_G, P)]
        L1 = take(S5_G, S5_T + 1, S5_C)
        UC, UI, MJ, PR, PI, SPR, SPI = (take(S5_T + 1, S5_G) for _ in range(7))
        BX2 = mem[:, oS:oS + 2 * S5_G * S5_C]
        BB, BX = take(S5_G, S5_C), take(S5_G, S5_C)
        q = [take(S5_G) for _ in range(14)]
        SNI, SN = take(2, S5_G), take(2, S5_G)
        assert oS <= MEM
        TO = view(oU, S5_G, P)
        TA, TB = view(oAK, 2080), view(oAK + 2080, 2080)
        G3 = TA[:, 0:2048].rearrange("p (g s c) -> p g s c", g=S5_G, s=S5_T)
        H3 = TB[:, 0:2048].rearrange("p (g s c) -> p g s c", g=S5_G, s=S5_T)
        GW = [view(oAQ + i * S5_G * P, S5_G, P) for i in range(2)]
        GA, GB = (v.rearrange("p g (s c) -> p g s c", s=S5_T) for v in GW)
        HS = TA[0:S5_C, 0:2048].rearrange("p (g n) -> p g n", g=S5_G)
        KK, L2 = view(oW, 2, L), view(oW + 2 * L, S5_G, S5_T, S5_C)
        NE0 = 32
        EC, ES = (par[:, P_B1 + i * 512:P_B1 + i * 512 + 512].rearrange("p (g k) -> p g k", k=NE0) for i in range(2))
        oS = oC
        COS, SIN = take(S5_G, S5_K), take(S5_G, S5_K)
        T1, T2 = take(S5_G * S5_K), take(S5_G * S5_K)
        assert oS <= oW
        oS = oW1
        US = take(S5_G, S5_K)
        assert oS <= oX
        XR = T1.rearrange("p (g k) -> p g k", g=S5_G)
        XS = T2.rearrange("p (g k) -> p g k", g=S5_G)
        YO = T1[:, 0:2048].rearrange("p (g k) -> p g k", g=S5_G)
        MIX = [view(oU, 2, X), HQ, AQ]

        def mix(k):
            return MIX[0][:, k, :] if k < 2 else MIX[1][:, k - 2, :] if k < 4 else MIX[2][:, k - 4, :]

        up_d = nc.dram_tensor("up_d", (2 * P, S5_T, S5_K), F32, kind="Internal").ap()
        y_d = nc.dram_tensor("y_d", (2 * P, S5_T, P), F32, kind="Internal").ap()
        dt_ready, phase_ready, sin_ready = sem("dt_ready"), sem("phase_ready"), sem("sin_ready")
        mag_ready, g_ready = sem("mag_ready"), sem("g_ready")
        l_ready, prep_done, prep_copied = sem("l_ready"), sem("prep_done"), sem("prep_copied")
        to_zeroed, to_loaded, up_stored, us_loaded = sem("to_zeroed"), sem("to_loaded"), sem("up_stored"), sem("us_loaded")
        x_done, x_turned, w_ready = sem("x_done"), sem("x_turned"), sem("w_ready")
        y_done, y_copied, y_stored, y_loaded = sem("y_done"), sem("y_copied"), sem("y_stored"), sem("y_loaded")
        yu_ready, gelu_ready, glu_done, glu_gate, s5_done = sem("yu_ready"), sem("gelu_ready"), sem("glu_done"), sem("glu_gate"), sem("s5_done")
        late_loaded = sem("late_loaded")
        UNITS = [(g, min(g + 3, S5_G)) for g in range(0, S5_G, 3)]

        def sp_s5_up(sp):
            sp.wait_ge(proj_evac, 6)
            for m in range(2):
                sp.dma_start(up_d[m * P:(m + 1) * P], UP[:, m]).then_inc(up_stored, 16)

        def sp_s5_toeplitz(sp):
            sp.wait_ge(to_zeroed, 1)
            sp.wait_ge(prep_copied, 12)
            for s in range(S5_T):
                sp.dma_start(TO[S5_C * s:S5_C * (s + 1), :, S5_C * s:], HS[:, :, 0:P - S5_C * s]).then_inc(to_loaded, 16)

        def sp_s5(sp):
            sp.wait_ge(proj_done, NJ)
            sp.wait_ge(up_stored, 32)
            src = up_d.rearrange("(g c) s k -> s c g k", c=S5_C)
            for s in range(S5_T):
                sp.dma_start(US[S5_C * s:S5_C * (s + 1)], src[s]).then_inc(us_loaded, 16)
            sp.wait_ge(y_done, 4)
            for m in range(2):
                sp.dma_start(UP[:, m], up_d[m * P:(m + 1) * P]).then_inc(up_loaded, 16)
            sp.wait_ge(y_copied, 4)
            dst = y_d.rearrange("(g c) t k -> t c g k", c=S5_C)
            for t in range(S5_T):
                sp.dma_start(dst[t], YO[S5_C * t:S5_C * (t + 1)]).then_inc(y_stored, 16)

        def act_s5_angles(act):
            act.wait_ge(params_loaded, 48)
            nc.scalar.activation(q[0], par[:, P_S5 + 32:P_S5 + 48], ACT.Exp).then_inc(dt_ready, 1)
            act.wait_ge(phase_ready, 1)
            nc.scalar.activation(q[8], q[1], ACT.Exp).then_inc(mag_ready, 1)
            act.wait_ge(phase_ready, 2)
            nc.scalar.activation(SN, SNI, ACT.Sin).then_inc(sin_ready, 1)

        def act_s5_prep(act, r):
            act.wait_ge(prep_done, r + 1)
            b = ps[:, 6 + r % 2, :]
            if r < 8:
                ins = nc.scalar.copy(WIN[r // 4][:, 4 * (r % 4):4 * (r % 4) + 4, :], b.rearrange("p (g n) -> p g n", g=4))
            else:
                ins = nc.scalar.copy(HS[:, 4 * (r - 8):4 * (r - 8) + 4, :], b[0:S5_C].rearrange("p (g n) -> p g n", g=4))
            ins.then_inc(prep_copied, 1)

        def act_s5(act, link):
            for b in range(4):
                act.wait_ge(y_done, b + 1)
                nc.scalar.copy(YO[:, 4 * b:4 * b + 4, :], ps[:, b, :].rearrange("p (g n) -> p g n", g=4)).then_inc(y_copied, 1)

        def dve_s5_phasors(dve, link):
            lr, li = par[:, P_S5:P_S5 + 16], par[:, P_S5 + 16:P_S5 + 32]
            sg = con[:, C_SG:C_SG + 1]
            tt, ts, stt = nc.vector.tensor_tensor, nc.vector.tensor_scalar, nc.vector.scalar_tensor_tensor
            dt_, lrdt, th, kf, em, e2, zr, den, mag, t0, t1, fr, fi, sfi = q[:14]
            dve.wait_ge(dt_ready, 1)
            tt(lrdt, lr, dt_, ALU.mult).then_inc(phase_ready, 1)
            link(tt(th, li, dt_, ALU.mult))
            MAGIC = 12582912.0
            link(ts(kf, th, float(1 / (2 * np.pi)), MAGIC, ALU.mult, ALU.add))
            link(ts(kf, kf, -MAGIC, None, ALU.add))
            for part in (6.28125, 0.0019350051879882812, 3.0199157e-07):
                link(stt(th, kf, -part, th, ALU.mult, ALU.add))
            link(ts(SNI[:, 0], th, 3.1415925, -3.1415925, ALU.min, ALU.max))
            ts(SNI[:, 1], th, 0.5, None, ALU.mult).then_inc(phase_ready, 1)
            dve.wait_ge(phase_ready, 1)
            link(ts(t0, lrdt, 1.0 / 8, 1.0, ALU.mult, ALU.add))
            for j in range(7, 1, -1):
                link(tt(t0, t0, lrdt, ALU.mult))
                link(ts(t0, t0, 1.0 / j, 1.0, ALU.mult, ALU.add))
            link(tt(em, t0, lrdt, ALU.mult))
            link(tt(t1, lrdt, lrdt, ALU.mult))
            link(ts(t1, t1, 0.16, None, ALU.is_gt))
            dve.wait_ge(mag_ready, 1)
            link(ts(e2, mag, -1.0, None, ALU.add))
            link(nc.vector.copy_predicated(em, t1.bitcast(I32), e2))
            link(ts(MJ[:, 1], em, 1.0, None, ALU.add))
            link(nc.vector.memset(MJ[:, 0], 1.0))
            dve.wait_ge(sin_ready, 1)
            link(nc.vector.memset(UC[:, 0], 1.0))
            link(nc.vector.memset(UI[:, 0], 0.0))
            link(nc.vector.tensor_copy(UI[:, 1], SN[:, 0]))
            link(tt(t0, SN[:, 1], SN[:, 1], ALU.mult))
            link(ts(t1, t0, -2.0, None, ALU.mult))
            link(ts(UC[:, 1], t1, 1.0, None, ALU.add))

            def cmul(oc, os_, ac, as_, bc, bs, shape):
                n = int(np.prod(shape[1:]))
                pa, pb = TA[:, 0:n], TA[:, 1040:1040 + n]
                if len(shape) == 3:
                    pa, pb = (v.rearrange("p (a b) -> p a b", a=shape[1]) for v in (pa, pb))
                link(tt(pa, ac, bc, ALU.mult))
                link(tt(pb, as_, bs, ALU.mult))
                link(tt(oc, pa, pb, ALU.subtract))
                link(tt(pa, ac, bs, ALU.mult))
                link(tt(pb, as_, bc, ALU.mult))
                link(tt(os_, pa, pb, ALU.add))

            for m in (1, 2, 4):
                sh = [P, m, S5_G]
                b = [v[:, m:m + 1].to_broadcast(sh) for v in (UC, UI, MJ)]
                cmul(UC[:, m + 1:2 * m + 1], UI[:, m + 1:2 * m + 1], UC[:, 1:m + 1], UI[:, 1:m + 1], b[0], b[1], sh)
                link(tt(MJ[:, m + 1:2 * m + 1], MJ[:, 1:m + 1], b[2], ALU.mult))
            link(tt(PR, MJ, UC, ALU.mult))
            link(tt(PI, MJ, UI, ALU.mult))
            link(ts(SPR, PR, sg, None, ALU.mult))
            link(ts(SPI, PI, sg, None, ALU.mult))
            link(tt(t0, em, UC[:, 1], ALU.mult))
            link(tt(zr, t0, t1, ALU.add))
            link(tt(den, lr, lr, ALU.mult))
            link(tt(t0, li, li, ALU.mult))
            link(tt(den, den, t0, ALU.add))
            link(nc.vector.reciprocal(den, den))
            link(tt(t0, zr, lr, ALU.mult))
            link(tt(t1, PI[:, 1], li, ALU.mult))
            link(tt(t0, t0, t1, ALU.add))
            link(tt(fr, t0, den, ALU.mult))
            link(tt(t0, PI[:, 1], lr, ALU.mult))
            link(tt(t1, zr, li, ALU.mult))
            link(tt(t0, t0, t1, ALU.subtract))
            link(tt(fi, t0, den, ALU.mult))
            link(ts(sfi, fi, sg, None, ALU.mult))

        def dve_s5_maps(dve, link):
            tt, ts = nc.vector.tensor_tensor, nc.vector.tensor_scalar
            sg, fr, sfi = con[:, C_SG:C_SG + 1], q[11], q[13]
            B1, B2, C1, C2 = (par[:, o:o + 256].rearrange("p (g c) -> p g c", g=S5_G) for o in (P_B1, P_B2, P_C1, P_C2))
            g2 = [P, S5_G, S5_C]
            ta, tb = (TA[:, o:o + 256].rearrange("p (g c) -> p g c", g=S5_G) for o in (0, 256))
            bf, bs = fr.unsqueeze(2).to_broadcast(g2), sfi.unsqueeze(2).to_broadcast(g2)
            for o, u, v, op in ((BB, B1, B2, ALU.add), (BX, B2, B1, ALU.subtract)):
                link(tt(ta, u, bf, ALU.mult))
                link(tt(tb, v, bs, ALU.mult))
                link(tt(o, ta, tb, op))

            def powers(tab, lo, n, rev=False):
                v = tab[:, lo:lo + n].rearrange("p s g -> p g s")
                if rev:
                    v = v[:, :, ::-1]
                return v.unsqueeze(3).to_broadcast([P, S5_G, n, S5_C])

            def rep(v, n):
                return v.unsqueeze(2).to_broadcast([P, S5_G, n, S5_C])

            link(tt(G3, rep(BB, 8), powers(PR, 0, 8, True), ALU.mult))
            link(tt(H3, rep(BX, 8), powers(SPI, 0, 8, True), ALU.mult))
            tt(GA, G3, H3, ALU.add).then_inc(g_ready, 1)
            dve.wait_ge(g_ready, 1)
            link(tt(G3, rep(BB, 8), powers(PI, 0, 8, True), ALU.mult))
            link(tt(H3, rep(BX, 8), powers(SPR, 0, 8, True), ALU.mult))
            tt(GB, G3, H3, ALU.subtract).then_inc(g_ready, 1)
            link(tt(L1, rep(C1, 9), powers(SPR, 0, 9), ALU.mult))
            dve.wait_ge(g_ready, 2)
            for lo, n in ((0, 8), (8, 1)):
                t3 = TB[:, 0:256 * n].rearrange("p (g s c) -> p g s c", g=S5_G, s=n)
                link(tt(t3, rep(C2, n), powers(PI, lo, n), ALU.mult))
                ins = stt_neg(L1[:, :, lo:lo + n], t3)
                if lo == 8:
                    ins.then_inc(l_ready, 1)
                else:
                    link(ins)
            dve_hgrn_bounds(dve, link)
            dve_gates(dve, link)
            dve.wait_ge(tables_loaded, 32)
            for r in range(NTQ):
                dve_rope(dve, link, r)
            dve.wait_ge(proj_done, last_of[4])
            nc.vector.tensor_copy(KK, KT_).then_inc(kk_moved, 1)
            for lo in range(0, 8, 2):
                t3 = BX2.rearrange("p (g s c) -> p g s c", g=S5_G, s=2)
                l2 = L2[:, :, lo:lo + 2]
                link(tt(l2, rep(C1, 2), powers(SPI, lo + 1, 2), ALU.mult))
                link(tt(t3, rep(C2, 2), powers(PR, lo + 1, 2), ALU.mult))
                link(tt(l2, l2, t3, ALU.subtract))
            for r in range(NTQ, len(TURNS)):
                dve_rope(dve, link, r)
                if r == NTQ + 4:
                    dve_first_angles(link)

        def dve_s5(dve, link):
            tt, stt = nc.vector.tensor_tensor, nc.vector.scalar_tensor_tensor
            dve.wait_ge(proj_done, NJ)
            dve.wait_ge(roped, len(TURNS))
            for o, e in ((COS, EC), (SIN, ES)):
                link(nc.vector.tensor_copy(o[:, :, 0:NE0], e))
            for m in (NE0 - 1, 2 * (NE0 - 1), 4 * (NE0 - 1)):
                angles(link, COS, SIN, m, min(m, S5_K - 1 - m), T2[:, 0:1024], T2[:, 1040:2080])

        def angles(link, cs, sn, m, n_new, ta, tb):
            tt = nc.vector.tensor_tensor
            sh = [P, S5_G, n_new]
            pa, pb = (t[:, 0:S5_G * n_new].rearrange("p (g k) -> p g k", g=S5_G) for t in (ta, tb))
            bc, bs = (v[:, :, m:m + 1].to_broadcast(sh) for v in (cs, sn))
            ac, as_ = (v[:, :, 1:n_new + 1] for v in (cs, sn))
            oc, os_ = (v[:, :, m + 1:m + 1 + n_new] for v in (cs, sn))
            link(tt(pa, ac, bc, ALU.mult))
            link(tt(pb, as_, bs, ALU.mult))
            link(tt(oc, pa, pb, ALU.subtract))
            link(tt(pa, ac, bs, ALU.mult))
            link(tt(pb, as_, bc, ALU.mult))
            link(tt(os_, pa, pb, ALU.add))

        def dve_first_angles(link):
            link(nc.vector.memset(EC[:, :, 0], 1.0))
            link(nc.vector.memset(ES[:, :, 0], 0.0))
            link(nc.vector.tensor_copy(EC[:, :, 1], UC[:, 8]))
            link(nc.vector.tensor_copy(ES[:, :, 1], UI[:, 8]))
            m = 1
            while m < NE0 - 1:
                angles(link, EC, ES, m, min(m, NE0 - 1 - m), BX2[:, 0:256], BX2[:, 256:512])
                m *= 2

        def dve_turned(dve, link):
            tt = nc.vector.tensor_tensor
            for n, (lo, hi) in enumerate(UNITS):
                b = 2 * (n % 4)
                w = (hi - lo) * S5_K
                dve.wait_ge(x_done, n + 1)
                link(tt(XR[:, lo:hi], ps[:, b, 0:w].rearrange("p (g k) -> p g k", k=S5_K), COS[:, lo:hi], ALU.mult))
                tt(XS[:, lo:hi], ps[:, b + 1, 0:w].rearrange("p (g k) -> p g k", k=S5_K), SIN[:, lo:hi], ALU.mult).then_inc(x_turned, 1)
                dve.wait_ge(x_turned, n + 1)
                link(tt(XR[:, lo:hi], XR[:, lo:hi], XS[:, lo:hi], ALU.add))
            for g in range(S5_G):
                ins = nc.vector.tensor_tensor_scan(XS[:, g], MJ[:, 8, g:g + 1].to_broadcast([P, S5_K]), XR[:, g], 0.0, ALU.mult, ALU.add)
            link(ins)
            tt(COS, COS, XS, ALU.mult).then_inc(w_ready, 1)
            tt(SIN, SIN, XS, ALU.mult).then_inc(w_ready, 1)

        def stt_neg(x, y):
            return nc.vector.scalar_tensor_tensor(x, x, -1.0, y, ALU.mult, ALU.subtract)

        def pe_s5_prep(pe, r):
            if r >= 2:
                pe.wait_ge(prep_copied, r - 1)
            if r < 8:
                pe.wait_ge(g_ready, r // 4 + 1)
            else:
                pe.wait_ge(l_ready, 1)
            for j in range(4):
                g = 4 * (r % 4) + j
                o = ps[:, 6 + r % 2, j * P:(j + 1) * P]
                if r < 8:
                    mm = nc.tensor.transpose(o, GW[r // 4][:, g], ident)
                else:
                    mm = nc.tensor.matmul(o[0:S5_C], BB[:, g], L1[:, g, 0:S5_T].rearrange("p t c -> p (t c)"), start=True, stop=True)
            mm.then_inc(prep_done, 1)

        def pe_s5(pe):
            for s, v in projected:
                pe.wait_ge(s, v)
            pe.wait_ge(roped, len(TURNS))
            pe.wait_ge(us_loaded, 16 * S5_T)
            pe.wait_ge(prep_copied, 12)
            for n, (lo, hi) in enumerate(UNITS):
                b = 2 * (n % 4)
                if n >= 4:
                    pe.wait_ge(x_turned, n - 3)
                for g in range(lo, hi):
                    for w in range(2):
                        mm = nc.tensor.matmul(ps[:, b + w, (g - lo) * S5_K:(g - lo + 1) * S5_K], WIN[w][:, g], US[:, g], start=True, stop=True)
                mm.then_inc(x_done, 1)
            pe.wait_ge(x_turned, len(UNITS))
            pe.wait_ge(to_loaded, 16 * S5_T)
            pe.wait_ge(w_ready, 2)
            for g in range(S5_G):
                o = ps[:, g // 4, (g % 4) * P:(g % 4 + 1) * P]
                nc.tensor.matmul(o, TO[:, g], US[:, g, S5_KM:], start=True, stop=False)
                nc.tensor.matmul(o, L1[:, g, 1:].rearrange("p t c -> p (t c)"), COS[:, g, S5_KM - 1:S5_K - 1], start=False, stop=False)
                mm = nc.tensor.matmul(o, L2[:, g].rearrange("p t c -> p (t c)"), SIN[:, g, S5_KM - 1:S5_K - 1], start=False, stop=True)
                if g % 4 == 3:
                    mm.then_inc(y_done, 1)

        CU = HF
        ZT, KT_ = view(oAK, 2, L), view(oAK + 2 * L, 2, L)
        RM = view(oAQ, L)
        oS = oC
        QC, KP, OH = take(X), take(L), take(NT, 256)
        DE = take(3, 512)
        KT = take(9, P)
        TM = take(2, HL * HC)
        PB = take(2, HC)
        assert oS <= oW
        oS = oW + 2 * L
        QE, KE = [take(HL, 512) for _ in range(2)], [take(HL, 512) for _ in range(2)]
        SH = take(X // HC, P)
        assert oS <= MEM
        QF, KF = ([v.rearrange("p a b -> p (a b)") for v in x] for x in (QE, KE))
        YT = QF[0][:, 0:2048].rearrange("p (m t k) -> p m t k", m=2, t=S5_T)
        WGLU = QF[0][:, 2048:3072].rearrange("p (k n) -> p k n", k=2)
        GT = KF[0][:, 0:2048].rearrange("p (m n) -> p m n", m=2)
        SGM = KF[1][:, 0:2048].rearrange("p (m n) -> p m n", m=2)
        OSQ = QF[1][:, 0:2048].rearrange("p (t c) -> p t c", t=NT)
        GN, GS = sml[:, 40:104], sml[:, 104:232]
        LBD, LBE, LBW, LBV, LBF, LFL, OML, L1P, LC0 = (sml[:, 240 + 2 * i:242 + 2 * i] for i in range(9))
        DEC, OMS, OSD, ORS = sml[:, 260:277], sml[:, 280:312], sml[:, 312:344], sml[:, 344:376]
        gains_loaded = sem("gains_loaded")
        lb_dve, lb_act = sem("lb_dve"), sem("lb_act")
        silu_ready = sem("silu_ready")
        zl_ready, ls_ready, ksig_ready, gap_ready, gapl_ready, lf_ready = (
            sem(n) for n in ("zl_ready", "ls_ready", "ksig_ready", "gap_ready", "gapl_ready", "lf_ready"))
        rm_ready, kk_moved, cum_ready, qdec_ready, kd_ready, kdec_ready, qc_ready, kp_ready = (
            sem(n) for n in ("rm_ready", "kk_moved", "cum_ready", "qdec_ready", "kd_ready", "kdec_ready", "qc_ready", "kp_ready"))
        kt_turned, kt_copied, u_done, state_ready = sem("kt_turned"), sem("kt_copied"), sem("u_done"), sem("state_ready")
        d_ready, e_ready, qe_done, ke_done = sem("d_ready"), sem("e_ready"), sem("qe_done"), sem("ke_done")
        sc_done, sc_masked, p_ready, o_done, o1_copied, o_added = (
            sem(n) for n in ("sc_done", "sc_masked", "p_ready", "o_done", "o1_copied", "o_added"))
        osq_ready, oms_ready, osd_ready, oh_ready, ot_done, hgrn_done = (
            sem(n) for n in ("osq_ready", "oms_ready", "osd_ready", "oh_ready", "ot_done", "hgrn_done"))
        LN2_64 = float(64 * np.log(2.0))

        def sp_hgrn(sp):
            sp.dma_start(GN, a["hgrn_norm_g"].to_broadcast([P, 64])).then_inc(gains_loaded, 16)
            sp.dma_start(GS, a["subln_g"].to_broadcast([P, P])).then_inc(gains_loaded, 16)
            sp.wait_ge(swapped, len(TURNS))
            sp.dma_start(con[:, C_MASK:C_MASK + P], a["consts"][:, C_MASK:C_MASK + P]).then_inc(gains_loaded, 16)
            sp.wait_ge(sc_done, 24)
            sp.dma_start(WGLU, a["w_glu"].rearrange("(k p) n -> p k n", p=P)).then_inc(late_loaded, 16)
            sp.wait_ge(y_stored, 16 * S5_T)
            for m in range(2):
                sp.dma_start(YT[:, m], y_d[m * P:(m + 1) * P]).then_inc(y_loaded, 16)

        def pool_hgrn(pool, link):
            pool.wait_ge(y_stored, 16 * S5_T)
            for u in range(4):
                hp, half = u // 2, u % 2
                c0 = 512 * half
                if u >= 2:
                    pool.wait_ge(sc_done, 8 * (u - 1))
                for lv in range(HL):
                    pool.wait_ge(e_ready, 7 * u + (1 if lv == 0 else 2 + lv))
                    sl = 1 if lv == 0 else (lv + 1) % 3
                    nc.gpsimd.tensor_tensor(KE[u % 2][:, lv], KK[:, hp, META + c0:META + c0 + 512], DE[:, sl], ALU.mult).then_inc(ke_done, 1)

        def act_gates(act, link, step):
            f = nc.scalar.activation
            if step == 0:
                act.wait_ge(lb_dve, 1)
                f(LBE, LBD, ACT.Exp).then_inc(lb_act, 1)
                act.wait_ge(to_loaded, 16 * S5_T)
                act.wait_ge(proj_evac, last_of[1])
                link(f(ZT, HF, ACT.Abs))
                link(f(ZT, ZT, ACT.Exp, scale=-1.0))
                f(ZT, ZT, ACT.Ln, bias=1.0).then_inc(zl_ready, 1)
                act.wait_ge(lb_dve, 2)
                f(LFL, LBF, ACT.Ln, scale=float(2.0 ** 64)).then_inc(lb_act, 1)
                f(L1P, OML, ACT.Ln).then_inc(lb_act, 1)
            elif step == 1:
                act.wait_ge(ls_ready, 1)
                f(KT_, KT_, ACT.Exp).then_inc(ksig_ready, 1)
            else:
                act.wait_ge(gap_ready, 1)
                link(f(ZT, ZT, ACT.Abs))
                link(f(ZT, ZT, ACT.Exp, scale=-1.0))
                f(ZT, ZT, ACT.Ln, bias=1.0).then_inc(gapl_ready, 1)

        def act_hgrn(act, link):
            f = nc.scalar.activation
            act.wait_ge(y_stored, 16 * S5_T)
            for hp in range(2):
                act.wait_ge(cum_ready, 1)
                if hp:
                    act.wait_ge(o_added, 4)
                f(QC, CU[:, hp, META:], ACT.Exp).then_inc(qdec_ready, 1)
                act.wait_ge(kd_ready, hp + 1)
                f(KP, KP, ACT.Exp).then_inc(kdec_ready, 1)
                f(DEC[:, 0:1], CU[:, hp, META - 1:META], ACT.Exp)
                f(DEC[:, 1:17], CU[:, hp, META + HC - 1::HC], ACT.Exp).then_inc(kdec_ready, 1)
                for b in range(3):
                    act.wait_ge(kt_turned, 3 * hp + b + 1)
                    if b == 0:
                        ins = nc.scalar.copy(KT[0:META, 0], ps[0:META, 4, 0:P])
                    else:
                        ins = nc.scalar.copy(KT[:, 4 * b - 3:4 * b + 1], ps[:, 4 + b, :].rearrange("p (t c) -> p t c", t=4))
                    ins.then_inc(kt_copied, 1)
                if hp == 0:
                    act_levels(act, 0)
                for half in range(2):
                    u = 2 * hp + half
                    if u < 3:
                        act_levels(act, u + 1)
                    else:
                        for m in range(2):
                            act.wait_ge(yu_ready, m + 1)
                            nc.scalar.activation(GT[:, m], YT[:, m].rearrange("p t k -> p (t k)"), ACT.Gelu_apprx_tanh).then_inc(gelu_ready, 1)
                    act.wait_ge(o_done, 8 * u + 8)
                    for r in range(2):
                        R = slice(64 * r, 64 * r + 64)
                        for h in range(2):
                            ins = nc.scalar.copy(OH[R, 4 * half:4 * half + 4, P * hp + 64 * h:P * hp + 64 * h + 64],
                                                 ps[R, 6 + r, 256 * h:256 * h + 256].rearrange("p (t v) -> p t v", t=4))
                    ins.then_inc(o1_copied, 1)
            act.wait_ge(o_added, 8)
            f(OSQ, OH, ACT.Square).then_inc(osq_ready, 1)
            act.wait_ge(oms_ready, 1)
            f(OSD, OMS, ACT.Sqrt).then_inc(osd_ready, 1)
            for m in range(2):
                for h in range(2):
                    act.wait_ge(glu_done, 2 * m + h + 1)
                    nc.scalar.activation(SGM[:, m, 512 * h:512 * h + 512], ps[:, 2 * m + h, :], ACT.Sigmoid).then_inc(glu_gate, 1)
            for n in range(4):
                k, h = n // 2, n % 2
                act.wait_ge(ot_done, n + 1)
                nc.scalar.copy(mix(2 + k)[:, 512 * h:512 * h + 512], ps[:, n, :]).then_inc(hgrn_done, 1)

        def act_levels(act, u):
            f = nc.scalar.activation
            act.wait_ge(d_ready, 6 * u + 1)
            f(DE[:, 1], DE[:, 0], ACT.Exp, scale=-1.0).then_inc(e_ready, 1)
            f(DE[:, 0], DE[:, 0], ACT.Exp).then_inc(e_ready, 1)
            for lv in range(1, HL):
                act.wait_ge(d_ready, 6 * u + lv + 1)
                sl = (lv + 1) % 3
                f(DE[:, sl], DE[:, sl], ACT.Exp).then_inc(e_ready, 1)

        def dve_hgrn_bounds(dve, link):
            tt, ts = nc.vector.tensor_tensor, nc.vector.tensor_scalar
            lb = par[:, P_LB:P_LB + 2]
            tt(LBD, lb, lb, ALU.subtract).then_inc(lb_dve, 1)
            dve.wait_ge(lb_act, 1)
            link(nc.vector.reciprocal(LBW, LBE))
            link(tt(LBW, LBW, LBE, ALU.mult))
            link(tt(LBV, LBW, LBW, ALU.subtract))
            link(ts(LBF, LBV, 1e-30, None, ALU.max))
            link(tt(LC0, LBV, LBF, ALU.subtract))
            ts(OML, LBV, -1.0, 1.0, ALU.mult, ALU.add).then_inc(lb_dve, 1)

        def dve_gates(dve, link):
            ts, stt = nc.vector.tensor_scalar, nc.vector.scalar_tensor_tensor
            dve.wait_ge(zl_ready, 1)
            link(stt(KT_, HF, 0.0, ZT, ALU.max, ALU.add))
            ts(KT_, KT_, -1.0, None, ALU.mult).then_inc(ls_ready, 1)
            link(stt(HF, HF, 0.0, ZT, ALU.min, ALU.subtract))
            dve.wait_ge(lb_act, 3)
            link(ts(LFL, LFL, -LN2_64, None, ALU.add))
            for m in range(2):
                link(ts(HF[:, m], HF[:, m], L1P[:, m:m + 1], None, ALU.add))
                ins = ts(ZT[:, m], HF[:, m], LFL[:, m:m + 1], None, ALU.subtract)
            ins.then_inc(gap_ready, 1)
            dve.wait_ge(ksig_ready, 1)
            for m in range(2):
                link(ts(KT_[:, m], KT_[:, m], OML[:, m:m + 1], LC0[:, m:m + 1], ALU.mult, ALU.add))
            dve.wait_ge(gapl_ready, 1)
            for m in range(2):
                link(stt(HF[:, m], HF[:, m], LFL[:, m:m + 1], ZT[:, m], ALU.max, ALU.add))
            dve.wait_ge(rm_ready, 1)
            for m in range(2):
                ins = nc.vector.tensor_tensor_scan(HF[:, m], RM, HF[:, m], 0.0, ALU.mult, ALU.add)
            ins.then_inc(cum_ready, 1)
            dve.wait_ge(cum_ready, 1)

        def dve_hgrn(dve, link):
            tt, ts, stt = nc.vector.tensor_tensor, nc.vector.tensor_scalar, nc.vector.scalar_tensor_tensor
            dve.wait_ge(y_stored, 16 * S5_T)
            for hp in range(2):
                if hp:
                    dve.wait_ge(qdec_ready, 2)
                for lo, n, w in ((0, 1, META), (META, 16, HC)):
                    cu = CU[:, hp, lo:lo + n * w].rearrange("p (n w) -> p n w", n=n)
                    ins = tt(KP[:, lo:lo + n * w].rearrange("p (n w) -> p n w", n=n),
                             cu[:, :, w - 1:w].to_broadcast([P, n, w]), cu, ALU.subtract)
                ins.then_inc(kd_ready, 1)
                dve.wait_ge(silu_ready, 1)
                dve.wait_ge(qdec_ready, hp + 1)
                tt(QC, QC, HQ[:, hp], ALU.mult).then_inc(qc_ready, 1)
                dve.wait_ge(kdec_ready, 2 * hp + 1)
                tt(KP, KP, KK[:, hp], ALU.mult).then_inc(kp_ready, 1)
                if hp == 0:
                    for n in range(len(LEVEL_STEPS)):
                        dve_level_step(dve, 0, n)
                dve.wait_ge(u_done, hp + 1)
                dve.wait_ge(kdec_ready, 2 * hp + 2)
                for c in range(16):
                    uc = u_bank(c)
                    if c == 0:
                        ins = nc.vector.tensor_copy(SH[:, 0], uc)
                    else:
                        ins = stt(SH[:, c], SH[:, c - 1], DEC[:, c:c + 1], uc, ALU.mult, ALU.add)
                    if c < 15:
                        link(ins)
                ins.then_inc(state_ready, 1)
                for half in range(2):
                    dve_scores(dve, 2 * hp + half)
            dve.wait_ge(osq_ready, 1)
            dve.wait_ge(o_added, 8)
            link(nc.vector.tensor_reduce(OMS, OSQ.rearrange("p t (h v) -> p (t h) v", h=4), AX.X, ALU.add))
            ts(OMS, OMS, 1.0 / 64, EPS, ALU.mult, ALU.add).then_inc(oms_ready, 1)
            dve.wait_ge(osd_ready, 1)
            link(nc.vector.reciprocal(ORS, OSD))
            dve.wait_ge(gains_loaded, 48)
            o4 = OH.rearrange("p t (h v) -> p (t h) v", h=4)
            link(tt(o4, o4, ORS.unsqueeze(2).to_broadcast([P, 32, 64]), ALU.mult))
            link(tt(o4, o4, GN.unsqueeze(1).to_broadcast([P, 32, 64]), ALU.mult))
            tt(OH, OH, V[:, 1:9, 256:512], ALU.mult).then_inc(oh_ready, 1)
            for m in range(2):
                for h in range(2):
                    dve.wait_ge(glu_done, 4 + 2 * m + h + 1)
                    dve.wait_ge(glu_gate, 2 * m + h + 1)
                    tt(mix(m).rearrange("p (k t) -> p t k", t=S5_T)[:, 4 * h:4 * h + 4],
                       ps[:, 4 + 2 * m + h, :].rearrange("p (t k) -> p t k", t=4),
                       SGM[:, m, 512 * h:512 * h + 512].rearrange("p (t k) -> p t k", t=4), ALU.mult).then_inc(s5_done, 1)

        LEVEL_STEPS = [("gaps", 0), ("gaps", 1)]
        for lv in range(HL):
            LEVEL_STEPS += [("queries", lv)] + [("gaps", lv + 2)] * (lv + 2 < HL)

        def dve_level_step(dve, u, n):
            tt = nc.vector.tensor_tensor
            hp, half = u // 2, u % 2
            lo = META + 512 * half
            what, lv = LEVEL_STEPS[n]
            sl = 0 if lv == 0 else (lv + 1) % 3
            if n == 0 and u >= 2:
                dve.wait_ge(sc_done, 8 * (u - 1))
            if what == "queries":
                dve.wait_ge(e_ready, 7 * u + 2 + lv)
                tt(QE[u % 2][:, lv], HQ[:, hp, lo - META:lo - META + 512], DE[:, sl], ALU.mult).then_inc(qe_done, 1)
                return
            B = 2 << lv
            if lv < 2 and u or lv in (2, 4, 5):
                dve.wait_ge(qe_done, 6 * u + (0, 0, 1, 0, 2, 3)[lv])
            if lv == 0:
                if u:
                    dve.wait_ge(ke_done, 6 * u)
            elif lv >= 3:
                dve.wait_ge(ke_done, 6 * u + lv - 2)
            cu = CU[:, hp, lo:lo + 512].rearrange("p (n b) -> p n b", b=B)
            de = DE[:, sl].rearrange("p (n b) -> p n b", b=B)
            if lv == 0:
                tt(de, cu, cu[:, :, 0:1].to_broadcast([P, 512 // B, B]), ALU.subtract).then_inc(d_ready, 1)
            else:
                h = B // 2
                ref = cu[:, :, h - 1:h].to_broadcast([P, 512 // B, h])
                tt(de[:, :, 0:h], ref, cu[:, :, 0:h], ALU.subtract)
                tt(de[:, :, h:B], cu[:, :, h:B], ref, ALU.subtract).then_inc(d_ready, 1)

        def dve_scores(dve, u):
            hm = con[:, C_HM:C_HM + HL * HC]
            hp, half = u // 2, u % 2
            for j in range(8):
                n = 8 * u + j
                dve.wait_ge(sc_done, n + 1)
                nc.vector.tensor_tensor(TM[:, n % 2], ps[:, n % 4, 0:HL * HC], hm, ALU.mult).then_inc(sc_masked, 1)
                dve.wait_ge(sc_masked, n + 1)
                if n >= 2:
                    dve.wait_ge(o_done, n - 1)
                nc.vector.tensor_reduce(PB[:, n % 2], TM[:, n % 2].rearrange("p (l t) -> p t l", l=HL), AX.X, ALU.add).then_inc(p_ready, 1)
                if u < 3:
                    for k in range(len(LEVEL_STEPS) * j // 8, len(LEVEL_STEPS) * (j + 1) // 8):
                        dve_level_step(dve, u + 1, k)
            if u == 3:
                for m in range(2):
                    dve.wait_ge(y_loaded, 32)
                    dve.wait_ge(up_loaded, 32)
                    nc.vector.scalar_tensor_tensor(YT[:, m], UP[:, m, :, S5_KM:], par[:, P_D + m:P_D + m + 1], YT[:, m], ALU.mult, ALU.add).then_inc(yu_ready, 1)
            dve.wait_ge(o_done, 8 * u + 8)
            dve.wait_ge(o1_copied, u + 1)
            for h in range(2):
                o = OH[:, 4 * half:4 * half + 4, P * hp + 64 * h:P * hp + 64 * h + 64]
                nc.vector.tensor_tensor(o, o, ps[:, 4 + h, 0:256].rearrange("p (t v) -> p t v", t=4), ALU.add).then_inc(o_added, 1)

        def u_bank(c):
            i = (c + 1) // 2 if c % 2 or c == 0 else (c - 2) // 2
            b = (i // 4) if c % 2 or c == 0 else (3, 7)[i // 4]
            return ps[:, b, (i % 4) * P:(i % 4 + 1) * P]

        def pe_hgrn(pe):
            pe.wait_ge(y_copied, 4)
            for hp in range(2):
                pe.wait_ge(kp_ready, hp + 1)
                pe.wait_ge(qc_ready, hp + 1)
                if hp:
                    pe.wait_ge(o_added, 4)
                mm = nc.tensor.transpose(ps[0:META, 4, 0:P], KP[:, 0:META], ident)
                mm.then_inc(kt_turned, 1)
                for t in range(8):
                    mm = nc.tensor.transpose(ps[:, 5 + t // 4, (t % 4) * P:(t % 4 + 1) * P], KP[:, META + P * t:META + P * (t + 1)], ident)
                    if t % 4 == 3:
                        mm.then_inc(kt_turned, 1)
                pe.wait_ge(kt_copied, 3 * hp + 3)
                for c in range(16):
                    if c == 0:
                        rr, t = slice(0, META), 0
                    else:
                        rr, t = slice(64 * ((c - 1) % 2), 64 * ((c - 1) % 2) + 64), 1 + (c - 1) // 2
                    mm = nc.tensor.matmul(u_bank(c), KT[rr, t], V[rr, t, P * hp:P * hp + P], start=True, stop=True)
                mm.then_inc(u_done, 1)
                pe.wait_ge(state_ready, hp + 1)
                for half in range(2):
                    u = 2 * hp + half
                    pe.wait_ge(qe_done, 6 * u + 6)
                    pe.wait_ge(ke_done, 6 * u + 6)
                    if half:
                        pe.wait_ge(o_added, 2 * u)
                    for j in range(10):
                        if j < 8:
                            scores(pe, u, j)
                        if j >= 2:
                            outputs(pe, u, j - 2)
            pe.wait_ge(late_loaded, 16)
            pe.wait_ge(gelu_ready, 2)
            pe.wait_ge(sc_masked, 32)
            pe.wait_ge(o_added, 8)
            for n, m in enumerate((2, 3, 0, 1)):
                for h in range(2):
                    for k in range(2):
                        mm = nc.tensor.matmul(ps[:, 2 * n + h, :], WGLU[:, k, m * P:(m + 1) * P], GT[:, k, 512 * h:512 * h + 512],
                                              start=(k == 0), stop=(k == 1))
                    mm.then_inc(glu_done, 1)
            pe.wait_ge(oh_ready, 1)
            pe.wait_ge(glu_gate, 4)
            for n in range(4):
                k, h = n // 2, n % 2
                for t in range(4):
                    mm = nc.tensor.transpose(ps[:, n, P * t:P * t + P], OH[:, 4 * h + t, P * k:P * k + P], ident)
                mm.then_inc(ot_done, 1)

        def scores(pe, u, j):
            tl, h = j // 2, j % 2
            n = 8 * u + j
            if n >= 4:
                pe.wait_ge(sc_masked, n - 3)
            R = slice(64 * h, 64 * h + 64)
            for c in range(2):
                cc = slice(P * tl + 64 * c, P * tl + 64 * c + 64)
                for lv in range(HL):
                    mm = nc.tensor.matmul(ps[64 * c:64 * c + 64, n % 4, HC * lv:HC * lv + HC], KE[u % 2][R, lv, cc], QE[u % 2][R, lv, cc],
                                          start=True, stop=True)
            mm.then_inc(sc_done, 1)

        def outputs(pe, u, j):
            tl, h = j // 2, j % 2
            hp, half = u // 2, u % 2
            n = 8 * u + j
            t = 4 * half + tl
            R = slice(64 * h, 64 * h + 64)
            for c in range(2):
                nc.tensor.matmul(ps[64 * c:64 * c + 64, 4 + h, 64 * tl:64 * tl + 64], QC[R, P * t + 64 * c:P * t + 64 * c + 64],
                                 SH[R, 2 * t + c, 64 * h:64 * h + 64], start=True, stop=True)
            pe.wait_ge(p_ready, n + 1)
            for c in range(2):
                S = slice(64 * c, 64 * c + 64)
                mm = nc.tensor.matmul(ps[S, 6 + c, 256 * h + 64 * tl:256 * h + 64 * tl + 64], PB[S, n % 2],
                                      V[S, 1 + t, P * hp + 64 * h:P * hp + 64 * h + 64], start=True, stop=True)
            mm.then_inc(o_done, 1)

        oS = oC
        PR_ = [take(2, L) for _ in range(2)]
        AT = [take(9, P) for _ in range(2)]
        OA = take(NT, 512)
        WO = take(KD, 1024)
        OSQA = take(512)
        assert oS <= MEM
        PRD, LAME, NLAM, GS8 = sml[:, 380:382], sml[:, 382:384], sml[:, 384:385], sml[:, 104:232]
        NMX, SUM, R0, R1, RW = (sml[:, 390 + 4 * i:394 + 4 * i] for i in range(5))
        ASS, HALF, ARS = sml[:, 412:416], sml[:, 416:420], sml[:, 420:424]
        prd_ready, lam_sum, lame_ready, nlam_ready, half_ready = (
            sem(n) for n in ("prd_ready", "lam_sum", "lame_ready", "nlam_ready", "half_ready"))
        qk_done, max_ready, exp_done, a_ready, ring_ready, ring_free = (
            sem(n) for n in ("qk_done", "max_ready", "exp_done", "a_ready", "ring_ready", "ring_free"))
        asq_ready, ams_ready, oa_ready = sem("asq_ready"), sem("ams_ready"), sem("oa_ready")
        NJOB = 4 * NT

        def groups(i):
            x = list(range(i + 1))
            g = [x[b:b + 4] for b in range(0, i + 1, 4)]
            if len(g[-1]) < 4:
                g[-1].append("meta")
            else:
                g.append(["meta"])
            return g

        def step_of(kind, n):
            return n + 1 if kind == "t" else n + 2 if kind == "o" else min(4 * n + 7, NJOB + 5)

        ring = []
        for step in range(NJOB + 6):
            ring += [("t", n, g) for n in range(NJOB) if step_of("t", n) == step for g in groups(n // 4)]
            ring += [("o", n, None) for n in range(NJOB) if step_of("o", n) == step]
            ring += [("m", n, None) for n in range(NT) if step_of("m", n) == step]
        at_ready = {}
        for r, (kind, n, g) in enumerate(ring):
            if kind == "t":
                at_ready[n] = r + 1
        out_at = {n: r + 1 for r, (kind, n, g) in enumerate(ring) if kind == "o"}
        mix_at = {n: r + 1 for r, (kind, n, g) in enumerate(ring) if kind == "m"}

        def sp_attention(sp):
            sp.wait_ge(oh_ready, 1)
            sp.wait_ge(hgrn_done, 4)
            sp.dma_start(WO, a["w_out"].rearrange("(k p) n -> p k n", p=P)).then_inc(late_loaded, 16)

        def pool_attention(pool, link):
            nc.gpsimd.memset(HALF, -0.5).then_inc(half_ready, 1)
            pool.wait_ge(half_ready, 1)
            pool.wait_ge(gains_loaded, 48)
            link(nc.gpsimd.tensor_scalar(GS8, GS8, 1.0 - LAM_INIT, None, ALU.mult))
            for i in range(NT):
                pool.wait_ge(ams_ready, i + 1)
                link(nc.gpsimd.tensor_tensor(ARS, ASS, HALF, ALU.pow))
                o = OA[:, i].rearrange("p (h v) -> p h v", h=4)
                link(nc.gpsimd.tensor_tensor(o, o, ARS.unsqueeze(2).to_broadcast([P, 4, P]), ALU.mult))
                nc.gpsimd.tensor_tensor(o, o, GS8.unsqueeze(1).to_broadcast([P, 4, P]), ALU.mult).then_inc(oa_ready, 1)

        def dve_lambda(dve, link):
            tt = nc.vector.tensor_tensor
            v = par[0:64, P_LAM:P_LAM + 4].rearrange("p (a b) -> p a b", b=2)
            tt(PRD[0:64], v[:, :, 0], v[:, :, 1], ALU.mult).then_inc(prd_ready, 1)
            dve.wait_ge(lame_ready, 1)
            link(tt(NLAM, LAME[:, 1:2], LAME[:, 0:1], ALU.subtract))
            nc.vector.tensor_scalar(NLAM, NLAM, -LAM_INIT, None, ALU.add).then_inc(nlam_ready, 1)

        def logits(c):
            return ps[:, 3 * c:3 * c + 3, :].rearrange("p b n -> p (b n)")

        def dve_attention(dve, link):
            dve_lambda(dve, link)
            dve.wait_ge(nlam_ready, 1)
            for n in range(NJOB + 1):
                if n >= 1:
                    dve_combine(dve, link, n - 1)
                if n < NJOB:
                    dve_maximum(dve, n, 0)
                    dve_maximum(dve, n, 1)
            dve_means(dve, link, NT - 1)

        def dve_maximum(dve, n, c):
            dve.wait_ge(qk_done, 2 * n + c + 1)
            if n >= 2:
                dve.wait_ge(exp_done, 2 * (n - 2) + c + 1)
            nc.vector.tensor_reduce(NMX[:, 2 * (n % 2) + c:2 * (n % 2) + c + 1], logits(c)[:, 0:META + P * (n // 4 + 1)], AX.X, ALU.max,
                                    negate=True).then_inc(max_ready, 1)

        def dve_combine(dve, link, j):
            stt = nc.vector.scalar_tensor_tensor
            o = 2 * (j % 2)
            nk = META + P * (j // 4 + 1)
            dve.wait_ge(exp_done, 2 * j + 2)
            if j >= 2:
                dve.wait_ge(ring_free, out_at[j - 2])
            link(nc.vector.reciprocal(R1[:, o:o + 2], SUM[:, o:o + 2]))
            link(stt(RW[:, j % 2:j % 2 + 1], SUM[:, o:o + 1], NLAM, R1[:, o + 1:o + 2], ALU.mult, ALU.mult))
            A = PR_[j % 2]
            stt(A[:, 0, 0:nk], A[:, 1, 0:nk], RW[:, j % 2:j % 2 + 1], A[:, 0, 0:nk], ALU.mult, ALU.add).then_inc(a_ready, 1)
            if j % 4 == 1 and j >= 5:
                dve_means(dve, link, j // 4 - 1)

        def dve_means(dve, link, i):
            dve.wait_ge(asq_ready, i + 1)
            if i:
                dve.wait_ge(oa_ready, i)
            link(nc.vector.tensor_reduce(ASS, OSQA.rearrange("p (h v) -> p h v", h=4), AX.X, ALU.add))
            nc.vector.tensor_scalar(ASS, ASS, 1.0 / P, EPS, ALU.mult, ALU.add).then_inc(ams_ready, 1)

        def act_attention(act, link):
            f = nc.scalar.activation
            act.wait_ge(lam_sum, 1)
            f(LAME, ps[:, 7, 0:2], ACT.Exp).then_inc(lame_ready, 1)
            r = 0
            for n in range(NJOB + 6):
                if n < NJOB:
                    nk = META + P * (n // 4 + 1)
                    while r < len(ring) and ring[r][0] == "t" and step_of(*ring[r][:2]) <= n:
                        act_ring(act, link, r)
                        r += 1
                    for c in range(2):
                        act.wait_ge(max_ready, 2 * n + c + 1)
                        if n >= 2:
                            act.wait_ge(a_ready, n - 1)
                            act.wait_ge(ring_ready, at_ready[n - 2])
                        o = 2 * (n % 2) + c
                        f(PR_[n % 2][:, c, 0:nk], logits(c)[:, 0:nk], ACT.Exp, bias=NMX[:, o:o + 1],
                          accum_out=SUM[:, o:o + 1]).then_inc(exp_done, 1)
                while r < len(ring) and step_of(*ring[r][:2]) <= n:
                    act_ring(act, link, r)
                    r += 1

        def act_ring(act, link, r):
            kind, n, g = ring[r]
            f = nc.scalar.activation
            act.wait_ge(ring_ready, r + 1)
            b = ps[:, 6 + r % 2, :]
            if kind == "t":
                x = [v for v in g if v != "meta"]
                ins = None
                if x:
                    ins = nc.scalar.copy(AT[n % 2][:, x[0]:x[-1] + 1], b[:, 0:P * len(x)].rearrange("p (k q) -> p k q", q=P))
                if "meta" in g:
                    ins = nc.scalar.copy(AT[n % 2][0:META, 8], b[0:META, P * len(x):P * len(x) + P])
                ins.then_inc(ring_free, 1)
            elif kind == "o":
                i, h = n // 4, n % 4
                f(OA[:, i, P * h:P * h + P], b[:, 0:P], ACT.Identity, scale=R1[:, 2 * (n % 2):2 * (n % 2) + 1]).then_inc(ring_free, 1)
                if h == 3:
                    act.wait_ge(ring_free, r + 1)
                    if i:
                        act.wait_ge(ams_ready, i)
                    f(OSQA, OA[:, i], ACT.Square).then_inc(asq_ready, 1)
            else:
                nc.scalar.copy(AQ[:, :, P * n:P * n + P], b.rearrange("p (h q) -> p h q", h=4)).then_inc(ring_free, 1)

        def pe_attention(pe):
            pe.wait_ge(hgrn_done, 4)
            pe.wait_ge(s5_done, 4)
            pe.wait_ge(prd_ready, 1)
            nc.tensor.matmul(ps[:, 7, 0:2], con[0:64, C_ONES:C_ONES + P], PRD[0:64], start=True, stop=True).then_inc(lam_sum, 1)
            pe.wait_ge(lame_ready, 1)
            r = 0
            for n in range(NJOB + 6):
                if n < NJOB:
                    pe_logits(pe, n)
                while r < len(ring) and step_of(*ring[r][:2]) <= n:
                    pe_ring(pe, r)
                    r += 1
                if n in (NJOB + 1, NJOB + 3):
                    pe_out_tile(pe, (n - NJOB) // 2)

        def pe_logits(pe, n):
            i, h = n // 4, n % 4
            nk = META + P * (i + 1)
            if n == 0:
                pe.wait_ge(roped, len(TURNS))
                pe.wait_ge(gains_loaded, 48)
            for c in range(2):
                R = slice(64 * c, 64 * c + 64)
                if n >= 1:
                    pe.wait_ge(exp_done, 2 * (n - 1) + c + 1)
                for k in range(0, nk, 512):
                    w = min(512, nk - k)
                    m = max(nk - P, k)
                    masked = m < k + w
                    mm = nc.tensor.matmul(logits(c)[:, k:k + w], AQ[R, h, P * i:P * i + P], AK[R, h, k:k + w], start=True, stop=not masked)
                    if masked:
                        mm = nc.tensor.matmul(logits(c)[:, m:k + w], ident, con[:, C_MASK + m - (nk - P):C_MASK + k + w - (nk - P)],
                                              start=False, stop=True)
                mm.then_inc(qk_done, 1)

        def pe_ring(pe, r):
            kind, n, g = ring[r]
            if r >= 2:
                pe.wait_ge(ring_free, r - 1)
            b = ps[:, 6 + r % 2, :]
            if kind == "t":
                pe.wait_ge(a_ready, n + 1)
                A = PR_[n % 2][:, 0]
                for j, v in enumerate(g):
                    if v == "meta":
                        mm = nc.tensor.transpose(b[0:META, P * j:P * j + P], A[:, 0:META], ident)
                    else:
                        mm = nc.tensor.transpose(b[:, P * j:P * j + P], A[:, META + P * v:META + P * v + P], ident)
            elif kind == "o":
                i, h = n // 4, n % 4
                pe.wait_ge(ring_free, at_ready[n])
                vc = slice(512 + P * h, 512 + P * h + P)
                for k in range(i + 1):
                    nc.tensor.matmul(b[:, 0:P], AT[n % 2][:, k], V[:, 1 + k, vc], start=(k == 0), stop=False)
                mm = nc.tensor.matmul(b[:, 0:P], AT[n % 2][0:META, 8], V[0:META, 0, vc], start=False, stop=True)
            else:
                pe.wait_ge(oa_ready, n + 1)
                for h in range(4):
                    mm = nc.tensor.transpose(b[:, P * h:P * h + P], OA[:, n, P * h:P * h + P], ident)
            mm.then_inc(ring_ready, 1)

        H1 = view(oV, NT, D)
        XB, XN2 = view(oAK, 2, D), view(oAK + 2 * D, 2, D)
        XT2 = view(oAK + 4 * D, 2, KD, P)
        GF, WRT, SQJ = view(oC + 21500, D), view(oC + 21500 + D, KD, 20), view(oC + 21500 + D + 160, D)
        SS2, VA2, SD2, RS2 = (sml[:, 8 * i:8 * i + 8] for i in range(4))
        BR = sml[:, 430:450]
        xn_d = nc.dram_tensor("xn_d", (X, D), F32, kind="Internal").ap()
        ffn_loaded, xb_loaded = sem("ffn_loaded"), [sem("xb_loaded0"), sem("xb_loaded1")]
        out_done, h1_ready, ss2_ready, va2_ready, sd2_ready, xn2_ready = (
            sem(n) for n in ("out_done", "h1_ready", "ss2_ready", "va2_ready", "sd2_ready", "xn2_ready"))
        xn2_stored, xt2_ready, xt2_copied, log_done = (
            [sem("xn2_stored0"), sem("xn2_stored1")], sem("xt2_ready"), sem("xt2_copied"), sem("log_done"))

        def sp_out(sp):
            sp.wait_ge(exp_done, 2 * NJOB)
            sp.dma_start(GF, a["norm_ffn_g"].to_broadcast([P, D])).then_inc(ffn_loaded, 16)
            sp.dma_start(WRT, a["w_router"].rearrange("(k p) n -> p k n", p=P)).then_inc(ffn_loaded, 16)
            sp.dma_start(BR, a["b_router"].to_broadcast([P, 20])).then_inc(ffn_loaded, 16)
            for t in range(NT + 1):
                if t == 2:
                    sp.wait_ge(ring_free, len(ring))
                    for i, w in enumerate(("w_gate", "w_up")):
                        sp.dma_start(WGU[:, 0:KD, i], a[w][0].rearrange("(k p) n -> p k n", p=P)).then_inc(first_loaded, 16)
                if t < NT:
                    if t >= 2:
                        sp.wait_ge(h1_ready, t - 1)
                    sp.dma_start(XB[:, t % 2], a["x"][P * t:P * t + P, :]).then_inc(xb_loaded[t % 2], 16)
                if t >= 1:
                    sp.wait_ge(xn2_ready, t)
                    sp.dma_start(xn_d[P * (t - 1):P * t, :], XN2[:, (t - 1) % 2]).then_inc(xn2_stored[(t - 1) % 2], 16)

        def act_out(act, link):
            for t in range(NT + 1):
                if t < NT:
                    act.wait_ge(h1_ready, t + 1)
                    nc.scalar.activation(SQJ, H1[:, t], ACT.Square,
                                         accum_out=SS2[:, t:t + 1]).then_inc(ss2_ready, 1)
                    act.wait_ge(va2_ready, t + 1)
                    nc.scalar.activation(SD2[:, t:t + 1], VA2[:, t:t + 1], ACT.Sqrt).then_inc(sd2_ready, 1)
                if t >= 1:
                    for j in range(2):
                        act.wait_ge(xt2_ready, 2 * (t - 1) + j + 1)
                        nc.scalar.copy(XT2[:, (t - 1) % 2, 4 * j:4 * j + 4],
                                       ps[:, 4 + j, :].rearrange("p (k q) -> p k q", k=4)).then_inc(xt2_copied, 1)

        def dve_out(dve, link):
            for t in range(NT):
                dve.wait_ge(out_done, t + 1)
                dve.wait_ge(xb_loaded[t % 2], 16 * (t // 2 + 1))
                if t == 0:
                    dve.wait_ge(ring_free, out_at[NJOB - 1])
                nc.vector.tensor_tensor(H1[:, t], ps[:, 2 * (t % 2):2 * (t % 2) + 2, :].rearrange("p b n -> p (b n)"),
                                        XB[:, t % 2], ALU.add).then_inc(h1_ready, 1)
                dve.wait_ge(ss2_ready, t + 1)
                nc.vector.tensor_scalar(VA2[:, t:t + 1], SS2[:, t:t + 1], 1.0 / D, EPS, ALU.mult, ALU.add).then_inc(va2_ready, 1)
                dve.wait_ge(sd2_ready, t + 1)
                link(nc.vector.reciprocal(RS2[:, t:t + 1], SD2[:, t:t + 1]))
                if t >= 2:
                    dve.wait_ge(xn2_stored[t % 2], 16 * (t // 2))
                    dve.wait_ge(xt2_ready, 2 * (t - 1))
                if t == 0:
                    dve.wait_ge(ffn_loaded, 48)
                nc.vector.scalar_tensor_tensor(XN2[:, t % 2], H1[:, t], RS2[:, t:t + 1], GF, ALU.mult, ALU.mult).then_inc(xn2_ready, 1)

        def pe_out_tile(pe, t):
            if t == 0:
                pe.wait_ge(late_loaded, 32)
                pe.wait_ge(exp_done, 2 * NJOB)
                pe.wait_ge(ring_free, mix_at[1])
            if t >= 2:
                pe.wait_ge(h1_ready, t - 1)
            for h in range(2):
                for k in range(KD):
                    mm = nc.tensor.matmul(ps[:, 2 * (t % 2) + h, :], mix(k)[:, P * t:P * t + P], WO[:, k, 512 * h:512 * h + 512],
                                          start=(k == 0), stop=(k == KD - 1))
            mm.then_inc(out_done, 1)

        def pe_out(pe):
            pe.wait_ge(ring_free, len(ring))
            for t in range(NT + 2):
                if 2 <= t < NT:
                    pe_out_tile(pe, t)
                if 1 <= t <= NT:
                    s = t - 1
                    pe.wait_ge(xn2_ready, s + 1)
                    for j in range(2):
                        if s:
                            pe.wait_ge(xt2_copied, 2 * s - 1 + j)
                        for k in range(4):
                            mm = nc.tensor.transpose(ps[:, 4 + j, P * k:P * k + P], XN2[:, s % 2, P * (4 * j + k):P * (4 * j + k) + P], ident)
                        mm.then_inc(xt2_ready, 1)
                if t >= 2:
                    s = t - 2
                    pe.wait_ge(xt2_copied, 2 * s + 2)
                    if s == 0:
                        pe.wait_ge(ffn_loaded, 48)
                    for k in range(KD):
                        mm = nc.tensor.matmul(ps[:, 6, 20 * s:20 * s + 20], XT2[:, s % 2, k], WRT[:, k], start=(k == 0), stop=(k == KD - 1))
                    mm.then_inc(log_done, 1)

        oS = oU
        LG = take(NT, 20)
        GM, GX, GS_, GP = take(NT), take(NT, 4), take(NT), take(NT)
        OHG, VAL, MX = take(NT, 4), take(NT, 4), take(NT)
        IG, M1, O1, M2, O2, E2 = take(NT, 4), take(NT), take(NT, 4), take(NT), take(NT, 4), take(NT)
        EXO = take(NT, 4, 4)
        OK1, OK2, OKS = take(NT, NE), take(NT, NE), take(NT, NE)
        RK, TOT, PRE = take(NT, NE), take(NT, NE), take(NT, NE)
        CNT, BLK, CB, BASE, BCMP, ECMP = take(NE), take(NE), take(NE), take(NE), take(NE, 8), take(NB, NE)
        SLF, EBF = take(2, NT), take(NB)
        NEW, OLD, RUN, PRV, BUF, NHALF, NPR = take(NB), take(NB), take(NB), take(NB), take(NB), take(1), take(1)
        PCMP = take(NB // 2)
        BLKF, REM, HOTR, HOTB = take(2, NT), take(2, NT), take(2 * NT, P), take(2 * NT, NB)
        IOTAP = ps[:, 2, 0:P]
        assert oS <= oC
        W12 = sml[:, 460:476].rearrange("p (k t) -> p k t", k=2)
        slots = sml[:, 480:496].bitcast(I32).rearrange("p (k t) -> p k t", k=2)
        ixb, ixc = sml[:, 538:538 + NB].bitcast(I32), sml[:, 602:604].bitcast(I32)
        eblk, ebuf, enew = (sml[:, o:o + NB].bitcast(I32) for o in (506, 570, 398))
        efree, edown, npair = sml[:, 366:366 + NB].bitcast(I32), sml[:, 334:334 + NB].bitcast(I32), sml[:, 504:505].bitcast(I32)
        rt_gap, rt_exp, onehot_ready, rank_done, slots_ready, tables_ready, slot_hot_ready, idx_done = (
            sem(n) for n in ("rt_gap", "rt_exp", "onehot_ready", "rank_done", "slots_ready", "tables_ready", "slot_hot_ready", "idx_done"))

        def act_route(act, link):
            act.wait_ge(rt_gap, 1)
            nc.scalar.activation(GX, GX, ACT.Exp).then_inc(rt_exp, 1)
            act.wait_ge(rt_gap, 2)
            nc.scalar.activation(E2, E2, ACT.Exp).then_inc(rt_exp, 1)

        def pe_route(pe):
            pe.wait_ge(onehot_ready, 1)
            nc.tensor.matmul(IOTAP, con[:, C_ONES:C_ONES + P], con[:, C_TRI:C_TRI + P], start=True, stop=True)
            f = OKS.rearrange("p t e -> p (t e)")
            nc.tensor.matmul(ps[:, 0, 0:P], con[:, C_TRI:C_TRI + P], f, start=True, stop=True)
            nc.tensor.matmul(ps[:, 0, P:2 * P], con[:, C_ONES:C_ONES + P], f, start=True, stop=True).then_inc(rank_done, 1)

            pe.wait_ge(slot_hot_ready, 1)
            for n in range(2 * NT):
                mm = nc.tensor.matmul(ps[:, 1, 0:NB], HOTR[:, n], HOTB[:, n], start=(n == 0), stop=(n == 2 * NT - 1))
            mm.then_inc(idx_done, 1)

        def dve_route(dve, link):
            tt, ts, stt, red = (nc.vector.tensor_tensor, nc.vector.tensor_scalar, nc.vector.scalar_tensor_tensor,
                                nc.vector.tensor_reduce)
            s4 = [P, NT, 4]

            def b4(v):
                return v.unsqueeze(2).to_broadcast(s4)

            def first_of_max(oh, x, m):
                link(red(m, x, AX.X, ALU.max))
                link(tt(oh, x, b4(m), ALU.is_equal))
                link(tt(VAL, oh, con[:, C_DESC4:C_DESC4 + 4].unsqueeze(1).to_broadcast(s4), ALU.mult))
                link(red(MX, VAL, AX.X, ALU.max))
                link(tt(oh, VAL, b4(MX), ALU.is_equal))

            dve.wait_ge(log_done, NT)
            link(tt(LG, ps[:, 6, 0:20 * NT].rearrange("p (t n) -> p t n", t=NT), BR.unsqueeze(1).to_broadcast([P, NT, 20]), ALU.add))
            gl = LG[:, :, 0:4]
            first_of_max(OHG, gl, GM)
            tt(GX, gl, b4(GM), ALU.subtract).then_inc(rt_gap, 1)
            link(tt(EXO, LG[:, :, 4:20].rearrange("p t (g e) -> p t g e", g=4), OHG.unsqueeze(3).to_broadcast([P, NT, 4, 4]), ALU.mult))
            link(red(IG, EXO.rearrange("p t g e -> p t e g"), AX.X, ALU.add))
            first_of_max(O1, IG, M1)
            link(stt(IG, O1, -3.0e38, IG, ALU.mult, ALU.add))
            first_of_max(O2, IG, M2)
            tt(E2, M2, M1, ALU.subtract).then_inc(rt_gap, 1)
            for o, oh in ((OK1, O1), (OK2, O2)):
                link(tt(o.rearrange("p t (g e) -> p t g e", g=4), OHG.unsqueeze(3).to_broadcast([P, NT, 4, 4]),
                        oh.unsqueeze(2).to_broadcast([P, NT, 4, 4]), ALU.mult))
            tt(OKS, OK1, OK2, ALU.add).then_inc(onehot_ready, 1)
            dve.wait_ge(rank_done, 1)
            link(red(CNT, ps[:, 0, P:2 * P].rearrange("p (t e) -> p e t", t=NT), AX.X, ALU.add))
            link(tt(BCMP, CNT.unsqueeze(2).to_broadcast([P, NE, 8]), con[:, C_128J:C_128J + 8].unsqueeze(1).to_broadcast([P, NE, 8]), ALU.is_gt))
            link(red(BLK, BCMP, AX.X, ALU.add))
            link(nc.vector.tensor_tensor_scan(CB, con[:, C_ONES:C_ONES + NE], BLK, 0.0, ALU.mult, ALU.add))
            link(nc.vector.tensor_copy(TOT, ps[:, 0, P:2 * P].rearrange("p (t e) -> p t e", t=NT)))
            link(nc.vector.memset(PRE[:, 0], 0.0))
            for t in range(1, NT):
                link(tt(PRE[:, t], PRE[:, t - 1], TOT[:, t - 1], ALU.add))
            link(tt(RK, ps[:, 0, 0:P].rearrange("p (t e) -> p t e", t=NT), PRE, ALU.add))
            link(tt(BASE, CB, BLK, ALU.subtract))
            link(ts(BASE, BASE, float(P), None, ALU.mult))
            link(tt(RK, RK, BASE.unsqueeze(1).to_broadcast([P, NT, NE]), ALU.add))
            for k, o in enumerate((OK1, OK2)):
                link(tt(o, o, RK, ALU.mult))
                link(red(SLF[:, k], o, AX.X, ALU.add))
            MAGIC = 12582912.0
            link(ts(BLKF, SLF, 1.0 / P, 0.5 / P - 0.5, ALU.mult, ALU.add))
            link(ts(BLKF, BLKF, MAGIC, None, ALU.add))
            link(ts(BLKF, BLKF, -MAGIC, None, ALU.add))
            link(stt(REM, BLKF, -float(P), SLF, ALU.mult, ALU.add))
            n2 = 2 * NT
            fl = [v.rearrange("p k t -> p (k t)").unsqueeze(2) for v in (REM, BLKF)]
            link(tt(HOTR, fl[0].to_broadcast([P, n2, P]), IOTAP.unsqueeze(1).to_broadcast([P, n2, P]), ALU.is_equal))
            link(tt(HOTB, fl[1].to_broadcast([P, n2, NB]), con[:, C_IOTAB:C_IOTAB + NB].unsqueeze(1).to_broadcast([P, n2, NB]), ALU.is_equal))
            for k in range(2):
                ins = tt(HOTB[:, NT * k:NT * k + NT], HOTB[:, NT * k:NT * k + NT], con[:, C_TOK:C_TOK + NT].unsqueeze(2).to_broadcast([P, NT, NB]), ALU.mult)
            ins.then_inc(slot_hot_ready, 1)
            dve.wait_ge(idx_done, 1)
            nc.vector.tensor_copy(ixb, ps[:, 1, 0:NB]).then_inc(slots_ready, 1)
            link(nc.vector.tensor_copy(slots[:, :, :], SLF))
            dve.wait_ge(rt_exp, 2)
            link(red(GS_, GX, AX.X, ALU.add))
            link(nc.vector.reciprocal(GP, GS_))
            link(ts(M1, E2, 1.0, None, ALU.add))
            link(nc.vector.reciprocal(M1, M1))
            link(tt(W12[:, 0], M1, GP, ALU.mult))
            link(tt(W12[:, 1], W12[:, 0], E2, ALU.mult))
            link(tt(ECMP, CB.unsqueeze(1).to_broadcast([P, NB, NE]), con[:, C_IOTAB:C_IOTAB + NB].unsqueeze(2).to_broadcast([P, NB, NE]), ALU.is_le))
            link(red(EBF, ECMP, AX.X, ALU.add))
            link(ts(EBF, EBF, float(NE - 1), None, ALU.min))
            link(nc.vector.tensor_copy(eblk[:, :], EBF))
            scan = nc.vector.tensor_tensor_scan
            link(nc.vector.memset(NEW[:, 0:1], 1.0))
            link(tt(NEW[:, 1:NB], EBF[:, 1:NB], EBF[:, 0:NB - 1], ALU.not_equal))
            link(ts(OLD, NEW, -1.0, 1.0, ALU.mult, ALU.add))
            link(tt(PRV, NEW, con[:, C_IOTAB:C_IOTAB + NB], ALU.mult))
            link(scan(RUN, OLD, PRV, 0.0, ALU.mult, ALU.add))
            link(nc.vector.memset(PRV[:, 0:1], 0.0))
            link(tt(PRV[:, 1:NB], NEW[:, 1:NB], RUN[:, 0:NB - 1], ALU.mult))
            link(scan(BUF, OLD, PRV, 0.0, ALU.mult, ALU.add))
            link(ts(PRV, BUF, 12.0, 1.0, ALU.mult, ALU.add))
            link(nc.vector.tensor_copy(efree, PRV))
            link(ts(BUF, BUF, 0.0, 12.0, ALU.is_gt, ALU.mult))
            link(tt(PRV, PRV, BUF, ALU.add))
            link(nc.vector.tensor_copy(edown, PRV))
            link(tt(OLD, OLD, NEW, ALU.subtract))
            link(scan(BUF, OLD, NEW, 1.0, ALU.mult, ALU.add))
            link(nc.vector.tensor_copy(ebuf, BUF))
            link(ts(NEW[:, 0:1], EBF[:, 0:1], 0.0, None, ALU.is_gt))
            link(nc.vector.tensor_copy(enew, NEW))
            link(ts(NHALF, CB[:, NE - 1:NE], 0.5, None, ALU.mult))
            link(tt(PCMP, NHALF.to_broadcast([P, NB // 2]), con[:, C_IOTAB:C_IOTAB + NB // 2], ALU.is_gt))
            link(red(NPR, PCMP, AX.X, ALU.add))
            link(ts(NPR, NPR, float(-(LEAST // 2)), None, ALU.add))
            nc.vector.tensor_copy(npair, NPR).then_inc(tables_ready, 1)

        WGU = weights[:, 0:4 * KD * FF].rearrange("p (k i n) -> p k i n", i=2, n=FF)
        WDN = weights[:, 4 * KD * FF:].rearrange("p (k n) -> p k n", n=D)
        oS = NT * D
        def take_split(n):
            nonlocal oS
            v = split[:, oS - NT * D:oS - NT * D + n]
            oS += n
            return v
        XH, XL = (take_split(2 * D).rearrange("p (b k q) -> p b k q", b=2, k=KD) for _ in range(2))
        HH, HLO = (take_split(FF).rearrange("p (k q) -> p k q", k=FF // P) for _ in range(2))
        WH, WL = ([take_split(D) for _ in range(RING)] for _ in range(2))
        SG, HE = take(FF), take(FF)
        XG = con[:, C_COS:C_COS + 2 * D].rearrange("p (b n) -> p b n", b=2)
        YE = par[:, P_B1:P_END]
        assert oS <= oC
        GFN = view(oC, D)
        OUTB = view(oC + D, 2, D)
        NY = 4
        Y12 = [view(oC + (3 + 2 * i) * D, 2, D) for i in range(NY)]
        SQF = view(oC + (3 + 2 * NY) * D, D)
        first_loaded = sem("first_loaded")
        w_loads, wdn_loaded = [sem("gate_loaded"), sem("up_w_loaded")], sem("wdn_loaded")
        ix_ready, xg_loaded = sem("ix_ready"), [sem(f"xg_loaded{i}") for i in range(2)]
        xgt_ready, xh_ready, xl_ready, sg_ready, he_ready, het_ready, hh_ready, hl_ready, ye_copied = (
            sem(n) for n in ("xgt_ready", "xh_ready", "xl_ready", "sg_ready", "he_ready", "het_ready", "hh_ready",
                             "hl_ready", "ye_copied"))
        wh_ready, wl_dve, wl_pool, chunk_used = sem("wh_ready"), sem("wl_dve"), sem("wl_pool"), sem("chunk_used")
        ix_seen, act_seen = sem("ix_seen"), sem("act_seen")
        ye_stored = sem("ye_stored")

        def chunks(last_block):
            return ([] if last_block else [("gu", k) for k in range(KD)]) + [("down", k) for k in range(FF // P)]

        def raw(kind, k, q):
            if kind == "gu":
                return WGU[:, bass.ds(q * KD + k, 1)].rearrange("p a i n -> p (a i n)")
            return WDN[:, bass.ds(q * (FF // P) + k, 1)].rearrange("p a n -> p (a n)")

        def by_dve(c0, place):
            return c0 // RING * (RING - 1) + place // RING * (RING - 1) + place % RING

        USED0 = 5

        def gu_used(b):
            return USED0 + KD if isinstance(b, int) and b == 0 else 12 * b + (USED0 + KD - FF // P)

        def down_used(b, last_block):
            return 12 * b + (USED0 + KD + FF // P + (0 if last_block else KD))

        def counts(b, place):
            if b is None:
                return place, by_dve(0, place), place // RING
            return b * 12 + (KD + place), b * 9 + by_dve(KD, place), b * 3 + (KD // RING + place // RING)

        def blocks(eng, body):
            for par in range(2):
                body(0, par, True, False)
            eng.wait_ge(tables_ready, 1)
            pairs = eng.value_load(npair[0:1, 0:1], min_val=0, max_val=(NB - LEAST) // 2) + LEAST // 2
            with eng.Fori(1, pairs - 1) as j:
                for par in range(2):
                    body(j, par, False, False)
            for par in range(2):
                body(pairs - 1, par, False, True)
            return pairs

        def has(par, last, ahead):
            return not last or par + ahead < 2

        def sp_experts(sp):
            sp.wait_ge(out_done, NT)
            sp.wait_ge(log_done, NT)
            sp.dma_start(WDN[:, 0:FF // P], a["w_down"][0].rearrange("(k p) n -> p k n", p=P)).then_inc(first_loaded, 16)
            sp.wait_ge(first_loaded, 48)
            sp.wait_ge(tables_ready, 1)

            def body(j, par, first, last):
                b = 2 * j + par
                e, q, new, free, free_down = (sp.value_load(tab[0:1, bass.ds(b, 1)], min_val=0, max_val=hi)
                                   for tab, hi in ((eblk, NE - 1), (ebuf, 1), (enew, 1), (efree, 12 * NB), (edown, 12 * NB + 12)))
                if par or not first:
                    for i in range(2):
                        sp.wait_ge(w_loads[i], 16 * b)
                sp.wait_ge(chunk_used, free)
                for i, w in enumerate(("w_gate", "w_up")):
                    sp.dma_start(WGU[:, bass.ds(q * KD, KD), i], a[w][bass.ds(e, 1)].rearrange("a (k p) n -> p (a k) n", p=P),
                                 cond=new).then_inc(w_loads[i], 16)
                if par or not first:
                    sp.wait_ge(wdn_loaded, 16 * b)
                sp.wait_ge(chunk_used, free_down)
                sp.dma_start(WDN[:, bass.ds(q * (FF // P), FF // P)], a["w_down"][bass.ds(e, 1)].rearrange("a (k p) n -> p (a k) n", p=P),
                             cond=new).then_inc(wdn_loaded, 16)

            return blocks(sp, body)

        def buffer_of(eng, b):
            return eng.value_load(ebuf[0:1, bass.ds(b, 1)], min_val=0, max_val=1)

        def buffers(eng, b, par, last):
            q = buffer_of(eng, b)
            return q, (buffer_of(eng, b + 1) if has(par, last, 1) else None)

        def pool_experts(pool):
            pool.wait_ge(slots_ready, 1)
            for t in range(2):
                pool.wait_ge(xn2_stored[t], 16 * NT // 2)

            def gather(b, par):
                pool.sem_inc(ix_seen, 1)
                nc.gpsimd.tensor_copy(ixc[:, par:par + 1], ixb[:, bass.ds(b, 1)]).then_inc(ix_ready, 1)
                pool.wait_ge(ix_ready, b + 1)
                pool.sem_inc(ix_seen, 1)
                pool.indirect_dma_start(XG[:, par], None, xn_d, bass.IndirectOffsetOnAxis(ap=ixc[:, par:par + 1], axis=0)).then_inc(xg_loaded[par], 16)

            def lower(b, place, kind, k, q):
                pool.wait_ge(wh_ready, counts(b, place)[0] + 1)
                pool.sem_inc(ix_seen, 1)
                nc.gpsimd.tensor_tensor(WL[place % RING], raw(kind, k, q), WH[place % RING].bitcast(F32), ALU.subtract).then_inc(wl_pool, 1)

            gather(0, 0)
            gather(1, 1)
            pool.wait_ge(tables_ready, 1)
            q0 = buffer_of(pool, 0)
            for k in range(RING - 1, KD, RING):
                lower(None, k, "gu", k, q0)

            def body(j, par, first, last):
                b = 2 * j + par
                q, q_next = buffers(pool, b, par, last)
                if has(par, last, 2):
                    pool.wait_ge(xgt_ready, 2 * b + 2)
                    gather(b + 2, par)
                for place, (kind, k) in enumerate(chunks(not has(par, last, 1))):
                    if place % RING == RING - 1:
                        lower(b, place, kind, k, q_next if kind == "gu" else q)

            return blocks(pool, body)

        def pe_experts(pe):
            def turn_x(j, par):
                pe.wait_ge(xg_loaded[par], 16 * (j + 1))
                for h in range(2):
                    for k in range(4):
                        mm = nc.tensor.transpose(ps[:, 6 + h, P * k:P * k + P], XG[:, par, P * (4 * h + k):P * (4 * h + k) + P], ident)
                    mm.then_inc(xgt_ready, 1)

            def product(b, place, k, n, hi, lo, bank):
                c, dve_parts, pool_parts = counts(b, place)
                if place % RING == RING - 1:
                    pe.wait_ge(wl_pool, pool_parts + 1)
                else:
                    pe.wait_ge(wl_dve, dve_parts + 1)
                for p_, (x, w) in enumerate(((hi, WH), (hi, WL), (lo, WH))):
                    for h in range(2):
                        mm = nc.tensor.matmul(ps[:, bank + h, :], x, w[place % RING][:, 512 * h:512 * h + 512],
                                              start=(k == 0 and p_ == 0), stop=(k == n - 1 and p_ == 2))
                mm.then_inc(chunk_used, 1)

            def gate_up(b, par, turn):
                pe.wait_ge(xl_ready, 2 * b + 2)
                for k in range(KD):
                    product(turn, k, k, KD, XH[:, par, k], XL[:, par, k], 2 * par)

            pe.wait_ge(slots_ready, 1)
            pe.sem_inc(chunk_used, USED0)
            turn_x(0, 0)
            gate_up(0, 0, None)
            turn_x(0, 1)

            def body(j, par, first, last):
                b = 2 * j + par
                pe.wait_ge(he_ready, b + 1)
                pe.wait_ge(xl_ready, 2 * b + (4 if has(par, last, 1) else 2))
                for k in range(FF // P):
                    mm = nc.tensor.transpose(ps[:, 6, P * k:P * k + P], HE[:, P * k:P * k + P], ident)
                mm.then_inc(het_ready, 1)
                if has(par, last, 1):
                    gate_up(b + 1, 1 - par, b)
                pe.wait_ge(hl_ready, b + 1)
                if has(par, last, 2):
                    turn_x(j + 1, par)
                if par or not first:
                    pe.wait_ge(ye_copied, 2 * b)
                for place, (kind, k) in enumerate(chunks(not has(par, last, 1))):
                    if kind == "down":
                        product(b, place, k, FF // P, HH[:, k], HLO[:, k], 4)

            blocks(pe, body)

        def act_experts(act):
            act.wait_ge(slots_ready, 1)

            def higher(b, place, kind, k, q):
                c = counts(b, place)[0]
                if b is not None or place >= RING:
                    act.wait_ge(chunk_used, c + (USED0 - RING + 1))
                    act.sem_inc(act_seen, 1)
                nc.scalar.copy(WH[place % RING], raw(kind, k, q)).then_inc(wh_ready, 1)

            def copy_x(b, par):
                for h in range(2):
                    act.wait_ge(xgt_ready, 2 * b + 1 + h)
                    nc.scalar.copy(XH[:, par, 4 * h:4 * h + 4], ps[:, 6 + h, :].rearrange("p (k q) -> p k q", k=4)).then_inc(xh_ready, 1)

            def silu(b, par):
                act.wait_ge(chunk_used, gu_used(b))
                nc.scalar.activation(SG, ps[:, 2 * par, :], ACT.Silu).then_inc(sg_ready, 1)

            def store(b):
                act.wait_ge(ye_copied, 2 * b + 2)
                act.dma_start(ye_d[bass.ds(b * P, P), :], YE).then_inc(ye_stored, 16)

            copy_x(0, 0)
            act.wait_ge(tables_ready, 1)
            act.wait_ge(first_loaded, 48)
            for i in range(2):
                act.wait_ge(w_loads[i], 16)
            q0 = buffer_of(act, 0)
            for k in range(KD):
                higher(None, k, "gu", k, q0)
            silu(0, 0)
            copy_x(1, 1)

            def body(j, par, first, last):
                b = 2 * j + par
                q, q_next = buffers(act, b, par, last)
                for place, (kind, k) in enumerate(chunks(not has(par, last, 1))):
                    if (kind, k) == ("gu", 0):
                        for i in range(2):
                            act.wait_ge(w_loads[i], 16 * b + 32)
                        act.sem_inc(act_seen, 1)
                    if (kind, k) == ("down", 0):
                        act.wait_ge(wdn_loaded, 16 * b + 16)
                        act.sem_inc(act_seen, 1)
                    higher(b, place, kind, k, q_next if kind == "gu" else q)
                    if place == RING - 1:
                        act.wait_ge(het_ready, b + 1)
                        nc.scalar.copy(HH, ps[:, 6, :].rearrange("p (k q) -> p k q", k=4)).then_inc(hh_ready, 1)
                        if par or not first:
                            store(b - 1)
                if has(par, last, 1):
                    silu(b + 1, 1 - par)
                if has(par, last, 2):
                    copy_x(b + 2, par)

            pairs = blocks(act, body)
            store(2 * pairs - 1)

        def dve_experts(dve):
            def lower(b, place, kind, k, q):
                dve.wait_ge(wh_ready, counts(b, place)[0] + 1)
                nc.vector.tensor_tensor(WL[place % RING], raw(kind, k, q), WH[place % RING].bitcast(F32), ALU.subtract).then_inc(wl_dve, 1)

            def x_lower(b, par):
                for h in range(2):
                    dve.wait_ge(xh_ready, 2 * b + 1 + h)
                    x = slice(4 * h, 4 * h + 4)
                    nc.vector.tensor_tensor(XL[:, par, x], ps[:, 6 + h, :].rearrange("p (k q) -> p k q", k=4), XH[:, par, x].bitcast(F32),
                                            ALU.subtract).then_inc(xl_ready, 1)

            def hidden(b, par):
                dve.wait_ge(sg_ready, b + 1)
                nc.vector.tensor_tensor(HE, SG, ps[:, 2 * par + 1, :], ALU.mult).then_inc(he_ready, 1)

            def outputs_of(b, b_is_first, last_block=False):
                dve.wait_ge(chunk_used, down_used(b, last_block))
                if not b_is_first:
                    dve.wait_ge(ye_stored, 16 * b)
                for h in range(2):
                    nc.vector.tensor_copy(YE[:, 512 * h:512 * h + 512], ps[:, 4 + h, :]).then_inc(ye_copied, 1)

            x_lower(0, 0)
            q0 = buffer_of(dve, 0)
            for k in range(KD):
                if k % RING < RING - 1:
                    lower(None, k, "gu", k, q0)
            hidden(0, 0)
            x_lower(1, 1)

            def body(j, par, first, last):
                b = 2 * j + par
                q, q_next = buffers(dve, b, par, last)
                for place, (kind, k) in enumerate(chunks(not has(par, last, 1))):
                    if place % RING < RING - 1:
                        lower(b, place, kind, k, q_next if kind == "gu" else q)
                    if place == RING - 1:
                        if par or not first:
                            outputs_of(b - 1, first)
                        dve.wait_ge(hh_ready, b + 1)
                        nc.vector.tensor_tensor(HLO, ps[:, 6, :].rearrange("p (k q) -> p k q", k=4), HH.bitcast(F32), ALU.subtract).then_inc(hl_ready, 1)
                if has(par, last, 1):
                    hidden(b + 1, 1 - par)
                if has(par, last, 2):
                    x_lower(b + 2, par)

            pairs = blocks(dve, body)
            outputs_of(2 * pairs - 1, False, True)

        y_gathered = [sem(f"y_gathered{i}") for i in range(NY)]
        y_added, ob_ready = sem("y_added"), sem("ob_ready")
        out_stored = [sem("out_stored0"), sem("out_stored1")]

        def sp_final(sp, pairs):
            sp.wait_ge(ye_copied, 4 * pairs)
            sp.dma_start(GFN, a["final_norm_g"].to_broadcast([P, D])).then_inc(late_loaded, 16)
            for t in range(NT):
                sp.wait_ge(ob_ready, t + 1)
                sp.dma_start(out[P * t:P * t + P, :], OUTB[:, t % 2]).then_inc(out_stored[t % 2], 16)
            for i in range(2):
                sp.wait_ge(out_stored[i], 16 * NT // 2)

        def pool_final(pool, pairs):
            pool.wait_ge(ye_stored, 32 * pairs)
            pool.sem_inc(ix_seen, 1)
            for t in range(NT):
                if t >= NY:
                    pool.wait_ge(y_added, 2 * (t - NY + 1))
                for k in range(2):
                    pool.indirect_dma_start(Y12[t % NY][:, k], None, ye_d,
                                            bass.IndirectOffsetOnAxis(ap=slots[:, k, t:t + 1], axis=0)).then_inc(y_gathered[t % NY], 16)

        def act_final(act):
            for t in range(NT):
                act.wait_ge(y_added, 2 * t + 2)
                nc.scalar.activation(SQF, H1[:, t], ACT.Square, accum_out=SS2[:, t:t + 1]).then_inc(ss2_ready, 1)
                act.wait_ge(va2_ready, NT + t + 1)
                nc.scalar.activation(SD2[:, t:t + 1], VA2[:, t:t + 1], ACT.Sqrt).then_inc(sd2_ready, 1)

        def dve_final(dve, link):
            dve.wait_ge(late_loaded, 48)
            for t in range(NT + 1):
                if t < NT:
                    dve.wait_ge(y_gathered[t % NY], 32 * (t // NY + 1))
                    for k in range(2):
                        nc.vector.scalar_tensor_tensor(H1[:, t], Y12[t % NY][:, k], W12[:, k, t:t + 1], H1[:, t], ALU.mult, ALU.add).then_inc(y_added, 1)
                        dve.wait_ge(y_added, 2 * t + k + 1)
                if t >= 1:
                    s = t - 1
                    dve.wait_ge(ss2_ready, NT + s + 1)
                    nc.vector.tensor_scalar(VA2[:, s:s + 1], SS2[:, s:s + 1], 1.0 / D, EPS, ALU.mult, ALU.add).then_inc(va2_ready, 1)
                    dve.wait_ge(sd2_ready, NT + s + 1)
                    link(nc.vector.reciprocal(RS2[:, s:s + 1], SD2[:, s:s + 1]))
                    if s >= 2:
                        dve.wait_ge(out_stored[s % 2], 16 * (s // 2))
                    nc.vector.scalar_tensor_tensor(OUTB[:, s % 2], H1[:, s], RS2[:, s:s + 1], GFN, ALU.mult, ALU.mult).then_inc(ob_ready, 1)

        def sp_rest(sp):
            sp_s5(sp)
            sp_hgrn(sp)
            sp_attention(sp)
            sp_out(sp)
            sp_final(sp, sp_experts(sp))

        def act_rest(act, link):
            act_s5(act, link)
            act_hgrn(act, link)
            act_attention(act, link)
            act_out(act, link)
            act_route(act, link)
            act_experts(act)
            act_final(act)

        def dve_rest(dve, link):
            dve_s5(dve, link)
            dve_turned(dve, link)
            dve_hgrn(dve, link)
            dve_attention(dve, link)
            dve_out(dve, link)
            dve_route(dve, link)
            dve_experts(dve)
            dve_final(dve, link)

        def pe_rest(pe):
            pe_s5(pe)
            pe_hgrn(pe)
            pe_attention(pe)
            pe_out(pe)
            pe_route(pe)
            pe_experts(pe)

        def pool_rest(pool, link):
            pool_hgrn(pool, link)
            pool_attention(pool, link)
            pool_final(pool, pool_experts(pool))


        with nc.Block() as block:
            @block.sync
            def _(sp):
                sp_project(sp)
                sp_rest(sp)

            @block.scalar
            def _(act):
                link = Chain(act, act_chain)
                act_project(act, link)
                act_rest(act, link)

            @block.vector
            def _(dve):
                link = Chain(dve, dve_chain)
                dve_project(dve, link)
                dve_rest(dve, link)

            @block.tensor
            def _(pe):
                pe_project(pe)
                pe_rest(pe)

            @block.gpsimd
            def _(pool):
                link = Chain(pool, pool_chain)
                pool_project(pool, link)
                pool_rest(pool, link)


def layout(inputs):
    g = {k: np.asarray(v) for k, v in inputs.items()}
    par = np.zeros((P, P_END), np.float32)
    par[:, P_GMIX:P_GMIX + 8] = g["norm_mix_g"].reshape(8, P).T
    for j, name in enumerate(("s5_lambda_re", "s5_lambda_im")):
        par[:, P_S5 + 16 * j:P_S5 + 16 * j + 16] = np.concatenate([g[name][0].T] * 2)
    par[:, P_S5 + 32:P_S5 + 48] = g["s5_log_dt"][0][None, :]
    par[:, P_D:P_D + 2] = g["s5_d"].reshape(2, P).T
    par[:, P_LB:P_LB + 2] = g["hgrn_lower_bounds"].reshape(2, P).T
    for j, name in enumerate(("diff_lambda_q1", "diff_lambda_k1", "diff_lambda_q2", "diff_lambda_k2")):
        par[0:64, P_LAM + j] = g[name][0]
    b = [g["s5_b_re"][0].transpose(1, 0, 2).reshape(64, 256), g["s5_b_im"][0].transpose(1, 0, 2).reshape(64, 256)]
    c = [g["s5_c_re"][0].transpose(2, 0, 1).reshape(64, 256), g["s5_c_im"][0].transpose(2, 0, 1).reshape(64, 256)]
    par[:, P_B1:P_B1 + 256], par[:, P_B2:P_B2 + 256] = np.concatenate(b), np.concatenate(b[::-1])
    par[:, P_C1:P_C1 + 256], par[:, P_C2:P_C2 + 256] = np.concatenate(c), np.concatenate(c[::-1])
    router = np.concatenate([g["moe_w_group"][0], g["moe_w_expert"][0]], axis=1)
    return {
        "consts": constants(), "params": par, "x": g["x"][0], "meta_tokens": g["meta_tokens"],
        "w_in": g["w_in"][0], "w_glu": g["s5_w_glu"][0], "w_out": g["w_out"][0],
        "hgrn_norm_g": g["hgrn_norm_g"], "subln_g": g["diff_subln_g"], "norm_ffn_g": g["norm_ffn_g"],
        "final_norm_g": g["final_norm_g"][None], "w_router": router,
        "b_router": np.concatenate([g["moe_b_group"], g["moe_b_expert"]], axis=1),
        "w_gate": g["moe_w_gate"][0], "w_up": g["moe_w_up"][0], "w_down": g["moe_w_down"][0],
    }


def kernel(**inputs):
    import concourse.bacc as bacc
    from concourse.bass_utils import run_bass_kernel_spmd

    nc = bacc.Bacc("TRN2", target_bir_lowering=False, num_devices=1)
    arrays = {f"in_{k}": np.ascontiguousarray(v) for k, v in layout(inputs).items()}
    a = {k[3:]: nc.dram_tensor(k, v.shape, mybir.dt.from_np(v.dtype), kind="ExternalInput").ap() for k, v in arrays.items()}
    out = nc.dram_tensor("out", (X, D), F32, kind="ExternalOutput").ap()
    build(nc, a, out)
    r = run_bass_kernel_spmd(nc, [arrays], core_ids=[0])
    return np.asarray(r.results[0]["out"]).reshape(1, X, D)
```
